# Optimizing a Trainium2 kernel written in Bass

```python
import math
import jax, jax.numpy as jnp
from jax import lax
import numpy as np

D_MODEL = 1024
BATCH = 1
SEQ = 512
DEPTH = 2

N_MIXERS = 2
N_ATTN_LAYERS = (DEPTH + 1) // 2
N_POOL_LAYERS = DEPTH // 2
N_HEADS = 8
HEAD_DIM = D_MODEL // N_HEADS // 2
V_DIM = 2 * HEAD_DIM
ATTN_SCALE = HEAD_DIM ** -0.5
Q_BLOCK = 128
POOL_WINDOWS = (2, 4, 8, 16)
N_POOL_GROUPS = len(POOL_WINDOWS)
POOL_GROUP_DIM = D_MODEL // N_POOL_GROUPS
D_FF = 2816
CONV_WIDTH = 3
PLE_DIM = 256
RMS_EPS = 1e-6

kernel_name = "hybrid_diffattn_multipool_convglu_ple"

def rmsnorm(x, g):
    xf = x.astype(jnp.float32)
    inv = lax.rsqrt(jnp.mean(xf * xf, axis=-1, keepdims=True) + RMS_EPS)
    return (xf * inv).astype(x.dtype) * g

def lambda_init_fn(layer_idx):
    return 0.8 - 0.6 * math.exp(-0.3 * layer_idx)

def diff_attention(xn, w_qkv, lam_q1, lam_k1, lam_q2, lam_k2, sub_g, w_o, lambda_init):
    B, S, _ = xn.shape
    qkv = xn @ w_qkv
    q, k, v = jnp.split(qkv, 3, axis=-1)
    q = q.reshape(B, S, N_HEADS, 2, HEAD_DIM).transpose(0, 2, 3, 1, 4)
    k = k.reshape(B, S, N_HEADS, 2, HEAD_DIM).transpose(0, 2, 3, 1, 4)
    v = v.reshape(B, S, N_HEADS, V_DIM).transpose(0, 2, 1, 3)
    lam = (jnp.exp(jnp.sum(lam_q1.astype(jnp.float32) * lam_k1.astype(jnp.float32)))
           - jnp.exp(jnp.sum(lam_q2.astype(jnp.float32) * lam_k2.astype(jnp.float32)))
           + lambda_init)
    n_blocks = S // Q_BLOCK
    q_blocks = q.reshape(B, N_HEADS, 2, n_blocks, Q_BLOCK, HEAD_DIM).transpose(3, 0, 1, 2, 4, 5)
    k_pos = jnp.arange(S)

    def one_block(args):
        q_blk, blk_idx = args
        s = jnp.einsum('bhcqd,bhckd->bhcqk', q_blk, k).astype(jnp.float32) * ATTN_SCALE
        q_pos = blk_idx * Q_BLOCK + jnp.arange(Q_BLOCK)
        causal = k_pos[None, :] <= q_pos[:, None]
        s = jnp.where(causal, s, -jnp.inf)
        a = jax.nn.softmax(s, axis=-1)
        w = (a[:, :, 0] - lam * a[:, :, 1]).astype(v.dtype)
        return jnp.einsum('bhqk,bhkv->bhqv', w, v)

    o = lax.map(one_block, (q_blocks, jnp.arange(n_blocks)))
    o = o.transpose(1, 0, 3, 2, 4).reshape(B, S, N_HEADS, V_DIM)
    o = rmsnorm(o, sub_g) * (1.0 - lambda_init)
    return o.reshape(B, S, N_HEADS * V_DIM) @ w_o

def multiscale_pool(xn, w_pool, b_pool, scale):
    B, S, D = xn.shape
    xf = xn.astype(jnp.float32)
    cs = jnp.cumsum(xf, axis=1)
    count_base = jnp.arange(1, S + 1, dtype=jnp.float32)[None, :, None]
    outs = []
    for g, win in enumerate(POOL_WINDOWS):
        sl = slice(g * POOL_GROUP_DIM, (g + 1) * POOL_GROUP_DIM)
        cs_g = cs[..., sl]
        lag = jnp.pad(cs_g, ((0, 0), (win, 0), (0, 0)))[:, :S]
        mean = (cs_g - lag) / jnp.minimum(count_base, float(win))
        outs.append(mean - xf[..., sl])
    y = jnp.stack(outs, axis=2).astype(xn.dtype)
    y = jnp.einsum('bsgc,gce->bsge', y, w_pool) + b_pool
    return y.reshape(B, S, D) * scale

def conv_glu_ffn(xn, w_up, conv_w, conv_b, w_down):
    u = xn @ w_up
    u = lax.conv_general_dilated(
        u, conv_w[:, None, :].astype(u.dtype), window_strides=(1,),
        padding=((CONV_WIDTH - 1, 0),),
        dimension_numbers=('NWC', 'WIO', 'NWC'),
        feature_group_count=2 * D_FF) + conv_b
    gate, up = jnp.split(u, 2, axis=-1)
    return (jax.nn.silu(gate) * up) @ w_down

def setup_inputs(seed: int = 0) -> dict:
    key = jax.random.key(seed)
    ks = jax.random.split(key, 24)
    f32 = jnp.float32

    def nrm(k, shape, scale):
        return jax.random.normal(k, shape, f32) * scale

    def gain(k, shape):
        return 1.0 + 0.05 * jax.random.normal(k, shape, f32)

    return {
        "x": nrm(ks[0], (BATCH, SEQ, D_MODEL), 1.0),
        "p": nrm(ks[1], (DEPTH, BATCH, SEQ, PLE_DIM), 1.0),
        "mix_norm_g": gain(ks[2], (DEPTH, D_MODEL)),
        "w_qkv": nrm(ks[3], (N_ATTN_LAYERS, D_MODEL, 3 * D_MODEL), D_MODEL ** -0.5),
        "lam_q1": nrm(ks[4], (N_ATTN_LAYERS, HEAD_DIM), 0.1),
        "lam_k1": nrm(ks[5], (N_ATTN_LAYERS, HEAD_DIM), 0.1),
        "lam_q2": nrm(ks[6], (N_ATTN_LAYERS, HEAD_DIM), 0.1),
        "lam_k2": nrm(ks[7], (N_ATTN_LAYERS, HEAD_DIM), 0.1),
        "attn_sub_g": gain(ks[8], (N_ATTN_LAYERS, V_DIM)),
        "w_attn_out": nrm(ks[9], (N_ATTN_LAYERS, N_HEADS * V_DIM, D_MODEL), (N_HEADS * V_DIM) ** -0.5),
        "w_pool": nrm(ks[10], (N_POOL_LAYERS, N_POOL_GROUPS, POOL_GROUP_DIM, POOL_GROUP_DIM), POOL_GROUP_DIM ** -0.5),
        "b_pool": nrm(ks[11], (N_POOL_LAYERS, N_POOL_GROUPS, POOL_GROUP_DIM), 0.02),
        "pool_scale": 0.5 + 0.05 * jax.random.normal(ks[12], (N_POOL_LAYERS, D_MODEL), f32),
        "ffn_norm_g": gain(ks[13], (DEPTH, D_MODEL)),
        "w_up": nrm(ks[14], (DEPTH, D_MODEL, 2 * D_FF), D_MODEL ** -0.5),
        "conv_w": nrm(ks[15], (DEPTH, CONV_WIDTH, 2 * D_FF), CONV_WIDTH ** -0.5),
        "conv_b": nrm(ks[16], (DEPTH, 2 * D_FF), 0.02),
        "w_down": nrm(ks[17], (DEPTH, D_FF, D_MODEL), D_FF ** -0.5),
        "ple_norm_g": gain(ks[18], (DEPTH, D_MODEL)),
        "w_ple_gate": nrm(ks[19], (DEPTH, D_MODEL, D_MODEL), D_MODEL ** -0.5),
        "w_ple_proj": nrm(ks[20], (DEPTH, PLE_DIM, D_MODEL), PLE_DIM ** -0.5),
        "final_norm_g": gain(ks[21], (D_MODEL,)),
    }

def reference(x, p, mix_norm_g, w_qkv, lam_q1, lam_k1, lam_q2, lam_k2, attn_sub_g, w_attn_out,
              w_pool, b_pool, pool_scale, ffn_norm_g, w_up, conv_w, conv_b, w_down,
              ple_norm_g, w_ple_gate, w_ple_proj, final_norm_g):
    h = x
    attn_idx = 0
    pool_idx = 0
    for i in range(DEPTH):
        hn = rmsnorm(h, mix_norm_g[i])
        if i % N_MIXERS == 0:
            mix = diff_attention(hn, w_qkv[attn_idx], lam_q1[attn_idx], lam_k1[attn_idx],
                                 lam_q2[attn_idx], lam_k2[attn_idx], attn_sub_g[attn_idx],
                                 w_attn_out[attn_idx], lambda_init_fn(i))
            attn_idx += 1
        else:
            mix = multiscale_pool(hn, w_pool[pool_idx], b_pool[pool_idx], pool_scale[pool_idx])
            pool_idx += 1
        h = h + mix
        h = h + conv_glu_ffn(rmsnorm(h, ffn_norm_g[i]), w_up[i], conv_w[i], conv_b[i], w_down[i])
        gate = jax.nn.sigmoid(rmsnorm(h, ple_norm_g[i]) @ w_ple_gate[i])
        h = h + gate * (p[i] @ w_ple_proj[i])
    return rmsnorm(h, final_norm_g)


_drawn_inputs = setup_inputs


def setup_inputs(seed=0):
    import zlib

    import numpy as np

    out = dict(_drawn_inputs(seed))
    spreads = {}
    factors = {'lam_k1': 2.706, 'lam_q2': 2.876, 'b_pool': 8.0, 'conv_b': 3.697, 'ple_norm_g': 6.16}
    for name, (base, spread) in spreads.items():
        noise = np.random.default_rng([zlib.crc32(name.encode()), seed]).standard_normal(out[name].shape)
        drawn = base * np.exp(spread * noise) if base else spread * noise
        out[name] = __import__('jax').numpy.asarray(drawn.astype(out[name].dtype))
    for name, factor in factors.items():
        out[name] = (out[name] * factor).astype(out[name].dtype)
    return out
```

```python
import math
from contextlib import ExitStack

import numpy as np

import concourse.bass as bass
from concourse import mybir

F32 = mybir.dt.float32
F32R = mybir.dt.float32r
BF16 = mybir.dt.bfloat16
ALU = mybir.AluOpType
ACT = mybir.ActivationFunctionType
AX_X = mybir.AxisListType.X

P = 128
D_MODEL = 1024
SEQ = 512
DEPTH = 2
N_HEADS = 8
HEAD_DIM = 64
POOL_WINDOWS = (2, 4, 8, 16)
D_FF = 2816
PLE_DIM = 256
EPS = 1e-6
ATTN_SCALE = HEAD_DIM ** -0.5
LAMBDA_INIT = 0.8 - 0.6 * math.exp(-0.3 * 0)
MASKED = -1e30

KT = D_MODEL // P
TT = SEQ // P
FT = D_FF // P
PLE_KT = PLE_DIM // P
POOL_KT = D_MODEL // len(POOL_WINDOWS) // P
FFN_PARTS = (8, 8, 6)
SLOTS = 4
SLOT_BLOCKS = KT + PLE_KT
LOOK = 2
PAD = 16


def plan():
    phases, n = {}, 0

    def add(name, units, blocks):
        nonlocal n
        phases[name] = (n, units, blocks)
        n += units

    add("qkv", 3 * N_HEADS, KT)
    add("wo", KT, KT)
    for layer in range(DEPTH):
        if layer:
            add("pool", KT, POOL_KT)
        for part, tiles in enumerate(FFN_PARTS):
            add(f"up{layer}{part}", 2 * tiles, KT)
            add(f"down{layer}{part}", KT, tiles)
        add(f"ple{layer}", KT, KT + PLE_KT)
    return phases, n


PHASES, N_UNITS = plan()
FIRST_RING4 = 3 * N_HEADS


def blocks_of(n):
    return next(b for first, units, b in PHASES.values() if first <= n < first + units)


def slot_of(n):
    return n % 3 if n < FIRST_RING4 else (n + 3) % SLOTS


def uses_before(n):
    if n < FIRST_RING4:
        return n // 3
    return (n - FIRST_RING4) // SLOTS + (N_HEADS if slot_of(n) != 3 else 0)


def hybrid_trunk(nc, x, p, mix_norm_g, w_qkv, lam_q1, lam_k1, lam_q2, lam_k2, attn_sub_g, w_attn_out,
                 w_pool, b_pool, pool_scale, ffn_norm_g, w_up, conv_w, conv_b, w_down,
                 ple_norm_g, w_ple_gate, w_ple_proj, final_norm_g, out):
    with ExitStack() as ctx:
        def sem(name):
            return ctx.enter_context(nc.semaphore(name))

        def sb(name, shape, dt, scope=ctx):
            return scope.enter_context(nc.sbuf_tensor(name, shape, dt))

        w_raw = [sb(f"w_raw{s}", [P, SLOT_BLOCKS * P], F32) for s in range(SLOTS)]
        w_hi = [sb(f"w_hi{s}", [P, SLOT_BLOCKS * P], F32R) for s in range(SLOTS)]
        w_lo = [sb(f"w_lo{s}", [P, SLOT_BLOCKS * P], F32R) for s in range(SLOTS)]
        h = sb("h", [P, KT, SEQ], F32)
        x_hi = sb("x_hi", [P, KT, SEQ], F32R)
        x_lo = sb("x_lo", [P, KT, SEQ], F32R)
        pT_hi = sb("pT_hi", [P, DEPTH * PLE_KT, SEQ], F32R)
        pT_lo = sb("pT_lo", [P, DEPTH * PLE_KT, SEQ], F32R)
        inv = sb("inv", [P, SEQ], F32)
        rms = sb("rms", [P, SEQ], F32)
        sq = sb("sq", [P, 2, SEQ], F32)
        acc = sb("acc", [P, SEQ], F32)
        params = sb("params", [P, 4, P], F32)
        ident = sb("ident", [P, P], F32)
        ones = sb("ones", [P, P], F32)
        eps = sb("eps", [P, 1], F32)
        small = sb("small", [P, 64], F32)
        bank1_scratch = sb("bank1_scratch", [P, 1], F32)
        bs = sb("bs", [P, KT], F32)
        edge = sb("edge", [P, len(POOL_WINDOWS), PAD], F32)
        ident16 = sb("ident16", [P, P], BF16)
        mask16 = sb("mask16", [P, P], BF16)

        start = ExitStack()
        x_tok = sb("x_tok", [P, TT, D_MODEL], F32, start)
        p_tok = sb("p_tok", [P, DEPTH * TT, PLE_DIM], F32, start)
        par_rows = sb("par_rows", [P, 4, P], F32, start)
        lam_rows = sb("lam_rows", [HEAD_DIM, 8], F32, start)
        square_scratch = sb("square_scratch", [P, D_MODEL], F32, start)
        diag = sb("diag", [P, TT, P], F32, start)
        start.close()

        attn = ExitStack()
        oT_hi = sb("oT_hi", [P, N_HEADS, SEQ], F32R, attn)
        oT_lo = sb("oT_lo", [P, N_HEADS, SEQ], F32R, attn)
        qk32 = sb("qk32", [P, SEQ], F32, attn)
        q_hi = sb("q_hi", [P, SEQ], F32R, attn)
        q_lo = sb("q_lo", [P, SEQ], F32R, attn)
        k_hi = sb("k_hi", [P, SEQ], F32R, attn)
        k_lo = sb("k_lo", [P, SEQ], F32R, attn)
        vT = sb("vT", [P, SEQ], F32, attn)
        v_hi = sb("v_hi", [P, TT, P], F32R, attn)
        v_lo = sb("v_lo", [P, TT, P], F32R, attn)
        CAUSAL = P * TT * (TT + 1) // 2
        probs = sb("probs", [P, 2, CAUSAL], F32, attn)
        wT_hi = sb("wT_hi", [P, CAUSAL], F32R, attn)
        wT_lo = sb("wT_lo", [P, CAUSAL], F32R, attn)
        o32 = acc
        attn.close()

        ffn = ExitStack()
        g_hi = sb("g_hi", [P, max(FFN_PARTS), SEQ], F32R, ffn)
        g_lo = sb("g_lo", [P, max(FFN_PARTS), SEQ], F32R, ffn)
        u32 = sb("u32", [P, 2, PAD + SEQ], F32, ffn)
        c32 = sb("c32", [P, 2, SEQ], F32, ffn)
        s32 = sb("s32", [P, SEQ], F32, ffn)
        g32 = sb("g32", [P, SEQ], F32, ffn)
        hn = sb("hn", [P, PAD + SEQ], F32, ffn)
        ffn.close()

        tail = ExitStack()
        y_tok = sb("y_tok", [P, TT, D_MODEL], F32, tail)
        g_final = sb("g_final", [P, D_MODEL], F32, tail)
        tail.close()

        bank = [ctx.enter_context(nc.psum_tensor(f"bank{b}", [P, SEQ], F32)) for b in range(8)]

        raw_in = [sem(f"raw_in{s}") for s in range(SLOTS)]
        hi_done, lo_done, unit_done, evac_done = sem("hi_done"), sem("lo_done"), sem("unit_done"), sem("evac_done")
        x_in = [sem(f"x_in{t}") for t in range(TT)]
        par_in, p_in, lam_in, gfin_in = sem("par_in"), sem("p_in"), sem("lam_in"), sem("gfin_in")
        ident_zero, const_done, mask_done = sem("ident_zero"), sem("const_done"), sem("mask_done")
        par_T, par_done, x_T, p_T, pT_hi_done, pT_done = (
            sem("par_T"), sem("par_done"), sem("x_T"), sem("p_T"), sem("pT_hi_done"), sem("pT_done"))
        tok_ss, diag_done = sem("tok_ss"), sem("diag_done")
        lam_prod, lam_sum, lam_exp, lam_diff, lam_done, subg_done = (
            sem("lam_prod"), sem("lam_sum"), sem("lam_exp"), sem("lam_diff"), sem("lam_done"), sem("subg_done"))
        x0_done, xhi_done, x_ready, sq_done, acc_zero, acc_done = (
            sem("x0_done"), sem("xhi_done"), sem("x_ready"), sem("sq_done"), sem("acc_zero"), sem("acc_done"))
        ss_done, rms_done, inv_done = sem("ss_done"), sem("rms_done"), sem("inv_done")
        qk32_done, qkhi_done, qklo_done = sem("qk32_done"), sem("qkhi_done"), sem("qklo_done")
        v_T, vhi_done, vlo_done = sem("v_T"), sem("vhi_done"), sem("vlo_done")
        scores_done, max_done, neg_done, exp_done = sem("scores_done"), sem("max_done"), sem("neg_done"), sem("exp_done")
        rsum_done, second_done, w_done = sem("rsum_done"), sem("second_done"), sem("w_done")
        w_T, wthi_done, wtlo_done = sem("w_T"), sem("wthi_done"), sem("wtlo_done")
        pv_done, o32_done, osq_done, oss_done, bank1_free, oinv_done, onorm_done, ohi_done, olo_done = (
            sem("pv_done"), sem("o32_done"), sem("osq_done"), sem("oss_done"), sem("bank1_free"), sem("oinv_done"),
            sem("onorm_done"), sem("ohi_done"), sem("olo_done"))
        pad_zero, vT_done, tap_done, conv1_done, conv_done, silu_done, gmul_done, ghi_done, glo_done = (
            sem("pad_zero"), sem("vT_done"), sem("tap_done"), sem("conv1_done"), sem("conv_done"), sem("silu_done"),
            sem("gmul_done"), sem("ghi_done"), sem("glo_done"))
        z_done, sig_done, ple_done = sem("z_done"), sem("sig_done"), sem("ple_done")
        bs_done, edge_done, hn_done, win_done, fix_done, y32_done, mixed_done = (
            sem("bs_done"), sem("edge_done"), sem("hn_done"), sem("win_done"), sem("fix_done"), sem("y32_done"),
            sem("mixed_done"))
        y_T, y_copied, fin_ss, fin_rms, fin_inv, y_normed, out_done = (
            sem("y_T"), sem("y_copied"), sem("fin_ss"), sem("fin_rms"), sem("fin_inv"), sem("y_normed"), sem("out_done"))

        CH = 2 * FT

        def tap(layer, w, j):
            return params[:, 2 * layer + w // 2, bass.ds((w % 2) * CH + j, 1)]

        def conv_bias(layer, j):
            return params[:, 2 * layer + 1, bass.ds(CH + j, 1)]

        MIX, FFN, PLE = 0, 1, 2

        def gain(layer, which, kt):
            return params[:, 2 * layer, bass.ds(2 * CH + which * KT + kt, 1)]

        B_POOL = 2 * CH + 3 * KT
        pool_b = params[:, 0, B_POOL:B_POOL + KT]
        pool_s = params[:, 0, B_POOL + KT:B_POOL + 2 * KT]
        sub_g = params[:, 1, 2 * CH:2 * CH + 1]
        par_count = [2 * CH + 5 * KT, 2 * CH + 1, 2 * CH + 3 * KT, 2 * CH]

        tok_sum = small[:, 0:TT]
        tok_scratch = small[:, 4:8]
        lam = small[:, 8:9]
        lam_e = small[:, 9:11]
        sub_g_scaled = small[:, 11:12]
        mx = small[:, 16:24]
        negmx = small[:, 24:32]
        sums = small[:, 32:40]
        rsums = small[:, 40:48]
        fin_col = small[:, 48:52]
        fin_icol = small[:, 52:56]

        NORM_MIX0, NORM_FFN0, NORM_PLE0, NORM_MIX1, NORM_FFN1, NORM_PLE1 = range(6)

        def evacuated(n):
            return n - FIRST_RING4 + 1

        refill = {NORM_MIX0: 0, NORM_FFN0: 1, NORM_PLE0: 2, NORM_MIX1: 3, NORM_FFN1: 4, NORM_PLE1: 5}
        sums_of = {NORM_FFN0: 0, NORM_PLE0: 1, NORM_MIX1: 2, NORM_FFN1: 3, NORM_PLE1: 4, 6: 5}
        LAST = FFN_PARTS.__len__() - 1

        def key_off(qt):
            return P * qt * (qt + 1) // 2

        def wt_off(kt):
            return P * (kt * TT - kt * (kt - 1) // 2)

        def scores_at(qt, c):
            at = P * qt if qt < 2 else 0
            return bank[2 + 2 * max(qt - 1, 0) + c][:, at:at + (qt + 1) * P]

        WT_BANKS = [(0, 512), (512, 384), (896, 384)]

        block = ctx.enter_context(nc.Block())

        @block.sync
        def _(sp):
            x_view = x.rearrange("b (t p) d -> p (b t) d", p=P)

            def load(slot, blocks, src, at=0):
                dst = w_raw[slot][:, at * P:(at + blocks) * P].rearrange("p (k c) -> p k c", c=P)
                return sp.dma_start(dst, src)

            wq = w_qkv[0].rearrange("(k p) f -> p k f", p=P)

            def load_qkv(hd, which):
                load(which, KT, wq[:, :, bass.ds(hd * P + which * D_MODEL, P)]).then_inc(raw_in[which], 16)

            for t in range(TT):
                sp.dma_start(x_tok[:, t, :], x_view[:, t, :]).then_inc(x_in[t], 16)
            for which in range(3):
                load_qkv(0, which)
            with sp.Fori(1, N_HEADS) as hd:
                for which in range(3):
                    sp.wait_ge(lo_done, 3 * hd + which - 2)
                    load_qkv(hd, which)

            def stream(name, src_of):
                first, units, blocks = PHASES[name]

                def body(a):
                    for u in range(SLOTS):
                        slot = slot_of(first + u)
                        if first + u > FIRST_RING4 or not isinstance(a, int) or a > 0:
                            sp.wait_ge(lo_done, SLOTS * a + first + u - SLOTS + 1)
                        at = 0
                        for k, src in src_of(a, u):
                            load(slot, k, src, at).then_inc(raw_in[slot], 16)
                            at += k

                bodies = units // SLOTS
                if name == "wo" or name == "pool":
                    for a in range(bodies):
                        body(a)
                else:
                    with sp.Fori(0, bodies) as a:
                        body(a)

            wo = w_attn_out[0].rearrange("(k p) f -> p k f", p=P)
            stream("wo", lambda a, u: [(KT, wo[:, :, bass.ds((SLOTS * a + u) * P, P)])])
            for layer in range(DEPTH):
                if layer:
                    wp = w_pool[0].rearrange("g (k p) e -> p g k e", p=P)
                    stream("pool", lambda a, u: [(POOL_KT, wp[:, (SLOTS * a + u) // 2, :, (u % 2) * P:(u % 2 + 1) * P])])
                up = w_up[layer].rearrange("(k p) f -> p k f", p=P)
                down = w_down[layer].rearrange("(k p) f -> p k f", p=P)
                gate = w_ple_gate[layer].rearrange("(k p) f -> p k f", p=P)
                proj = w_ple_proj[layer].rearrange("(k p) f -> p k f", p=P)
                done = 0
                for part, tiles in enumerate(FFN_PARTS):
                    stream(f"up{layer}{part}", lambda a, u: [
                        (KT, up[:, :, bass.ds((2 * a + u // 2 + done) * P + (u % 2) * D_FF, P)])])
                    stream(f"down{layer}{part}", lambda a, u: [
                        (tiles, down[:, done:done + tiles, bass.ds((SLOTS * a + u) * P, P)])])
                    done += tiles
                stream(f"ple{layer}", lambda a, u: [
                    (KT, gate[:, :, bass.ds((SLOTS * a + u) * P, P)]),
                    (PLE_KT, proj[:, :, bass.ds((SLOTS * a + u) * P, P)])])
            sp.wait_ge(unit_done, PHASES[f"ple{DEPTH - 1}"][0])
            sp.dma_start(g_final[:, :], final_norm_g.rearrange("(a d) -> a d", a=1).broadcast_to((P, D_MODEL))).then_inc(gfin_in, 16)
            for t in range(TT):
                sp.wait_ge(y_normed, t + 1)
                sp.dma_start(out.rearrange("b (t p) d -> p (b t) d", p=P)[:, t, :], y_tok[:, t, :]).then_inc(out_done, 16)
            sp.wait_ge(out_done, 16 * TT)

        def landed(n, a=0):
            before = 0
            s = slot_of(n)
            for first, units, _ in (PHASES[k] for k in PHASES if k[:3] == "ple"):
                before += sum(1 for m in range(first, first + units) if slot_of(m) == s and m < n)
            ple = any(PHASES[k][0] <= n < PHASES[k][0] + PHASES[k][1] for k in PHASES if k[:3] == "ple")
            per = 2 if ple else 1
            return 16 * (uses_before(n) + before + per) + 16 * per * a

        @block.scalar
        def _(act):
            def split_hi(n, a=0):
                if n >= N_UNITS:
                    return
                s, w = slot_of(n), blocks_of(n) * P
                act.wait_ge(raw_in[s], landed(n, a))
                if n >= FIRST_RING4 + 1:
                    act.wait_ge(unit_done, SLOTS * a + n - SLOTS + 1)
                act.activation(w_hi[s][:, 0:w], w_raw[s][:, 0:w], ACT.Copy).then_inc(hi_done, 1)

            def split_hi_qkv(hd, which):
                act.wait_ge(raw_in[which], 16 * hd + 16)
                if not isinstance(hd, int) or hd > 0:
                    act.wait_ge(unit_done, 3 * hd + which - 2)
                act.activation(w_hi[which][:, 0:KT * P], w_raw[which][:, 0:KT * P], ACT.Copy).then_inc(hi_done, 1)

            def rms_of(norm, src):
                act.wait_ge(ss_done, norm + 1)
                act.activation(rms[:, :], src, ACT.Sqrt, bias=eps[:, 0:1]).then_inc(rms_done, 1)

            def rows(t, at, src):
                act.dma_start(par_rows[at:at + src.shape[0], t, :], src).then_inc(par_in, 16)

            n_par = 0
            for i in range(DEPTH):
                rows(2 * i, 0, conv_w[i, 0:2].rearrange("w (j p) -> (w j) p", p=P))
                rows(2 * i, 2 * CH, mix_norm_g[i].rearrange("(j p) -> j p", p=P))
                rows(2 * i, 2 * CH + KT, ffn_norm_g[i].rearrange("(j p) -> j p", p=P))
                rows(2 * i, 2 * CH + 2 * KT, ple_norm_g[i].rearrange("(j p) -> j p", p=P))
                rows(2 * i + 1, 0, conv_w[i, 2].rearrange("(j p) -> j p", p=P))
                rows(2 * i + 1, CH, conv_b[i].rearrange("(j p) -> j p", p=P))
            rows(0, B_POOL, b_pool[0].rearrange("g (j p) -> (g j) p", p=P))
            rows(0, B_POOL + KT, pool_scale[0].rearrange("(j p) -> j p", p=P))
            rows(1, 2 * CH, attn_sub_g)
            for i, v in enumerate((lam_q1, lam_k1, lam_q2, lam_k2)):
                act.dma_start(lam_rows[:, i:i + 1], v.rearrange("a d -> d a")).then_inc(lam_in, 16)
            act.dma_start(p_tok[:, :, :], p.rearrange("i b (t p) d -> p (i b t) d", p=P)).then_inc(p_in, 16)

            for t in range(TT):
                act.wait_ge(x_in[t], 16)
                if t:
                    act.wait_ge(tok_ss, t)
                act.activation(square_scratch[:, :], x_tok[:, t, :], ACT.Square,
                               accum_out=tok_sum[:, t:t + 1]).then_inc(tok_ss, 1)
            split_hi_qkv(0, 0)
            act.wait_ge(par_done, 4)
            for kt in range(KT):
                act.wait_ge(x0_done, kt + 1)
                act.activation(x_hi[:, kt, :], h[:, kt, :], ACT.Copy, scale=gain(0, MIX, kt)).then_inc(xhi_done, 1)
            split_hi_qkv(0, 1)
            rms_of(NORM_MIX0, bank[2][:, :])
            for j in range(DEPTH * PLE_KT):
                act.wait_ge(p_T, j + 1)
                act.activation(pT_hi[:, j, :], bank[3 + j % 2][:, :], ACT.Copy).then_inc(pT_hi_done, 1)
            act.wait_ge(lam_sum, 1)
            act.activation(lam_e, bank[7][:, 0:2], ACT.Exp, scale=float(D_MODEL)).then_inc(lam_exp, 1)

            def qk_hi(hd, i, dst):
                act.wait_ge(qk32_done, 2 * hd + i + 1)
                act.activation(dst[:, :], qk32[:, :], ACT.Copy).then_inc(qkhi_done, 1)

            def back_first(hp):
                act.wait_ge(v_T, hp + 1)
                act.activation(v_hi[:, :, :].rearrange("p t c -> p (t c)"), bank[5][:, :], ACT.Copy).then_inc(vhi_done, 1)
                for b, (at, w) in enumerate(WT_BANKS):
                    act.wait_ge(w_T, 3 * hp + b + 1)
                    act.activation(wT_hi[:, at:at + w], bank[2 + b][:, 0:w], ACT.Copy).then_inc(wthi_done, 1)

            def back_second(hp):
                act.wait_ge(pv_done, hp + 1)
                act.activation(o32[:, :], bank[6][:, :], ACT.Copy, scale=sub_g_scaled).then_inc(o32_done, 1)
                act.activation(sq[:, 0, :], bank[6][:, :], ACT.Square).then_inc(osq_done, 1)

            def exps(hd):
                for qt in range(TT):
                    w = (qt + 1) * P
                    act.wait_ge(neg_done, 2 * hd + qt // 2 + 1)
                    for c in range(2):
                        at = key_off(qt)
                        act.activation(probs[:, c, at:at + w], scores_at(qt, c), ACT.Exp, scale=ATTN_SCALE,
                                       bias=negmx[:, 2 * qt + c:2 * qt + c + 1],
                                       accum_out=sums[:, 2 * qt + c:2 * qt + c + 1]).then_inc(exp_done, 1)

            def back_third(hp):
                act.wait_ge(oss_done, hp + 1)
                act.activation(rms[:, :], bank[1][:, :], ACT.Sqrt, bias=eps[:, 0:1],
                               scale=float(D_MODEL // P)).then_inc(bank1_free, 1)
                act.wait_ge(onorm_done, hp + 1)
                act.activation(oT_hi[:, hp, :], o32[:, :], ACT.Copy).then_inc(ohi_done, 1)

            split_hi_qkv(0, 2)
            qk_hi(0, 0, q_hi)
            split_hi_qkv(1, 0)
            qk_hi(0, 1, k_hi)
            exps(0)
            split_hi_qkv(1, 1)
            with act.Fori(1, N_HEADS - 1) as hd:
                split_hi_qkv(hd, 2)
                qk_hi(hd, 0, q_hi)
                back_first(hd - 1)
                split_hi_qkv(hd + 1, 0)
                qk_hi(hd, 1, k_hi)
                back_second(hd - 1)
                exps(hd)
                split_hi_qkv(hd + 1, 1)
                back_third(hd - 1)
            last = N_HEADS - 1
            split_hi_qkv(last, 2)
            qk_hi(last, 0, q_hi)
            back_first(last - 1)
            split_hi(FIRST_RING4)
            qk_hi(last, 1, k_hi)
            back_second(last - 1)
            exps(last)
            split_hi(FIRST_RING4 + 1)
            back_third(last - 1)
            back_first(last)
            back_second(last)
            back_third(last)

            def loop(name, body):
                bodies = PHASES[name][1] // SLOTS
                with act.Fori(0, bodies - 1) as a:
                    body(a)
                body(bodies - 1)

            def look_hi(name, u, a):
                n = PHASES[name][0] + u + LOOK
                if isinstance(a, int):
                    split_hi(n + SLOTS * a)
                else:
                    split_hi(n, a)

            def y_copy(m):
                act.wait_ge(y_T, m + 1)
                act.activation(y_tok[:, :, m * P:(m + 1) * P],
                               bank[6 + m % 2][:, :].rearrange("p (t c) -> p t c", c=P), ACT.Copy).then_inc(y_copied, 1)

            def residual_tile(n, m, g, n_sq):
                act.wait_ge(evac_done, evacuated(n))
                if g is not None:
                    act.activation(x_hi[:, m, :], h[:, m, :], ACT.Copy, scale=g).then_inc(xhi_done, 1)
                if n_sq >= 2:
                    act.wait_ge(acc_done, n_sq - 1)
                act.activation(sq[:, n_sq % 2, :], h[:, m, :], ACT.Square).then_inc(sq_done, 1)

            def residual_phase(name, norm, layer, which):
                for m in range(KT):
                    n = PHASES[name][0] + m
                    split_hi(n + LOOK)
                    if norm is not None:
                        residual_tile(n, m, gain(layer, which, m), KT * sums_of[norm] + m)

            residual_phase("wo", NORM_FFN0, 0, FFN)
            for layer in range(DEPTH):
                if layer:
                    rms_of(NORM_MIX1, bank[6][:, :])
                    first = PHASES["pool"][0]
                    for c in range(KT):
                        act.wait_ge(y32_done, c + 1)
                        act.activation(x_hi[:, c, :], c32[:, c % 2, :], ACT.Copy).then_inc(xhi_done, 1)
                    for m in range(KT):
                        split_hi(first + m + LOOK)
                        act.wait_ge(unit_done, first + m + 1)
                        if m >= 2:
                            act.wait_ge(evac_done, evacuated(first + m - 2))
                        act.activation((s32, g32)[m % 2][:, :], bank[m % SLOTS][:, :], ACT.Identity,
                                       scale=pool_s[:, m:m + 1], bias=bs[:, m:m + 1]).then_inc(mixed_done, 1)
                        act.wait_ge(unit_done, first + m // 2 * 2 + 2)
                        residual_tile(first + m, m, gain(1, FFN, m), KT * sums_of[NORM_FFN1] + m)
                rms_of(NORM_FFN1 if layer else NORM_FFN0, bank[6][:, :])
                done = 0
                for part, tiles in enumerate(FFN_PARTS):
                    name = f"up{layer}{part}"
                    pairs = layer * FT + done

                    def up_body(a):
                        for v in range(2):
                            j = 2 * a + v + done
                            pair = 2 * a + v + pairs
                            for c in range(2):
                                look_hi(name, 2 * v + c, a)
                                n = PHASES[name][0] + 2 * v + c
                                act.wait_ge(evac_done, SLOTS * a + evacuated(n))
                                act.activation(c32[:, c, :], u32[:, c, PAD:PAD + SEQ], ACT.Identity,
                                               scale=tap(layer, 2, j + c * FT),
                                               bias=conv_bias(layer, j + c * FT)).then_inc(tap_done, 1)
                                if c == 0:
                                    act.wait_ge(conv_done, 2 * pair + 1)
                                    act.activation(s32[:, :], c32[:, 0, :], ACT.Silu).then_inc(silu_done, 1)
                            act.wait_ge(gmul_done, pair + 1)
                            act.activation(g_hi[:, 2 * a + v, :], g32[:, :], ACT.Copy).then_inc(ghi_done, 1)

                    loop(name, up_body)
                    norm = (NORM_PLE1 if layer else NORM_PLE0) if part == LAST else None
                    residual_phase(f"down{layer}{part}", norm, layer, PLE)
                    done += tiles
                rms_of(NORM_PLE1 if layer else NORM_PLE0, bank[6][:, :])
                name = f"ple{layer}"
                after = 6 if layer else NORM_MIX1

                for m in range(KT):
                    n = PHASES[name][0] + m
                    split_hi(n + LOOK)
                    act.wait_ge(z_done, KT * layer + m + 1)
                    act.activation(s32[:, :], c32[:, 0, :], ACT.Sigmoid).then_inc(sig_done, 1)
                    residual_tile(n, m, None, KT * sums_of[after] + m)
                    if layer == DEPTH - 1 and m > 0:
                        y_copy(m - 1)
            y_copy(KT - 1)
            act.wait_ge(fin_ss, 1)
            act.activation(fin_col, bank[4][:, 0:TT], ACT.Sqrt, bias=eps[:, 0:1]).then_inc(fin_rms, 1)

        @block.gpsimd
        def _(pool):
            pool.memset(ident[:, :], 0.0).then_inc(ident_zero, 1)
            pool.memset(ones[:, :], 1.0 / D_MODEL).then_inc(const_done, 1)
            pool.memset(eps[:, :], EPS).then_inc(const_done, 1)
            pool.wait_ge(ident_zero, 1)
            pool.affine_select(out=ident[:, :], in_=ident[:, :], compare_op=ALU.not_equal, fill=1.0, base=0,
                               pattern=[[-1, P]], channel_multiplier=1).then_inc(const_done, 1)
            pool.memset(mask16[:, :], 0.0).then_inc(ident_zero, 1)
            pool.memset(ident16[:, :], 0.0).then_inc(ident_zero, 1)
            pool.wait_ge(ident_zero, 3)
            pool.affine_select(out=mask16[:, :], in_=mask16[:, :], compare_op=ALU.is_ge, fill=MASKED, base=0,
                               pattern=[[-1, P]], channel_multiplier=1).then_inc(mask_done, 1)
            pool.affine_select(out=ident16[:, :], in_=ident16[:, :], compare_op=ALU.not_equal, fill=1.0, base=0,
                               pattern=[[-1, P]], channel_multiplier=1).then_inc(mask_done, 1)
            pool.memset(edge[:, :, :], 1.0).then_inc(ident_zero, 1)
            pool.wait_ge(ident_zero, 4)
            for g, win in enumerate(POOL_WINDOWS):
                for t in range(win - 1):
                    pool.memset(edge[:, g, t:t + 1], win / (t + 1)).then_inc(edge_done, 1)
            pool.memset(bank1_scratch[:, :], 0.0).then_inc(bank1_free, 1)

        @block.vector
        def _(dve):
            def split_lo(n, a=0):
                if n >= N_UNITS:
                    return
                s, w = slot_of(n), blocks_of(n) * P
                dve.wait_ge(hi_done, SLOTS * a + n + 1)
                dve.tensor_tensor(w_lo[s][:, 0:w], w_raw[s][:, 0:w], w_hi[s][:, 0:w].bitcast(F32),
                                  ALU.subtract).then_inc(lo_done, 1)

            def split_lo_qkv(hd, which):
                w = KT * P
                dve.wait_ge(hi_done, 3 * hd + which + 1)
                dve.tensor_tensor(w_lo[which][:, 0:w], w_raw[which][:, 0:w], w_hi[which][:, 0:w].bitcast(F32),
                                  ALU.subtract).then_inc(lo_done, 1)

            dve.wait_ge(par_T, 1)
            for t in range(4):
                dve.tensor_copy(params[:, t, 0:par_count[t]], bank[7][:, t * P:t * P + par_count[t]]).then_inc(par_done, 1)
            dve.wait_ge(par_done, 4)
            dve.tensor_tensor(bs[:, :], pool_b, pool_s, ALU.mult).then_inc(bs_done, 1)
            dve.tensor_scalar(sub_g_scaled, sub_g, 1.0 - LAMBDA_INIT, None, ALU.mult).then_inc(subg_done, 1)
            dve.wait_ge(lam_in, 64)
            for i in range(2):
                dve.tensor_tensor(lam_rows[:, 4 + i:5 + i], lam_rows[:, 2 * i:2 * i + 1],
                                  lam_rows[:, 2 * i + 1:2 * i + 2], ALU.mult).then_inc(lam_prod, 1)
            split_lo_qkv(0, 0)

            def x0_copy(kt):
                dve.wait_ge(x_T, kt + 1)
                dve.tensor_copy(h[:, kt, :], bank[kt][:, :]).then_inc(x0_done, 1)

            def x_low(norm, m, g):
                dve.wait_ge(xhi_done, KT * refill[norm] + m + 1)
                dve.scalar_tensor_tensor(out=x_lo[:, m, :], in0=h[:, m, :], scalar=g, in1=x_hi[:, m, :].bitcast(F32),
                                         op0=ALU.mult, op1=ALU.subtract).then_inc(x_ready, 1)

            def inverse(norm):
                dve.wait_ge(rms_done, norm + 1)
                dve.reciprocal(inv[:, :], rms[:, :]).then_inc(inv_done, 1)
                dve.wait_ge(inv_done, norm + 1)

            x0_copy(0)
            for kt in range(1, KT):
                x0_copy(kt)
                x_low(NORM_MIX0, kt - 1, gain(0, MIX, kt - 1))
            x_low(NORM_MIX0, KT - 1, gain(0, MIX, KT - 1))
            dve.wait_ge(tok_ss, TT)
            for t in range(TT):
                dve.tensor_scalar(diag[:, t, :], ident[:, :], tok_sum[:, t:t + 1], None, ALU.mult).then_inc(diag_done, 1)
            split_lo_qkv(0, 1)
            inverse(NORM_MIX0)
            for j in range(DEPTH * PLE_KT):
                dve.wait_ge(pT_hi_done, j + 1)
                dve.tensor_tensor(pT_lo[:, j, :], bank[3 + j % 2][:, :], pT_hi[:, j, :].bitcast(F32),
                                  ALU.subtract).then_inc(pT_done, 1)
            dve.wait_ge(lam_exp, 1)
            dve.tensor_tensor(lam, lam_e[:, 0:1], lam_e[:, 1:2], ALU.subtract).then_inc(lam_diff, 1)
            dve.wait_ge(lam_diff, 1)
            dve.tensor_scalar(lam, lam, LAMBDA_INIT, None, ALU.add).then_inc(lam_done, 1)

            def qk_rows(hd, i):
                dve.wait_ge(unit_done, 3 * hd + i + 1)
                if i:
                    dve.wait_ge(qklo_done, 2 * hd + 1)
                dve.tensor_tensor(qk32[:, :], bank[i][:, :], inv[:, :], ALU.mult).then_inc(qk32_done, 1)

            def qk_low(hd, i, lo, hi):
                dve.wait_ge(qkhi_done, 2 * hd + i + 1)
                dve.tensor_tensor(lo[:, :], qk32[:, :], hi[:, :].bitcast(F32), ALU.subtract).then_inc(qklo_done, 1)

            def softmax_first(hd):
                for qt in range(TT):
                    dve.wait_ge(scores_done, 3 * hd + max(qt, 1))
                    for c in range(2):
                        i = 2 * qt + c
                        dve.tensor_reduce(mx[:, i:i + 1], scores_at(qt, c), AX_X, ALU.max).then_inc(max_done, 1)
                    if qt % 2:
                        neg(hd, qt // 2)

            def neg(hd, half):
                dve.wait_ge(max_done, 2 * TT * hd + 4 * half + 4)
                dve.tensor_scalar(negmx[:, 4 * half:4 * half + 4], mx[:, 4 * half:4 * half + 4], -ATTN_SCALE, None,
                                  ALU.mult).then_inc(neg_done, 1)

            def v_rows(hd):
                dve.wait_ge(unit_done, 3 * hd + 3)
                dve.tensor_tensor(vT[:, :], bank[0][:, :], inv[:, :], ALU.mult).then_inc(vT_done, 1)

            def softmax_second(hd):
                def second(qt):
                    at, w = key_off(qt), (qt + 1) * P
                    dve.tensor_scalar(probs[:, 1, at:at + w], probs[:, 1, at:at + w], rsums[:, 2 * qt + 1:2 * qt + 2], lam,
                                      ALU.mult, ALU.mult).then_inc(second_done, 1)

                def difference(qt):
                    at, w = key_off(qt), (qt + 1) * P
                    dve.wait_ge(second_done, TT * hd + qt + 1)
                    dve.scalar_tensor_tensor(out=probs[:, 0, at:at + w], in0=probs[:, 0, at:at + w],
                                             scalar=rsums[:, 2 * qt:2 * qt + 1], in1=probs[:, 1, at:at + w],
                                             op0=ALU.mult, op1=ALU.subtract).then_inc(w_done, 1)

                dve.wait_ge(exp_done, 2 * TT * (hd + 1))
                dve.reciprocal(rsums, sums).then_inc(rsum_done, 1)
                dve.wait_ge(rsum_done, hd + 1)
                second(0)
                for qt in range(1, TT):
                    second(qt)
                    difference(qt - 1)
                difference(TT - 1)

            def back_first(hp):
                dve.wait_ge(vhi_done, hp + 1)
                dve.tensor_tensor(v_lo[:, :, :].rearrange("p t c -> p (t c)"), bank[5][:, :],
                                  v_hi[:, :, :].rearrange("p t c -> p (t c)").bitcast(F32), ALU.subtract).then_inc(vlo_done, 1)
                for b, (at, w) in enumerate(WT_BANKS):
                    dve.wait_ge(wthi_done, 3 * hp + b + 1)
                    dve.tensor_tensor(wT_lo[:, at:at + w], bank[2 + b][:, 0:w], wT_hi[:, at:at + w].bitcast(F32),
                                      ALU.subtract).then_inc(wtlo_done, 1)

            def back_second(hp):
                dve.wait_ge(bank1_free, hp + 2)
                dve.reciprocal(sq[:, 1, :], rms[:, :]).then_inc(oinv_done, 1)
                dve.wait_ge(oinv_done, hp + 1)
                dve.tensor_tensor(o32[:, :], o32[:, :], sq[:, 1, :], ALU.mult).then_inc(onorm_done, 1)
                dve.wait_ge(ohi_done, hp + 1)
                dve.tensor_tensor(oT_lo[:, hp, :], o32[:, :], oT_hi[:, hp, :].bitcast(F32), ALU.subtract).then_inc(olo_done, 1)

            def head(hd, back, split_next):
                qk_rows(hd, 0)
                split_lo_qkv(hd, 2)
                qk_low(hd, 0, q_lo, q_hi)
                if back:
                    back_first(hd - 1)
                split_next(0)
                qk_rows(hd, 1)
                qk_low(hd, 1, k_lo, k_hi)
                softmax_first(hd)
                split_next(1)
                v_rows(hd)
                softmax_second(hd)
                if back:
                    back_second(hd - 1)

            head(0, False, lambda i: split_lo_qkv(1, i))
            with dve.Fori(1, N_HEADS - 1) as hd:
                head(hd, True, lambda i: split_lo_qkv(hd + 1, i))
            head(N_HEADS - 1, True, lambda i: split_lo(FIRST_RING4 + i))
            back_first(N_HEADS - 1)
            back_second(N_HEADS - 1)

            def residual_add(n, m, src):
                dve.tensor_tensor(h[:, m, :], src, h[:, m, :], ALU.add).then_inc(evac_done, 1)

            def sum_squares(n_sq):
                dve.wait_ge(sq_done, n_sq + 1)
                if n_sq % KT:
                    dve.wait_ge(acc_done, n_sq)
                else:
                    dve.wait_ge(acc_zero, n_sq // KT + 1)
                dve.tensor_tensor(acc[:, :], acc[:, :], sq[:, n_sq % 2, :], ALU.add).then_inc(acc_done, 1)

            def residual_phase(name, norm, layer, which):
                for m in range(KT):
                    n = PHASES[name][0] + m
                    split_lo(n + LOOK)
                    dve.wait_ge(unit_done, n + 1)
                    residual_add(n, m, bank[m % SLOTS][:, :])
                    if norm is not None:
                        x_low(norm, m, gain(layer, which, m))
                        sum_squares(KT * sums_of[norm] + m)

            def norm_end(norm):
                inverse(norm)
                dve.memset(acc[:, :], 0.0).then_inc(acc_zero, 1)

            def loop(name, body):
                bodies = PHASES[name][1] // SLOTS
                with dve.Fori(0, bodies - 1) as a:
                    body(a)
                body(bodies - 1)

            def look_lo(name, u, a):
                n = PHASES[name][0] + u + LOOK
                if isinstance(a, int):
                    split_lo(n + SLOTS * a)
                else:
                    split_lo(n, a)

            dve.wait_ge(olo_done, N_HEADS)
            dve.memset(acc[:, :], 0.0).then_inc(acc_zero, 1)
            residual_phase("wo", NORM_FFN0, 0, FFN)
            dve.memset(u32[:, :, 0:PAD], 0.0).then_inc(pad_zero, 1)
            dve.memset(hn[:, 0:PAD], 0.0).then_inc(pad_zero, 1)
            dve.wait_ge(pad_zero, 2)
            for layer in range(DEPTH):
                if layer:
                    norm_end(NORM_MIX1)
                    first = PHASES["pool"][0]
                    dve.wait_ge(edge_done, sum(POOL_WINDOWS) - len(POOL_WINDOWS))

                    def pool_low(c):
                        dve.wait_ge(xhi_done, KT * refill[NORM_MIX1] + c + 1)
                        dve.tensor_tensor(x_lo[:, c, :], c32[:, c % 2, :], x_hi[:, c, :].bitcast(F32),
                                          ALU.subtract).then_inc(x_ready, 1)

                    wins = 0
                    for c in range(KT):
                        g = c // POOL_KT
                        win = POOL_WINDOWS[g]
                        if c:
                            dve.wait_ge(y32_done, c)
                        dve.scalar_tensor_tensor(out=hn[:, PAD:], in0=h[:, c, :], scalar=gain(1, MIX, c), in1=inv[:, :],
                                                 op0=ALU.mult, op1=ALU.mult).then_inc(hn_done, 1)
                        dve.wait_ge(hn_done, c + 1)
                        src = hn[:, :]
                        for level in range(g + 1):
                            back = 2 ** level
                            dve.tensor_tensor(u32[:, level % 2, PAD:], src[:, PAD:PAD + SEQ],
                                              src[:, PAD - back:PAD - back + SEQ], ALU.add).then_inc(win_done, 1)
                            wins += 1
                            dve.wait_ge(win_done, wins)
                            src = u32[:, level % 2, :]
                        dve.tensor_tensor(src[:, PAD:2 * PAD], src[:, PAD:2 * PAD], edge[:, g, :],
                                          ALU.mult).then_inc(fix_done, 1)
                        dve.wait_ge(fix_done, c + 1)
                        dve.scalar_tensor_tensor(out=c32[:, c % 2, :], in0=src[:, PAD:PAD + SEQ], scalar=1.0 / win,
                                                 in1=hn[:, PAD:], op0=ALU.mult, op1=ALU.subtract).then_inc(y32_done, 1)
                        if c:
                            pool_low(c - 1)
                    pool_low(KT - 1)
                    for m in range(KT):
                        split_lo(first + m + LOOK)
                        dve.wait_ge(mixed_done, m + 1)
                        residual_add(first + m, m, (s32, g32)[m % 2][:, :])
                        x_low(NORM_FFN1, m, gain(1, FFN, m))
                        sum_squares(KT * sums_of[NORM_FFN1] + m)
                norm_end(NORM_FFN1 if layer else NORM_FFN0)
                done = 0
                for part, tiles in enumerate(FFN_PARTS):
                    name = f"up{layer}{part}"
                    pairs = layer * FT + done

                    def up_body(a):
                        for v in range(2):
                            j = 2 * a + v + done
                            pair = 2 * a + v + pairs
                            for c in range(2):
                                n = PHASES[name][0] + 2 * v + c
                                dve.wait_ge(unit_done, SLOTS * a + n + 1)
                                dve.tensor_tensor(u32[:, c, PAD:], bank[2 * v + c][:, :], inv[:, :],
                                                  ALU.mult).then_inc(evac_done, 1)
                                look_lo(name, 2 * v + c, a)
                                dve.wait_ge(tap_done, 2 * pair + c + 1)
                                dve.scalar_tensor_tensor(
                                    out=c32[:, c, :], in0=u32[:, c, PAD - 1:PAD - 1 + SEQ],
                                    scalar=tap(layer, 1, j + c * FT), in1=c32[:, c, :],
                                    op0=ALU.mult, op1=ALU.add).then_inc(conv1_done, 1)
                                dve.wait_ge(conv1_done, 2 * pair + c + 1)
                                dve.scalar_tensor_tensor(
                                    out=c32[:, c, :], in0=u32[:, c, PAD - 2:PAD - 2 + SEQ],
                                    scalar=tap(layer, 0, j + c * FT), in1=c32[:, c, :],
                                    op0=ALU.mult, op1=ALU.add).then_inc(conv_done, 1)
                            dve.wait_ge(silu_done, pair + 1)
                            dve.wait_ge(conv_done, 2 * pair + 2)
                            dve.tensor_tensor(g32[:, :], s32[:, :], c32[:, 1, :], ALU.mult).then_inc(gmul_done, 1)
                            dve.wait_ge(ghi_done, pair + 1)
                            dve.tensor_tensor(g_lo[:, 2 * a + v, :], g32[:, :], g_hi[:, 2 * a + v, :].bitcast(F32),
                                              ALU.subtract).then_inc(glo_done, 1)

                    loop(name, up_body)
                    norm = (NORM_PLE1 if layer else NORM_PLE0) if part == LAST else None
                    residual_phase(f"down{layer}{part}", norm, layer, PLE)
                    done += tiles
                norm_end(NORM_PLE1 if layer else NORM_PLE0)
                after = 6 if layer else NORM_MIX1
                for m in range(KT):
                    n = PHASES[f"ple{layer}"][0] + m
                    dve.wait_ge(unit_done, n + 1)
                    dve.tensor_tensor(c32[:, 0, :], bank[m % SLOTS][:, :], inv[:, :], ALU.mult).then_inc(z_done, 1)
                    split_lo(n + LOOK)
                    dve.wait_ge(sig_done, KT * layer + m + 1)
                    dve.tensor_tensor(c32[:, 1, :], bank[4 + m % 2][:, :], s32[:, :], ALU.mult).then_inc(ple_done, 1)
                    dve.wait_ge(ple_done, KT * layer + m + 1)
                    residual_add(n, m, c32[:, 1, :])
                    sum_squares(KT * sums_of[after] + m)
            dve.wait_ge(fin_rms, 1)
            dve.reciprocal(fin_icol, fin_col).then_inc(fin_inv, 1)
            dve.wait_ge(fin_inv, 1)
            dve.wait_ge(gfin_in, 16)
            dve.wait_ge(y_copied, KT)
            for t in range(TT):
                dve.scalar_tensor_tensor(out=y_tok[:, t, :], in0=y_tok[:, t, :], scalar=fin_icol[:, t:t + 1],
                                         in1=g_final[:, :], op0=ALU.mult, op1=ALU.mult).then_inc(y_normed, 1)

        @block.tensor
        def _(pe):
            def exact(dst, parts, start=True, stop=True):
                for i, ((w1, w0), (m1, m0), before) in enumerate(parts):
                    before()
                    pe.matmul(dst, w1, m1, start=start and i == 0, stop=False)
                    pe.matmul(dst, w1, m0, start=False, stop=False)
                    last = pe.matmul(dst, w0, m1, start=False, stop=stop and i == len(parts) - 1)
                return last

            def no_wait():
                pass

            def block_of(slot, k):
                return w_hi[slot][:, k * P:(k + 1) * P], w_lo[slot][:, k * P:(k + 1) * P]

            def x_parts(slot, ready=None):
                def wait(k):
                    return (lambda: pe.wait_ge(x_ready, ready + k)) if ready else no_wait
                return [(block_of(slot, k), (x_hi[:, k, :], x_lo[:, k, :]), wait(k)) for k in range(KT)]

            def y_transposes(m):
                pe.wait_ge(evac_done, evacuated(PHASES[f"ple{DEPTH - 1}"][0] + m))
                if m >= 2:
                    pe.wait_ge(y_copied, m - 1)
                else:
                    pe.wait_ge(rms_done, NORM_PLE1 + 1)
                for t in range(TT):
                    last = pe.transpose(bank[6 + m % 2][:, t * P:(t + 1) * P], h[:, m, t * P:(t + 1) * P], ident[:, :])
                last.then_inc(y_T, 1)

            pe.wait_ge(const_done, 3)
            pe.wait_ge(par_in, 16 * (6 * DEPTH + 3))
            for t in range(4):
                last = pe.transpose(bank[7][:, t * P:t * P + par_count[t]], par_rows[0:par_count[t], t, :],
                                    ident[0:par_count[t], 0:par_count[t]])
            last.then_inc(par_T, 1)
            for t in range(TT):
                pe.wait_ge(x_in[t], 16)
                for kt in range(KT):
                    if t == 0 and kt == KT - 1:
                        pe.wait_ge(par_done, 4)
                    last = pe.transpose(bank[kt][:, t * P:(t + 1) * P], x_tok[:, t, kt * P:(kt + 1) * P], ident[:, :])
                    if t == TT - 1:
                        last.then_inc(x_T, 1)

            def project(hd, which, before):
                pe.wait_ge(lo_done, 3 * hd + which + 1)
                before()
                ready = 1 if isinstance(hd, int) and hd == 0 and which == 0 else None
                exact(bank[which % 2][:, :], x_parts(which, ready)).then_inc(unit_done, 1)

            def scores(hd, first):
                pe.wait_ge(qklo_done, 2 * hd + 2)
                for qt in range(TT):
                    if not first:
                        if qt == 0:
                            pe.wait_ge(wtlo_done, 3 * hd - 1)
                        if qt == 2:
                            pe.wait_ge(wtlo_done, 3 * hd)
                            pe.wait_ge(vlo_done, hd)
                        if qt == 3:
                            pe.wait_ge(osq_done, hd)
                            pe.wait_ge(exp_done, 2 * TT * hd)
                    w = (qt + 1) * P
                    dst = [scores_at(qt, c) for c in range(2)]
                    rows = [slice(HEAD_DIM * c, HEAD_DIM * (c + 1)) for c in range(2)]
                    keys = slice(qt * P, (qt + 1) * P)
                    for i, (q, k) in enumerate(((q_hi, k_hi), (q_hi, k_lo), (q_lo, k_hi))):
                        for c in range(2):
                            pe.matmul(dst[c], q[rows[c], keys], k[rows[c], 0:w], start=i == 0, stop=False)
                    for c in range(2):
                        last = pe.matmul(dst[c][:, w - P:w], ident16[:, :], mask16[:, :], start=False, stop=True)
                    if qt:
                        last.then_inc(scores_done, 1)

            def back_transposes(hp):
                pe.wait_ge(vT_done, hp + 1)
                pe.wait_ge(exp_done, 2 * TT * (hp + 1))
                for t in range(TT):
                    last = pe.transpose(bank[5][:, t * P:(t + 1) * P], vT[:, t * P:(t + 1) * P], ident[:, :])
                last.then_inc(v_T, 1)
                pe.wait_ge(w_done, TT * (hp + 1))
                for kt in range(TT):
                    for qt in range(kt, TT):
                        b = min(kt, 2)
                        at = wt_off(kt) + (qt - kt) * P - WT_BANKS[b][0]
                        src = key_off(qt) + kt * P
                        last = pe.transpose(bank[2 + b][:, at:at + P], probs[:, 0, src:src + P], ident[:, :])
                    if kt != 2:
                        last.then_inc(w_T, 1)

            def back_product(hp):
                pe.wait_ge(vlo_done, hp + 1)
                for kt in range(TT):
                    pe.wait_ge(wtlo_done, 3 * hp + min(kt, 2) + 1)
                    at, w = wt_off(kt), (TT - kt) * P
                    last = exact(bank[6][:, kt * P:SEQ],
                                 [((v_hi[:, kt, :], v_lo[:, kt, :]), (wT_hi[:, at:at + w], wT_lo[:, at:at + w]), no_wait)],
                                 start=kt == 0, stop=kt == TT - 1)
                last.then_inc(pv_done, 1)

            def back_norm(hp):
                pe.wait_ge(osq_done, hp + 1)
                pe.matmul(bank[1][:, :], ones[:, :], sq[:, 0, :], start=True, stop=True).then_inc(oss_done, 1)

            def head(hd, back):
                project(hd, 0, (lambda: pe.wait_ge(vT_done, hd)) if back else no_wait)
                if back:
                    back_transposes(hd - 1)
                else:
                    pe.wait_ge(diag_done, TT)
                    for t in range(TT):
                        last = pe.matmul(bank[2][:, t * P:(t + 1) * P], ones[:, :], diag[:, t, :], start=True, stop=True)
                    last.then_inc(ss_done, 1)
                    pe.wait_ge(p_in, 16)
                    for j in range(DEPTH * PLE_KT):
                        i, k = divmod(j, PLE_KT)
                        if j >= 2:
                            pe.wait_ge(pT_done, j - 1)
                        for t in range(TT):
                            last = pe.transpose(bank[3 + j % 2][:, t * P:(t + 1) * P],
                                                p_tok[:, i * TT + t, k * P:(k + 1) * P], ident[:, :])
                        last.then_inc(p_T, 1)
                    pe.wait_ge(lam_prod, 2)
                    pe.matmul(bank[7][:, 0:2], ones[0:HEAD_DIM, :], lam_rows[:, 4:6], start=True, stop=True)\
                        .then_inc(lam_sum, 1)
                project(hd, 1, (lambda: pe.wait_ge(bank1_free, hd)) if back else no_wait)
                if back:
                    back_product(hd - 1)
                else:
                    pe.wait_ge(mask_done, 2)
                    pe.wait_ge(pT_done, DEPTH * PLE_KT)
                    pe.wait_ge(lam_exp, 1)
                scores(hd, not back)
                project(hd, 2, lambda: pe.wait_ge(qk32_done, 2 * hd + 1))
                if back:
                    back_norm(hd - 1)

            head(0, False)
            with pe.Fori(1, N_HEADS) as hd:
                head(hd, True)
            back_transposes(N_HEADS - 1)
            back_product(N_HEADS - 1)
            back_norm(N_HEADS - 1)

            def unit(name, u, a, parts, dst=None):
                n = PHASES[name][0] + u
                pe.wait_ge(lo_done, SLOTS * a + n + 1)
                if n >= FIRST_RING4 + SLOTS:
                    pe.wait_ge(evac_done, SLOTS * a + evacuated(n - SLOTS))
                return exact(bank[u % SLOTS][:, :] if dst is None else dst, parts)

            def mean_squares(norm, k):
                pe.wait_ge(acc_done, KT * (k + 1))
                pe.matmul(bank[6][:, :], ones[:, :], acc[:, :], start=True, stop=True).then_inc(ss_done, 1)

            for m in range(KT):
                def o_ready(k, m=m):
                    return (lambda: pe.wait_ge(olo_done, k + 1)) if m == 0 else no_wait
                slot = slot_of(FIRST_RING4 + m)
                pe.wait_ge(lo_done, FIRST_RING4 + m + 1)
                if m >= SLOTS:
                    pe.wait_ge(evac_done, evacuated(FIRST_RING4 + m - SLOTS))
                exact(bank[m % SLOTS][:, :], [(block_of(slot, k), (oT_hi[:, k, :], oT_lo[:, k, :]), o_ready(k))
                                              for k in range(N_HEADS)]).then_inc(unit_done, 1)
            for layer in range(DEPTH):
                if layer:
                    mean_squares(NORM_MIX1, sums_of[NORM_MIX1])
                    for m in range(KT):
                        slot = slot_of(PHASES["pool"][0] + m)
                        c = m // POOL_KT * POOL_KT
                        unit("pool", m, 0, [
                            (block_of(slot, k), (x_hi[:, c + k, :], x_lo[:, c + k, :]),
                             (lambda k=k: pe.wait_ge(x_ready, KT * refill[NORM_MIX1] + c + k + 1)))
                            for k in range(POOL_KT)]).then_inc(unit_done, 1)
                norm = NORM_FFN1 if layer else NORM_FFN0
                for part, tiles in enumerate(FFN_PARTS):
                    name = f"up{layer}{part}"

                    def up_body(a, first):
                        for u in range(SLOTS):
                            ready = KT * refill[norm] + 1 if first and u == 0 else None
                            unit(name, u, a, x_parts(slot_of(PHASES[name][0] + u), ready)).then_inc(unit_done, 1)
                            if first and u == 0:
                                mean_squares(norm, sums_of[norm])

                    if part == 0:
                        up_body(0, True)
                    with pe.Fori(1 if part == 0 else 0, PHASES[name][1] // SLOTS) as a:
                        up_body(a, False)
                    name = f"down{layer}{part}"
                    pairs = layer * FT + sum(FFN_PARTS[:part])
                    with pe.Fori(0, KT // SLOTS) as a:
                        for u in range(SLOTS):
                            slot = slot_of(PHASES[name][0] + u)
                            unit(name, u, a, [
                                (block_of(slot, k), (g_hi[:, k, :], g_lo[:, k, :]),
                                 (lambda k=k: pe.wait_ge(glo_done, pairs + k + 1)) if u == 0 else no_wait)
                                for k in range(tiles)]).then_inc(unit_done, 1)
                norm = NORM_PLE1 if layer else NORM_PLE0
                name = f"ple{layer}"
                for m in range(KT):
                    slot = slot_of(PHASES[name][0] + m)
                    unit(name, m, 0, x_parts(slot, KT * refill[norm] + 1 if m == 0 else None))
                    if m >= 2:
                        pe.wait_ge(evac_done, evacuated(PHASES[name][0] + m - 2))
                    if m == 0:
                        pe.wait_ge(pT_done, DEPTH * PLE_KT)
                    exact(bank[4 + m % 2][:, :], [
                        (block_of(slot, KT + k), (pT_hi[:, layer * PLE_KT + k, :], pT_lo[:, layer * PLE_KT + k, :]), no_wait)
                        for k in range(PLE_KT)]).then_inc(unit_done, 1)
                    if m == 0:
                        mean_squares(norm, sums_of[norm])
                    if layer == DEPTH - 1 and m > 0:
                        y_transposes(m - 1)
            y_transposes(KT - 1)
            pe.wait_ge(acc_done, KT * (sums_of[6] + 1))
            for t in range(TT):
                last = pe.matmul(bank[4][:, t:t + 1], acc[:, t * P:(t + 1) * P], ones[:, 0:1], start=True, stop=True)
            last.then_inc(fin_ss, 1)


_INS = ['x', 'p', 'mix_norm_g', 'w_qkv', 'lam_q1', 'lam_k1', 'lam_q2', 'lam_k2', 'attn_sub_g', 'w_attn_out',
        'w_pool', 'b_pool', 'pool_scale', 'ffn_norm_g', 'w_up', 'conv_w', 'conv_b', 'w_down',
        'ple_norm_g', 'w_ple_gate', 'w_ple_proj', 'final_norm_g']


def kernel(**inputs):
    import concourse.bacc as bacc
    from concourse.bass_utils import run_bass_kernel_spmd

    nc = bacc.Bacc("TRN2", target_bir_lowering=False, num_devices=1)
    arrays, args = {}, []
    for name in _INS:
        a = np.ascontiguousarray(inputs[name])
        arrays[f"in_{name}"] = a
        args.append(nc.dram_tensor(f"in_{name}", a.shape, mybir.dt.from_np(a.dtype), kind="ExternalInput").ap())
    result = nc.dram_tensor("out", (1, SEQ, D_MODEL), F32, kind="ExternalOutput").ap()
    hybrid_trunk(nc, *args, result)
    r = run_bass_kernel_spmd(nc, [arrays], core_ids=[0])
    return r.results[0]["out"]
```

```python
import math
from contextlib import ExitStack

import numpy as np

import concourse.bass as bass
from concourse import mybir

F32 = mybir.dt.float32
F32R = mybir.dt.float32r
BF16 = mybir.dt.bfloat16
ALU = mybir.AluOpType
ACT = mybir.ActivationFunctionType
AX_X = mybir.AxisListType.X

P = 128
D_MODEL = 1024
SEQ = 512
DEPTH = 2
N_HEADS = 8
HEAD_DIM = 64
POOL_WINDOWS = (2, 4, 8, 16)
D_FF = 2816
PLE_DIM = 256
EPS = 1e-6
ATTN_SCALE = HEAD_DIM ** -0.5
LAMBDA_INIT = 0.8 - 0.6 * math.exp(-0.3 * 0)
MASKED = -1e30

KT = D_MODEL // P
TT = SEQ // P
FT = D_FF // P
PLE_KT = PLE_DIM // P
POOL_KT = D_MODEL // len(POOL_WINDOWS) // P
FFN_PARTS = (8, 8, 6)
SLOTS = 4
UNIT_BLOCKS = KT
LOOK = 2
PAD = 2
EDGE = max(POOL_WINDOWS)
BAND = P + EDGE


def plan():
    phases, before, n, results = {}, {}, 0, 0

    def add(name, units, blocks, gives):
        nonlocal n, results
        phases[name], before[name] = (n, units, blocks), results
        n, results = n + units, results + gives

    add("qkv", 3 * N_HEADS, KT, 0)
    add("wo", KT, KT, KT)
    add("emb0", 2, KT, 0)
    for layer in range(DEPTH):
        if layer:
            add("emb1a", 1, KT, 0)
            add("pool", 2, KT, KT)
            add("emb1b", 1, KT, 0)
        for part, tiles in enumerate(FFN_PARTS):
            add(f"up{layer}{part}", 2 * tiles, KT, 2 * tiles)
            add(f"down{layer}{part}", KT, tiles, KT)
        add(f"ple{layer}", KT, KT, KT)
    return phases, before, n


PHASES, RESULTS_BEFORE, N_UNITS = plan()
FIRST_RING4 = 3 * N_HEADS


def blocks_of(n):
    return next(b for first, units, b in PHASES.values() if first <= n < first + units)


def slot_of(n):
    return n % 3 if n < FIRST_RING4 else (n + 3) % SLOTS


def uses_before(n):
    if n < FIRST_RING4:
        return n // 3
    return (n - FIRST_RING4) // SLOTS + (N_HEADS if slot_of(n) != 3 else 0)


def landed(n, a=0):
    return 16 * (uses_before(n) + 1) + 16 * a


def result_of(name, u):
    return RESULTS_BEFORE[name] + u + 1


def hybrid_trunk(nc, x, p, mix_norm_g, w_qkv, lam_q1, lam_k1, lam_q2, lam_k2, attn_sub_g, w_attn_out,
                 w_pool, b_pool, pool_scale, ffn_norm_g, w_up, conv_w, conv_b, w_down,
                 ple_norm_g, w_ple_gate, w_ple_proj, final_norm_g, out):
    with ExitStack() as ctx:
        def sem(name):
            return ctx.enter_context(nc.semaphore(name))

        def sb(name, shape, dt, scope=ctx):
            return scope.enter_context(nc.sbuf_tensor(name, shape, dt))

        w_raw = [sb(f"w_raw{s}", [P, UNIT_BLOCKS * P], F32) for s in range(SLOTS)]
        w_hi = [sb(f"w_hi{s}", [P, UNIT_BLOCKS * P], F32R) for s in range(SLOTS)]
        w_lo = [sb(f"w_lo{s}", [P, UNIT_BLOCKS * P], F32R) for s in range(SLOTS)]
        h = sb("h", [P, KT, SEQ], F32)
        x_hi = sb("x_hi", [P, KT, SEQ], F32R)
        x_lo = sb("x_lo", [P, KT, SEQ], F32R)
        pT_hi = sb("pT_hi", [P, DEPTH * PLE_KT, SEQ], F32R)
        pT_lo = sb("pT_lo", [P, DEPTH * PLE_KT, SEQ], F32R)
        inv = sb("inv", [P, SEQ], F32)
        sq = sb("sq", [P, 2, SEQ], F32)
        diag = sq[:, 1, :].rearrange("p (t c) -> p t c", c=P)
        acc = sb("acc", [P, SEQ], F32)
        params = sb("params", [P, 4, P], F32)
        ident = sb("ident", [P, P], F32)
        ones = sb("ones", [P, P], F32)
        eps = sb("eps", [P, 1], F32)
        small = sb("small", [P, 64], F32)
        gain0 = sb("gain0", [P, KT], F32)
        bs = sb("bs", [P, KT], F32)
        ident16 = sb("ident16", [P, P], BF16)
        mask16 = sb("mask16", [P, P], BF16)

        start = ExitStack()
        x_tok = sb("x_tok", [P, TT, D_MODEL], F32, start)
        p_tok = sb("p_tok", [P, DEPTH * TT, PLE_DIM], F32, start)
        par_rows = sb("par_rows", [P, 4, P], F32, start)
        lam_rows = sb("lam_rows", [HEAD_DIM, 8], F32, start)
        gain0_rows = sb("gain0_rows", [KT, P], F32, start)
        square_scratch = sb("square_scratch", [P, D_MODEL], F32, start)
        start.close()

        attn = ExitStack()
        oT_hi = sb("oT_hi", [P, N_HEADS, SEQ], F32R, attn)
        oT_lo = sb("oT_lo", [P, N_HEADS, SEQ], F32R, attn)
        k32 = sb("k32", [P, SEQ], F32, attn)
        q_hi = sb("q_hi", [P, 2, SEQ], F32R, attn)
        q_lo = sb("q_lo", [P, 2, SEQ], F32R, attn)
        k_hi = sb("k_hi", [P, SEQ], F32R, attn)
        k_lo = sb("k_lo", [P, SEQ], F32R, attn)
        vT = sb("vT", [P, SEQ], F32, attn)
        v_hi = sb("v_hi", [P, TT, P], F32R, attn)
        v_lo = sb("v_lo", [P, TT, P], F32R, attn)
        CAUSAL = P * TT * (TT + 1) // 2
        probs = sb("probs", [P, 2, CAUSAL], F32, attn)
        wT_hi = sb("wT_hi", [P, CAUSAL], F32R, attn)
        wT_lo = sb("wT_lo", [P, CAUSAL], F32R, attn)
        o32 = acc
        attn.close()

        ffn = ExitStack()
        g_hi = sb("g_hi", [P, KT, SEQ], F32R, ffn)
        g_lo = sb("g_lo", [P, KT, SEQ], F32R, ffn)
        u32 = sb("u32", [P, 2, PAD + SEQ], F32, ffn)
        c32 = sb("c32", [P, 2, SEQ], F32, ffn)
        s32 = sb("s32", [P, SEQ], F32, ffn)
        g32 = sb("g32", [P, SEQ], F32, ffn)
        emb = sb("emb", [P, KT, SEQ], F32, ffn)
        xp_hi, xp_lo = g_hi, g_lo
        z0_hi = sb("z0_hi", [P, TT, SEQ], F32R, ffn)
        z0_lo = sb("z0_lo", [P, TT, SEQ], F32R, ffn)
        z_hi, z_lo = (z0_hi, g_hi), (z0_lo, g_lo)
        G = len(POOL_WINDOWS)
        band32 = sb("band32", [P, G, BAND], F32, ffn)
        edge32 = sb("edge32", [P, G, EDGE], F32, ffn)
        band = sb("band", [P, G, BAND], F32R, ffn)
        edge_hi = sb("edge_hi", [P, G, EDGE], F32R, ffn)
        edge_lo = sb("edge_lo", [P, G, EDGE], F32R, ffn)
        ffn.close()

        tail = ExitStack()
        y_tok = sb("y_tok", [P, TT, D_MODEL], F32, tail)
        y_gained = sb("y_gained", [P, KT, SEQ], F32, tail)
        tail.close()

        bank = [ctx.enter_context(nc.psum_tensor(f"bank{b}", [P, SEQ], F32)) for b in range(8)]

        raw_in = [sem(f"raw_in{s}") for s in range(SLOTS)]
        hi_done, lo_done, unit_done, evac_done = sem("hi_done"), sem("lo_done"), sem("unit_done"), sem("evac_done")
        x_in = [sem(f"x_in{t}") for t in range(TT)]
        par_in, p_in, lam_in = sem("par_in"), sem("p_in"), sem("lam_in")
        gain0_in, gain0_T, gain0_done = sem("gain0_in"), sem("gain0_T"), sem("gain0_done")
        ident_zero, const_done, mask_done = sem("ident_zero"), sem("const_done"), sem("mask_done")
        par_T, par_done, x_T, p_T, pT_hi_done, pT_done = (
            sem("par_T"), sem("par_done"), sem("x_T"), sem("p_T"), sem("pT_hi_done"), sem("pT_done"))
        tok_ss, qpad_zero, qscale_done = sem("tok_ss"), sem("qpad_zero"), sem("qscale_done")
        lam_prod, lam_sum, lam_exp, lam_diff, lam_done, subg_done = (
            sem("lam_prod"), sem("lam_sum"), sem("lam_exp"), sem("lam_diff"), sem("lam_done"), sem("subg_done"))
        h_dve, h_act = sem("h_dve"), sem("h_act")
        xhi_done, x_ready, sq_done, acc_done = sem("xhi_done"), sem("x_ready"), sem("sq_done"), sem("acc_done")
        ss_done, rms_done, icol_done, diag_done, spread_done, inv_done = (
            sem("ss_done"), sem("rms_done"), sem("icol_done"), sem("diag_done"), sem("spread_done"), sem("inv_done"))
        qhi_done, qlo_done, k32_done, khi_done, klo_done = (
            sem("qhi_done"), sem("qlo_done"), sem("k32_done"), sem("khi_done"), sem("klo_done"))
        v_T, vhi_done, vlo_done = sem("v_T"), sem("vhi_done"), sem("vlo_done")
        scores_done, max_done, neg_done, exp_done = sem("scores_done"), sem("max_done"), sem("neg_done"), sem("exp_done")
        rsum_done, second_done, w_done = sem("rsum_done"), sem("second_done"), sem("w_done")
        w_T, wthi_done, wtlo_done = sem("w_T"), sem("wthi_done"), sem("wtlo_done")
        pv_done, o32_done, osq_done, oss_done, orms_done, oicol_done, odiag_done, ospread_done = (
            sem("pv_done"), sem("o32_done"), sem("osq_done"), sem("oss_done"), sem("orms_done"), sem("oicol_done"),
            sem("odiag_done"), sem("ospread_done"))
        onorm_done, ohi_done, olo_done = sem("onorm_done"), sem("ohi_done"), sem("olo_done")
        pad_zero, vT_done, tap_done, conv1_done, conv_done, silu_done, gmul_done, ghi_done, glo_done = (
            sem("pad_zero"), sem("vT_done"), sem("tap_done"), sem("conv1_done"), sem("conv_done"), sem("silu_done"),
            sem("gmul_done"), sem("ghi_done"), sem("glo_done"))
        emb_mm, emb_done, arg_done, sig_done, ple_done = (
            sem("emb_mm"), sem("emb_done"), sem("arg_done"), sem("sig_done"), sem("ple_done"))
        bs_done, h_biased = sem("bs_done"), sem("h_biased")
        band_one, band_below, band_set, band_diff, band_done, edge_done = (
            sem("band_one"), sem("band_below"), sem("band_set"), sem("band_diff"), sem("band_done"), sem("edge_done"))
        z_mm, zhi_done, zlo_done, pool_mm = sem("z_mm"), sem("zhi_done"), sem("zlo_done"), sem("pool_mm")
        gained_done, y_T, y_copied, y_dve, y_act, out_done = (
            sem("gained_done"), sem("y_T"), sem("y_copied"), sem("y_dve"), sem("y_act"), sem("out_done"))
        table_loaded = sem("table_loaded")

        CH = 2 * FT

        def tap(layer, w, j):
            return params[:, 2 * layer + w // 2, bass.ds((w % 2) * CH + j, 1)]

        def conv_bias(layer, j):
            return params[:, 2 * layer + 1, bass.ds(CH + j, 1)]

        MIX, FFN, PLE = 0, 1, 2

        def gain(layer, which, kt):
            return params[:, 2 * layer, bass.ds(2 * CH + which * KT + kt, 1)]

        B_POOL = 2 * CH + 3 * KT
        pool_b = params[:, 0, B_POOL:B_POOL + KT]
        pool_s = params[:, 0, B_POOL + KT:B_POOL + 2 * KT]
        sub_g = params[:, 1, 2 * CH:2 * CH + 1]
        final_gain = params[:, 1, 2 * CH + 1:2 * CH + 1 + KT]
        par_count = [2 * CH + 5 * KT, 2 * CH + 1 + KT, 2 * CH + 3 * KT, 2 * CH]

        tok_sum = small[:, 0:TT]
        lam = small[:, 8:9]
        lam_e = small[:, 9:11]
        sub_g_scaled = small[:, 11:12]
        mx = small[:, 16:24]
        negmx = small[:, 24:32]
        sums = small[:, 32:40]
        rsums = small[:, 40:48]
        rms_col = small[:, 48:52]
        icol = small[:, 52:56]
        qscale = small[:, 56:60]
        neg_qscale = small[:, 12:16]
        orms_col = small[:, 4:8]
        oicol = small[:, 60:64]
        table_scratch = small[:, 8:9]

        NORM_MIX0, NORM_FFN0, NORM_PLE0, NORM_MIX1, NORM_FFN1, NORM_PLE1, NORM_FINAL = range(7)
        spread_of = {NORM_MIX0: 1, NORM_FFN0: 2, NORM_PLE0: 3, NORM_FFN1: 4, NORM_PLE1: 5}
        LAST = len(FFN_PARTS) - 1

        def key_off(qt):
            return P * qt * (qt + 1) // 2

        def wt_off(kt):
            return P * (kt * TT - kt * (kt - 1) // 2)

        def scores_at(qt, c):
            at = P * qt if qt < 2 else 0
            return bank[2 + 2 * max(qt - 1, 0) + c][:, at:at + (qt + 1) * P]

        WT_BANKS = [(0, 512), (512, 384), (896, 384)]

        block = ctx.enter_context(nc.Block())

        @block.sync
        def _(sp):
            x_view = x.rearrange("b (t p) d -> p (b t) d", p=P)

            def load(slot, blocks, src, width=P):
                dst = w_raw[slot][:, 0:blocks * P].rearrange("p (k c) -> p k c", c=width)
                return sp.dma_start(dst, src)

            wq = w_qkv[0].rearrange("(k p) f -> p k f", p=P)

            def load_qkv(hd, which):
                load(which, KT, wq[:, :, bass.ds(hd * P + which * D_MODEL, P)]).then_inc(raw_in[which], 16)

            for t in range(TT):
                sp.dma_start(x_tok[:, t, :], x_view[:, t, :]).then_inc(x_in[t], 16)
            for which in range(3):
                load_qkv(0, which)

            def rows(t, at, src):
                sp.dma_start(par_rows[at:at + src.shape[0], t, :], src).then_inc(par_in, 16)

            for i in range(DEPTH):
                rows(2 * i, 0, conv_w[i, 0:2].rearrange("w (j p) -> (w j) p", p=P))
                rows(2 * i, 2 * CH, mix_norm_g[i].rearrange("(j p) -> j p", p=P))
                rows(2 * i, 2 * CH + KT, ffn_norm_g[i].rearrange("(j p) -> j p", p=P))
                rows(2 * i, 2 * CH + 2 * KT, ple_norm_g[i].rearrange("(j p) -> j p", p=P))
                rows(2 * i + 1, 0, conv_w[i, 2].rearrange("(j p) -> j p", p=P))
                rows(2 * i + 1, CH, conv_b[i].rearrange("(j p) -> j p", p=P))
            rows(0, B_POOL, b_pool[0].rearrange("g (j p) -> (g j) p", p=P))
            rows(0, B_POOL + KT, pool_scale[0].rearrange("(j p) -> j p", p=P))
            rows(1, 2 * CH, attn_sub_g)
            rows(1, 2 * CH + 1, final_norm_g.rearrange("(j p) -> j p", p=P))
            for i, v in enumerate((lam_q1, lam_k1, lam_q2, lam_k2)):
                sp.dma_start(lam_rows[:, i:i + 1], v.rearrange("a d -> d a")).then_inc(lam_in, 16)
            sp.dma_start(p_tok[:, :, :], p.rearrange("i b (t p) d -> p (i b t) d", p=P)).then_inc(p_in, 16)
            with sp.Fori(1, N_HEADS) as hd:
                for which in range(3):
                    sp.wait_ge(lo_done, 3 * hd + which - 2)
                    load_qkv(hd, which)

            def load_unit(n, src, a=0, width=P):
                if n > FIRST_RING4:
                    sp.wait_ge(lo_done, SLOTS * a + n - SLOTS + 1)
                load(slot_of(n), blocks_of(n), src, width).then_inc(raw_in[slot_of(n)], 16)

            def stream(name, src_of):
                first, units, _ = PHASES[name]
                with sp.Fori(0, units // SLOTS) as a:
                    for u in range(SLOTS):
                        load_unit(first + u, src_of(a, u), a)

            def load_emb(n, layer, half):
                proj = w_ple_proj[layer].rearrange("(k p) f -> p k f", p=P)
                load_unit(n, proj[:, :, half * SEQ:(half + 1) * SEQ], width=SEQ)

            wo = w_attn_out[0].rearrange("(k p) f -> p k f", p=P)
            for m in range(KT):
                load_unit(PHASES["wo"][0] + m, wo[:, :, m * P:(m + 1) * P])
            for half in range(2):
                load_emb(PHASES["emb0"][0] + half, 0, half)
            for layer in range(DEPTH):
                if layer:
                    load_emb(PHASES["emb1a"][0], 1, 0)
                    wp = w_pool[0].rearrange("g (k p) e -> p (g k) e", p=P)
                    for half in range(2):
                        load_unit(PHASES["pool"][0] + half, wp[:, half * TT:(half + 1) * TT, :], width=POOL_KT * P)
                    load_emb(PHASES["emb1b"][0], 1, 1)
                up = w_up[layer].rearrange("(k p) f -> p k f", p=P)
                down = w_down[layer].rearrange("(k p) f -> p k f", p=P)
                gate = w_ple_gate[layer].rearrange("(k p) f -> p k f", p=P)
                done = 0
                for part, tiles in enumerate(FFN_PARTS):
                    stream(f"up{layer}{part}",
                           lambda a, u: up[:, :, bass.ds((2 * a + u // 2 + done) * P + (u % 2) * D_FF, P)])
                    stream(f"down{layer}{part}",
                           lambda a, u: down[:, done:done + tiles, bass.ds((SLOTS * a + u) * P, P)])
                    done += tiles
                stream(f"ple{layer}", lambda a, u: gate[:, :, bass.ds((SLOTS * a + u) * P, P)])
            half = TT // 2
            for t in range(half):
                for scaled, tile in ((y_dve, t), (y_act, half + t)):
                    sp.wait_ge(scaled, t + 1)
                    sp.dma_start(out.rearrange("b (t p) d -> p (b t) d", p=P)[:, tile, :], y_tok[:, tile, :]).then_inc(out_done, 16)
            sp.wait_ge(out_done, 16 * TT)

        @block.scalar
        def _(act):
            def split_hi(n, a=0):
                if n >= N_UNITS:
                    return
                s, w = slot_of(n), blocks_of(n) * P
                act.wait_ge(raw_in[s], landed(n, a))
                if n >= FIRST_RING4 + 1:
                    act.wait_ge(unit_done, SLOTS * a + n - SLOTS + 1)
                act.activation(w_hi[s][:, 0:w], w_raw[s][:, 0:w], ACT.Copy).then_inc(hi_done, 1)

            def split_hi_qkv(hd, which):
                act.wait_ge(raw_in[which], 16 * hd + 16)
                if not isinstance(hd, int) or hd > 0:
                    act.wait_ge(unit_done, 3 * hd + which - 2)
                act.activation(w_hi[which][:, 0:KT * P], w_raw[which][:, 0:KT * P], ACT.Copy).then_inc(hi_done, 1)

            def rms_of(norm):
                act.wait_ge(ss_done, norm)
                act.activation(rms_col, bank[7][:, 0:TT], ACT.Sqrt, bias=eps[:, 0:1]).then_inc(rms_done, 1)

            def inverse(norm):
                act.wait_ge(spread_done, spread_of[norm])
                act.activation(inv[:, :], bank[7 if norm else 2][:, :], ACT.Copy, scale=float(D_MODEL)).then_inc(inv_done, 1)

            act.dma_start(gain0_rows[:, :], mix_norm_g[0].rearrange("(j p) -> j p", p=P)).then_inc(gain0_in, 16)

            for t in range(TT):
                act.wait_ge(x_in[t], 16)
                if t:
                    act.wait_ge(tok_ss, t)
                act.activation(square_scratch[:, :], x_tok[:, t, :], ACT.Square,
                               accum_out=tok_sum[:, t:t + 1]).then_inc(tok_ss, 1)
            act.wait_ge(gain0_done, 1)
            for kt in range(KT):
                act.wait_ge(x_T, kt + 1)
                act.activation(x_hi[:, kt, :], bank[kt][:, :], ACT.Copy, scale=gain0[:, kt:kt + 1]).then_inc(xhi_done, 1)
                if kt == 1:
                    split_hi_qkv(0, 0)
            act.wait_ge(tok_ss, TT)
            act.wait_ge(const_done, 3)
            act.activation(rms_col, tok_sum, ACT.Sqrt, bias=eps[:, 0:1], scale=1.0 / D_MODEL).then_inc(rms_done, 1)
            split_hi_qkv(0, 1)
            for kt in range(KT // 2, KT):
                act.wait_ge(x_ready, kt + 1)
                act.activation(h[:, kt, :], bank[kt][:, :], ACT.Copy).then_inc(h_act, 1)
            inverse(NORM_MIX0)

            def start_rest():
                for j in range(DEPTH * PLE_KT):
                    act.wait_ge(p_T, j + 1)
                    act.activation(pT_hi[:, j, :], bank[4 + j][:, :], ACT.Copy).then_inc(pT_hi_done, 1)
                act.wait_ge(lam_sum, 1)
                act.activation(lam_e, bank[2][:, 0:2], ACT.Exp, scale=float(D_MODEL)).then_inc(lam_exp, 1)

            def q_high(hd):
                act.wait_ge(unit_done, 3 * hd + 1)
                for c in range(2):
                    rows = slice(c * HEAD_DIM, (c + 1) * HEAD_DIM)
                    act.activation(q_hi[rows, c, :], bank[0][rows, :], ACT.Copy).then_inc(qhi_done, 1)

            def k_high(hd):
                act.wait_ge(k32_done, hd + 1)
                act.activation(k_hi[:, :], k32[:, :], ACT.Copy).then_inc(khi_done, 1)

            def transposed_high(hp):
                act.wait_ge(v_T, hp + 1)
                act.activation(v_hi[:, :, :].rearrange("p t c -> p (t c)"), bank[5][:, :], ACT.Copy).then_inc(vhi_done, 1)
                for b, (at, w) in enumerate(WT_BANKS):
                    act.wait_ge(w_T, 3 * hp + b + 1)
                    act.activation(wT_hi[:, at:at + w], bank[2 + b][:, 0:w], ACT.Copy).then_inc(wthi_done, 1)

            def output_high(hp):
                act.wait_ge(onorm_done, hp + 1)
                act.activation(oT_hi[:, hp, :], o32[:, :], ACT.Copy).then_inc(ohi_done, 1)

            def output_copy(hp, back):
                act.wait_ge(pv_done, hp + 1)
                if back:
                    act.wait_ge(olo_done, hp)
                act.activation(o32[:, :], bank[6][:, :], ACT.Copy, scale=sub_g_scaled).then_inc(o32_done, 1)
                act.activation(sq[:, 0, :], bank[6][:, :], ACT.Square).then_inc(osq_done, 1)

            def output_rms(hp, src):
                act.wait_ge(oss_done, hp + 1)
                act.activation(orms_col, src[:, 0:TT], ACT.Sqrt, bias=eps[:, 0:1],
                               scale=float(D_MODEL // P)).then_inc(orms_done, 1)

            def exps(hd):
                for qt in range(TT):
                    w = (qt + 1) * P
                    act.wait_ge(neg_done, 2 * hd + qt // 2 + 1)
                    for c in range(2):
                        at = key_off(qt)
                        act.activation(probs[:, c, at:at + w], scores_at(qt, c), ACT.Exp, scale=qscale[:, qt:qt + 1],
                                       bias=negmx[:, 2 * qt + c:2 * qt + c + 1],
                                       accum_out=sums[:, 2 * qt + c:2 * qt + c + 1]).then_inc(exp_done, 1)

            def head(hd, back, split_next):
                split_hi_qkv(hd, 2)
                q_high(hd)
                k_high(hd)
                if back == 0:
                    start_rest()
                else:
                    transposed_high(hd - 1)
                split_next(0)
                split_next(1)
                if back >= 2:
                    output_high(hd - 2)
                if back >= 1:
                    output_copy(hd - 1, back >= 2)
                exps(hd)
                if back >= 1:
                    output_rms(hd - 1, bank[1])

            act.wait_ge(qpad_zero, 2)
            head(0, 0, lambda i: split_hi_qkv(1, i))
            act.wait_ge(subg_done, 1)
            head(1, 1, lambda i: split_hi_qkv(2, i))
            with act.Fori(2, N_HEADS - 1) as hd:
                head(hd, 2, lambda i: split_hi_qkv(hd + 1, i))
            last = N_HEADS - 1
            head(last, 2, lambda i: split_hi(FIRST_RING4 + i))
            transposed_high(last)
            split_hi(FIRST_RING4 + 2)
            output_high(last - 1)
            split_hi(FIRST_RING4 + 3)
            output_copy(last, True)
            output_rms(last, bank[4])
            output_high(last)

            def loop(name, body):
                bodies = PHASES[name][1] // SLOTS
                with act.Fori(0, bodies - 1) as a:
                    body(a)
                body(bodies - 1)

            def look_hi(name, u, a):
                n = PHASES[name][0] + u + LOOK
                if isinstance(a, int):
                    split_hi(n + SLOTS * a)
                else:
                    split_hi(n, a)

            def y_copy(m):
                act.wait_ge(y_T, m + 1)
                act.activation(y_tok[:, :, m * P:(m + 1) * P],
                               bank[5 + m % 2][:, :].rearrange("p (t c) -> p t c", c=P), ACT.Copy).then_inc(y_copied, 1)

            def residual_tile(name, m, norm, g, dst=x_hi):
                n_sq = KT * (norm - 1) + m
                act.wait_ge(evac_done, result_of(name, m))
                if g is not None:
                    act.activation(dst[:, m, :], h[:, m, :], ACT.Copy, scale=g).then_inc(xhi_done, 1)
                if n_sq >= 2:
                    act.wait_ge(acc_done, n_sq - 1)
                act.activation(sq[:, n_sq % 2, :], h[:, m, :], ACT.Square).then_inc(sq_done, 1)

            def residual_phase(name, norm, layer, which, look=LOOK):
                for m in range(KT):
                    if m + look < KT + LOOK:
                        split_hi(PHASES[name][0] + m + look)
                    if norm is not None:
                        residual_tile(name, m, norm, gain(layer, which, m))

            def add_pool_bias(m):
                act.wait_ge(x_ready, KT * NORM_MIX1 + m + 1)
                act.activation(h[:, m, :], h[:, m, :], ACT.Identity, bias=bs[:, m:m + 1]).then_inc(h_biased, 1)

            def wait_tile(n, t, tile_sem, before):
                if t == TT - 1:
                    act.wait_ge(unit_done, n + 1)
                else:
                    act.wait_ge(tile_sem, before + t + 1)

            def emb_copy(layer, half, n, tiles=range(TT)):
                for m in (half * TT + t for t in tiles):
                    wait_tile(n, m % TT, emb_mm, (2 * layer + half) * (TT - 1))
                    act.activation(emb[:, m, :], bank[4 + m % 3][:, :], ACT.Copy).then_inc(emb_done, 1)

            residual_phase("wo", NORM_FFN0, 0, FFN, look=SLOTS)
            emb_copy(0, 0, PHASES["emb0"][0], range(0, 2))
            split_hi(PHASES["emb0"][0] + LOOK)
            emb_copy(0, 0, PHASES["emb0"][0], range(2, 4))
            rms_of(NORM_FFN0)
            split_hi(PHASES["emb0"][0] + 1 + LOOK)
            emb_copy(0, 1, PHASES["emb0"][0] + 1)
            inverse(NORM_FFN0)
            for layer in range(DEPTH):
                if layer:
                    split_hi(PHASES["emb1a"][0] + LOOK)
                    rms_of(NORM_MIX1)
                    act.wait_ge(icol_done, NORM_MIX1 + 1)

                    def z_high(half, t):
                        wait_tile(PHASES["pool"][0] + half, t, z_mm, half * (TT - 1))
                        act.activation(z_hi[half][:, t, :], bank[4 + (half * TT + t) % 3][:, :], ACT.Copy,
                                       scale=icol[:, t:t + 1]).then_inc(zhi_done, 1)

                    def pooled_tile(m):
                        residual_tile("pool", m, NORM_FFN1, gain(1, FFN, m))

                    for t in range(TT):
                        z_high(0, t)
                    split_hi(PHASES["pool"][0] + LOOK)
                    for t in range(3):
                        z_high(1, t)
                    pooled_tile(0)
                    z_high(1, 3)
                    for m in range(1, 5):
                        pooled_tile(m)
                    split_hi(PHASES["pool"][0] + 1 + LOOK)
                    for m in range(5, 7):
                        pooled_tile(m)
                    emb_copy(1, 1, PHASES["emb1b"][0], range(0, 2))
                    pooled_tile(7)
                    emb_copy(1, 1, PHASES["emb1b"][0], range(2, 4))
                    split_hi(PHASES["emb1b"][0] + LOOK)
                    rms_of(NORM_FFN1)
                    inverse(NORM_FFN1)
                done = 0
                for part, tiles in enumerate(FFN_PARTS):
                    name = f"up{layer}{part}"
                    pairs = layer * FT + done

                    def up_body(a):
                        for v in range(2):
                            j = 2 * a + v + done
                            pair = 2 * a + v + pairs
                            for c in range(2):
                                look_hi(name, 2 * v + c, a)
                                act.wait_ge(evac_done, SLOTS * a + result_of(name, 2 * v + c))
                                act.activation(c32[:, c, :], u32[:, c, PAD:PAD + SEQ], ACT.Identity,
                                               scale=tap(layer, 2, j + c * FT),
                                               bias=conv_bias(layer, j + c * FT)).then_inc(tap_done, 1)
                                if c == 0:
                                    act.wait_ge(conv_done, 2 * pair + 1)
                                    act.activation(s32[:, :], c32[:, 0, :], ACT.Silu).then_inc(silu_done, 1)
                            act.wait_ge(gmul_done, pair + 1)
                            act.activation(g_hi[:, 2 * a + v, :], g32[:, :], ACT.Copy).then_inc(ghi_done, 1)

                    loop(name, up_body)
                    norm = (NORM_PLE1 if layer else NORM_PLE0) if part == LAST else None
                    residual_phase(f"down{layer}{part}", norm, layer, PLE)
                    done += tiles
                name = f"ple{layer}"
                norm = NORM_PLE1 if layer else NORM_PLE0
                split_hi(PHASES[name][0] + LOOK)
                rms_of(norm)
                split_hi(PHASES[name][0] + LOOK + 1)
                split_hi(PHASES[name][0] + LOOK + 2)
                inverse(norm)
                for m in range(KT):
                    act.wait_ge(arg_done, KT * layer + m + 1)
                    act.activation(s32[:, :], c32[:, 0, :], ACT.Sigmoid).then_inc(sig_done, 1)
                    if 2 <= m < KT - 1:
                        split_hi(PHASES[name][0] + m + LOOK + 1)
                    if layer == 0:
                        if m == 1:
                            act.wait_ge(band_diff, 2)
                            act.activation(band[:, :, :], band32[:, :, :], ACT.Copy).then_inc(band_done, 1)
                            act.activation(edge_hi[:, :, :], edge32[:, :, :], ACT.Copy).then_inc(band_done, 1)
                        if m == KT - 1:
                            emb_copy(1, 0, PHASES["emb1a"][0], range(0, 2))
                        residual_tile(name, m, NORM_MIX1, gain(1, MIX, m), xp_hi)
                        if m > 0:
                            add_pool_bias(m - 1)
                    else:
                        if m >= 2:
                            y_copy(m - 2)
                        if m == KT - 1:
                            act.activation(table_scratch, eps[:, 0:1], ACT.Sqrt).then_inc(table_loaded, 1)
                        residual_tile(name, m, NORM_FINAL, None)
                        act.activation(y_gained[:, m, :], h[:, m, :], ACT.Copy, scale=final_gain[:, m:m + 1]).then_inc(gained_done, 1)
                if layer == 0:
                    emb_copy(1, 0, PHASES["emb1a"][0], range(2, 4))
                    add_pool_bias(KT - 1)
            y_copy(KT - 2)
            rms_of(NORM_FINAL)
            y_copy(KT - 1)
            act.wait_ge(icol_done, NORM_FINAL + 1)
            act.wait_ge(y_copied, KT)
            for t in range(TT // 2, TT):
                act.activation(y_tok[:, t, :], y_tok[:, t, :], ACT.Copy, scale=icol[:, t:t + 1]).then_inc(y_act, 1)

        @block.gpsimd
        def _(pool):
            pool.memset(ident[:, :], 0.0).then_inc(ident_zero, 1)
            pool.memset(ones[:, :], 1.0 / D_MODEL).then_inc(const_done, 1)
            pool.memset(eps[:, :], EPS).then_inc(const_done, 1)
            pool.wait_ge(ident_zero, 1)
            pool.affine_select(out=ident[:, :], in_=ident[:, :], compare_op=ALU.not_equal, fill=1.0, base=0,
                               pattern=[[-1, P]], channel_multiplier=1).then_inc(const_done, 1)
            pool.memset(mask16[:, :], 0.0).then_inc(ident_zero, 1)
            pool.memset(ident16[:, :], 0.0).then_inc(ident_zero, 1)
            pool.wait_ge(ident_zero, 3)
            pool.affine_select(out=mask16[:, :], in_=mask16[:, :], compare_op=ALU.is_ge, fill=MASKED, base=0,
                               pattern=[[-1, P]], channel_multiplier=1).then_inc(mask_done, 1)
            pool.affine_select(out=ident16[:, :], in_=ident16[:, :], compare_op=ALU.not_equal, fill=1.0, base=0,
                               pattern=[[-1, P]], channel_multiplier=1).then_inc(mask_done, 1)
            for q in (q_hi, q_lo):
                pool.memset(q[:, :, :].bitcast(F32), 0.0).then_inc(qpad_zero, 1)
            pool.wait_ge(evac_done, result_of("wo", KT - 1))
            for g, win in enumerate(POOL_WINDOWS):
                pool.memset(band32[:, g, :], 1.0 / win).then_inc(band_one, 1)
                pool.memset(edge32[:, g, win - 1:], 1.0 / win).then_inc(band_one, 1)
                for t in range(win - 1):
                    pool.memset(edge32[:, g, t:t + 1], 1.0 / (t + 1)).then_inc(band_one, 1)
            pool.wait_ge(band_one, len(POOL_WINDOWS) + sum(POOL_WINDOWS))
            for mat, width in ((band32, BAND), (edge32, EDGE)):
                pool.affine_select(out=mat[:, :, :], in_=mat[:, :, :], compare_op=ALU.is_ge, fill=0.0, base=0,
                                   pattern=[[0, G], [1, width]], channel_multiplier=-1).then_inc(band_below, 1)
            pool.wait_ge(band_below, 2)
            for mat, width in ((band32, BAND), (edge32, EDGE)):
                for g, win in enumerate(POOL_WINDOWS):
                    pool.affine_select(out=mat[:, g, :], in_=mat[:, g, :], compare_op=ALU.is_ge, fill=0.0, base=win - 1,
                                       pattern=[[-1, width]], channel_multiplier=1).then_inc(band_set, 1)

        @block.vector
        def _(dve):
            def split_lo(n, a=0):
                if n >= N_UNITS:
                    return
                s, w = slot_of(n), blocks_of(n) * P
                dve.wait_ge(hi_done, SLOTS * a + n + 1)
                dve.tensor_tensor(w_lo[s][:, 0:w], w_raw[s][:, 0:w], w_hi[s][:, 0:w].bitcast(F32),
                                  ALU.subtract).then_inc(lo_done, 1)

            def split_lo_qkv(hd, which):
                w = KT * P
                dve.wait_ge(hi_done, 3 * hd + which + 1)
                dve.tensor_tensor(w_lo[which][:, 0:w], w_raw[which][:, 0:w], w_hi[which][:, 0:w].bitcast(F32),
                                  ALU.subtract).then_inc(lo_done, 1)

            dve.wait_ge(gain0_T, 1)
            dve.tensor_copy(gain0[:, :], bank[7][:, 0:KT]).then_inc(gain0_done, 1)

            def h_copy(kt):
                dve.wait_ge(xhi_done, kt + 1)
                dve.tensor_copy(h[:, kt, :], bank[kt][:, :]).then_inc(h_dve, 1)

            def x0_low(kt):
                dve.wait_ge(xhi_done, kt + 1)
                dve.scalar_tensor_tensor(out=x_lo[:, kt, :], in0=bank[kt][:, :], scalar=gain0[:, kt:kt + 1],
                                         in1=x_hi[:, kt, :].bitcast(F32), op0=ALU.mult, op1=ALU.subtract).then_inc(x_ready, 1)

            def x_low(norm, m, g, hi=x_hi, lo=x_lo):
                dve.wait_ge(xhi_done, KT * norm + m + 1)
                dve.scalar_tensor_tensor(out=lo[:, m, :], in0=h[:, m, :], scalar=g, in1=hi[:, m, :].bitcast(F32),
                                         op0=ALU.mult, op1=ALU.subtract).then_inc(x_ready, 1)

            def spread(column):
                return dve.tensor_tensor(diag, ident[:, :].rearrange("p (o c) -> p o c", o=1).broadcast_to((P, TT, P)),
                                         column.rearrange("p (t o) -> p t o", o=1).broadcast_to((P, TT, P)), ALU.mult)

            def inverse(norm):
                dve.wait_ge(rms_done, norm + 1)
                dve.reciprocal(icol, rms_col).then_inc(icol_done, 1)
                dve.wait_ge(icol_done, norm + 1)
                if norm in spread_of:
                    spread(icol).then_inc(diag_done, 1)

            x0_low(0)
            h_copy(0)
            x0_low(1)
            split_lo_qkv(0, 0)
            for kt in range(2, KT):
                x0_low(kt)
            inverse(NORM_MIX0)
            for scaled, s in ((qscale, ATTN_SCALE), (neg_qscale, -ATTN_SCALE)):
                dve.tensor_scalar(scaled, icol, s, None, ALU.mult).then_inc(qscale_done, 1)
            h_copy(1)
            split_lo_qkv(0, 1)
            h_copy(2)
            h_copy(3)

            def lambda_products():
                dve.wait_ge(lam_in, 64)
                for i in range(2):
                    dve.tensor_tensor(lam_rows[:, 4 + i:5 + i], lam_rows[:, 2 * i:2 * i + 1],
                                      lam_rows[:, 2 * i + 1:2 * i + 2], ALU.mult).then_inc(lam_prod, 1)

            def start_rest():
                dve.wait_ge(par_T, 1)
                for t in range(4):
                    dve.tensor_copy(params[:, t, 0:par_count[t]], bank[3][:, t * P:t * P + par_count[t]]).then_inc(par_done, 1)
                dve.wait_ge(par_done, 4)
                dve.tensor_tensor(bs[:, :], pool_b, pool_s, ALU.mult).then_inc(bs_done, 1)
                dve.tensor_scalar(sub_g_scaled, sub_g, 1.0 - LAMBDA_INIT, None, ALU.mult).then_inc(subg_done, 1)
                for j in range(DEPTH * PLE_KT):
                    dve.wait_ge(pT_hi_done, j + 1)
                    dve.tensor_tensor(pT_lo[:, j, :], bank[4 + j][:, :], pT_hi[:, j, :].bitcast(F32),
                                      ALU.subtract).then_inc(pT_done, 1)
                dve.wait_ge(lam_exp, 1)
                dve.tensor_tensor(lam, lam_e[:, 0:1], lam_e[:, 1:2], ALU.subtract).then_inc(lam_diff, 1)
                dve.wait_ge(lam_diff, 1)
                dve.tensor_scalar(lam, lam, LAMBDA_INIT, None, ALU.add).then_inc(lam_done, 1)

            def q_low(hd):
                for c in range(2):
                    rows = slice(c * HEAD_DIM, (c + 1) * HEAD_DIM)
                    dve.wait_ge(qhi_done, 2 * hd + c + 1)
                    dve.tensor_tensor(q_lo[rows, c, :], bank[0][rows, :], q_hi[rows, c, :].bitcast(F32),
                                      ALU.subtract).then_inc(qlo_done, 1)

            def k_rows(hd):
                dve.wait_ge(unit_done, 3 * hd + 2)
                dve.tensor_tensor(k32[:, :], bank[1][:, :], inv[:, :], ALU.mult).then_inc(k32_done, 1)

            def k_low(hd):
                dve.wait_ge(khi_done, hd + 1)
                dve.tensor_tensor(k_lo[:, :], k32[:, :], k_hi[:, :].bitcast(F32), ALU.subtract).then_inc(klo_done, 1)

            def softmax_first(hd):
                for qt in range(TT):
                    dve.wait_ge(scores_done, 3 * hd + max(qt, 1))
                    for c in range(2):
                        i = 2 * qt + c
                        dve.tensor_reduce(mx[:, i:i + 1], scores_at(qt, c), AX_X, ALU.max).then_inc(max_done, 1)
                    if qt % 2:
                        neg(hd, qt // 2)

            def neg(hd, half):
                dve.wait_ge(max_done, 2 * TT * hd + 4 * half + 4)
                both = neg_qscale[:, 2 * half:2 * half + 2].rearrange("p (t o) -> p t o", o=1).broadcast_to((P, 2, 2))
                dve.tensor_tensor(negmx[:, 4 * half:4 * half + 4].rearrange("p (t c) -> p t c", c=2),
                                  mx[:, 4 * half:4 * half + 4].rearrange("p (t c) -> p t c", c=2), both,
                                  ALU.mult).then_inc(neg_done, 1)

            def v_rows(hd):
                dve.wait_ge(unit_done, 3 * hd + 3)
                dve.tensor_tensor(vT[:, :], bank[0][:, :], inv[:, :], ALU.mult).then_inc(vT_done, 1)

            def softmax_second(hd):
                def second(qt):
                    at, w = key_off(qt), (qt + 1) * P
                    dve.tensor_scalar(probs[:, 1, at:at + w], probs[:, 1, at:at + w], rsums[:, 2 * qt + 1:2 * qt + 2], lam,
                                      ALU.mult, ALU.mult).then_inc(second_done, 1)

                def difference(qt):
                    at, w = key_off(qt), (qt + 1) * P
                    dve.wait_ge(second_done, TT * hd + qt + 1)
                    dve.scalar_tensor_tensor(out=probs[:, 0, at:at + w], in0=probs[:, 0, at:at + w],
                                             scalar=rsums[:, 2 * qt:2 * qt + 1], in1=probs[:, 1, at:at + w],
                                             op0=ALU.mult, op1=ALU.subtract).then_inc(w_done, 1)

                dve.wait_ge(exp_done, 2 * TT * (hd + 1))
                dve.reciprocal(rsums, sums).then_inc(rsum_done, 1)
                dve.wait_ge(rsum_done, hd + 1)
                second(0)
                for qt in range(1, TT):
                    second(qt)
                    difference(qt - 1)
                difference(TT - 1)

            def transposed_low(hp):
                dve.wait_ge(vhi_done, hp + 1)
                dve.tensor_tensor(v_lo[:, :, :].rearrange("p t c -> p (t c)"), bank[5][:, :],
                                  v_hi[:, :, :].rearrange("p t c -> p (t c)").bitcast(F32), ALU.subtract).then_inc(vlo_done, 1)
                for b, (at, w) in enumerate(WT_BANKS):
                    dve.wait_ge(wthi_done, 3 * hp + b + 1)
                    dve.tensor_tensor(wT_lo[:, at:at + w], bank[2 + b][:, 0:w], wT_hi[:, at:at + w].bitcast(F32),
                                      ALU.subtract).then_inc(wtlo_done, 1)

            def output_inverse(hp):
                dve.wait_ge(orms_done, hp + 1)
                dve.reciprocal(oicol, orms_col).then_inc(oicol_done, 1)
                dve.wait_ge(oicol_done, hp + 1)
                spread(oicol).then_inc(odiag_done, 1)

            def output_norm(hp):
                dve.wait_ge(ospread_done, hp + 1)
                dve.scalar_tensor_tensor(out=o32[:, :], in0=bank[7][:, :], scalar=float(D_MODEL), in1=o32[:, :],
                                         op0=ALU.mult, op1=ALU.mult).then_inc(onorm_done, 1)

            def output_low(hp):
                dve.wait_ge(ohi_done, hp + 1)
                dve.tensor_tensor(oT_lo[:, hp, :], o32[:, :], oT_hi[:, hp, :].bitcast(F32), ALU.subtract).then_inc(olo_done, 1)

            def head(hd, back, split_next):
                q_low(hd)
                split_lo_qkv(hd, 2)
                if back == 0:
                    lambda_products()
                    dve.wait_ge(inv_done, 1)
                k_rows(hd)
                k_low(hd)
                if back == 0:
                    start_rest()
                else:
                    transposed_low(hd - 1)
                split_next(0)
                if back >= 2:
                    output_norm(hd - 2)
                split_next(1)
                if back >= 2:
                    output_low(hd - 2)
                v_rows(hd)
                softmax_first(hd)
                softmax_second(hd)
                if back >= 1:
                    output_inverse(hd - 1)

            dve.wait_ge(qpad_zero, 2)
            dve.wait_ge(qscale_done, 2)
            head(0, 0, lambda i: split_lo_qkv(1, i))
            head(1, 1, lambda i: split_lo_qkv(2, i))
            with dve.Fori(2, N_HEADS - 1) as hd:
                head(hd, 2, lambda i: split_lo_qkv(hd + 1, i))
            last = N_HEADS - 1
            head(last, 2, lambda i: split_lo(FIRST_RING4 + i))
            transposed_low(last)
            output_norm(last - 1)
            split_lo(FIRST_RING4 + 2)
            output_low(last - 1)
            split_lo(FIRST_RING4 + 3)
            output_inverse(last)
            output_norm(last)
            output_low(last)

            def residual_add(m, src):
                dve.tensor_tensor(h[:, m, :], src, h[:, m, :], ALU.add).then_inc(evac_done, 1)

            def sum_squares(norm, m):
                n_sq = KT * (norm - 1) + m
                dve.wait_ge(sq_done, n_sq + 1)
                if m:
                    dve.wait_ge(acc_done, n_sq)
                    dve.tensor_tensor(acc[:, :], acc[:, :], sq[:, n_sq % 2, :], ALU.add).then_inc(acc_done, 1)
                else:
                    dve.tensor_copy(acc[:, :], sq[:, n_sq % 2, :]).then_inc(acc_done, 1)

            def residual_phase(name, norm, layer, which, look=LOOK):
                for m in range(KT):
                    n = PHASES[name][0] + m
                    if m + look < KT + LOOK:
                        split_lo(n + look)
                    dve.wait_ge(unit_done, n + 1)
                    residual_add(m, bank[m % SLOTS][:, :])
                    if norm is not None and m > 0:
                        x_low(norm, m - 1, gain(layer, which, m - 1))
                        sum_squares(norm, m - 1)
                if norm is not None:
                    x_low(norm, KT - 1, gain(layer, which, KT - 1))
                    sum_squares(norm, KT - 1)

            def loop(name, body):
                bodies = PHASES[name][1] // SLOTS
                with dve.Fori(0, bodies - 1) as a:
                    body(a)
                body(bodies - 1)

            def look_lo(name, u, a):
                n = PHASES[name][0] + u + LOOK
                if isinstance(a, int):
                    split_lo(n + SLOTS * a)
                else:
                    split_lo(n, a)

            residual_phase("wo", NORM_FFN0, 0, FFN, look=SLOTS)
            dve.memset(u32[:, :, 0:PAD], 0.0).then_inc(pad_zero, 1)
            split_lo(PHASES["emb0"][0] + LOOK)
            inverse(NORM_FFN0)
            split_lo(PHASES["emb0"][0] + 1 + LOOK)
            dve.wait_ge(pad_zero, 1)
            dve.wait_ge(inv_done, spread_of[NORM_FFN0])
            for layer in range(DEPTH):
                if layer:
                    split_lo(PHASES["emb1a"][0] + LOOK)
                    inverse(NORM_MIX1)

                    def z_low(half, t):
                        i = half * TT + t
                        dve.wait_ge(zhi_done, i + 1)
                        dve.scalar_tensor_tensor(out=z_lo[half][:, t, :], in0=bank[4 + i % 3][:, :],
                                                 scalar=icol[:, t:t + 1], in1=z_hi[half][:, t, :].bitcast(F32),
                                                 op0=ALU.mult, op1=ALU.subtract).then_inc(zlo_done, 1)

                    def add_pooled(m):
                        dve.wait_ge(pool_mm, m + 1)
                        dve.wait_ge(h_biased, m + 1)
                        dve.scalar_tensor_tensor(out=h[:, m, :], in0=bank[m % SLOTS][:, :], scalar=pool_s[:, m:m + 1],
                                                 in1=h[:, m, :], op0=ALU.mult, op1=ALU.add).then_inc(evac_done, 1)

                    def next_input(m):
                        x_low(NORM_FFN1, m, gain(1, FFN, m))
                        sum_squares(NORM_FFN1, m)

                    for t in range(TT):
                        z_low(0, t)
                    split_lo(PHASES["pool"][0] + LOOK)
                    for t in range(3):
                        z_low(1, t)
                    add_pooled(0)
                    z_low(1, 3)
                    for m in range(1, KT):
                        add_pooled(m)
                        next_input(m - 1)
                        if m == 5:
                            split_lo(PHASES["pool"][0] + 1 + LOOK)
                    next_input(KT - 1)
                    split_lo(PHASES["emb1b"][0] + LOOK)
                    inverse(NORM_FFN1)
                    dve.wait_ge(inv_done, spread_of[NORM_FFN1])
                done = 0
                for part, tiles in enumerate(FFN_PARTS):
                    name = f"up{layer}{part}"
                    pairs = layer * FT + done

                    def up_body(a):
                        for v in range(2):
                            j = 2 * a + v + done
                            pair = 2 * a + v + pairs
                            for c in range(2):
                                n = PHASES[name][0] + 2 * v + c
                                dve.wait_ge(unit_done, SLOTS * a + n + 1)
                                dve.tensor_tensor(u32[:, c, PAD:], bank[2 * v + c][:, :], inv[:, :],
                                                  ALU.mult).then_inc(evac_done, 1)
                                look_lo(name, 2 * v + c, a)
                                dve.wait_ge(tap_done, 2 * pair + c + 1)
                                dve.scalar_tensor_tensor(
                                    out=c32[:, c, :], in0=u32[:, c, PAD - 1:PAD - 1 + SEQ],
                                    scalar=tap(layer, 1, j + c * FT), in1=c32[:, c, :],
                                    op0=ALU.mult, op1=ALU.add).then_inc(conv1_done, 1)
                                dve.wait_ge(conv1_done, 2 * pair + c + 1)
                                dve.scalar_tensor_tensor(
                                    out=c32[:, c, :], in0=u32[:, c, PAD - 2:PAD - 2 + SEQ],
                                    scalar=tap(layer, 0, j + c * FT), in1=c32[:, c, :],
                                    op0=ALU.mult, op1=ALU.add).then_inc(conv_done, 1)
                            dve.wait_ge(silu_done, pair + 1)
                            dve.wait_ge(conv_done, 2 * pair + 2)
                            dve.tensor_tensor(g32[:, :], s32[:, :], c32[:, 1, :], ALU.mult).then_inc(gmul_done, 1)
                            dve.wait_ge(ghi_done, pair + 1)
                            dve.tensor_tensor(g_lo[:, 2 * a + v, :], g32[:, :], g_hi[:, 2 * a + v, :].bitcast(F32),
                                              ALU.subtract).then_inc(glo_done, 1)

                    loop(name, up_body)
                    norm = (NORM_PLE1 if layer else NORM_PLE0) if part == LAST else None
                    residual_phase(f"down{layer}{part}", norm, layer, PLE)
                    done += tiles
                name = f"ple{layer}"
                norm = NORM_PLE1 if layer else NORM_PLE0
                split_lo(PHASES[name][0] + LOOK)
                inverse(norm)
                if layer == 0:
                    dve.wait_ge(band_set, 2 * G)
                    for mat, width in ((band32, P), (edge32, EDGE)):
                        dve.tensor_tensor(mat[:, :, 0:width], mat[:, :, 0:width],
                                          ident[:, 0:width].rearrange("p (o c) -> p o c", o=1).broadcast_to((P, G, width)),
                                          ALU.subtract).then_inc(band_diff, 1)
                split_lo(PHASES[name][0] + LOOK + 1)
                split_lo(PHASES[name][0] + LOOK + 2)
                dve.wait_ge(inv_done, spread_of[norm])
                squared = NORM_FINAL if layer else NORM_MIX1

                def next_input(m):
                    if layer == 0:
                        x_low(NORM_MIX1, m, gain(1, MIX, m), xp_hi, xp_lo)
                    sum_squares(squared, m)

                for m in range(KT):
                    n = PHASES[name][0] + m
                    dve.wait_ge(unit_done, n + 1)
                    dve.tensor_tensor(c32[:, 0, :], bank[m % SLOTS][:, :], inv[:, :], ALU.mult).then_inc(arg_done, 1)
                    if m > 0:
                        next_input(m - 1)
                    if layer == 0 and m == 2:
                        dve.wait_ge(band_done, 2)
                        dve.tensor_tensor(edge_lo[:, :, :], edge32[:, :, :], edge_hi[:, :, :].bitcast(F32),
                                          ALU.subtract).then_inc(edge_done, 1)
                    dve.wait_ge(sig_done, KT * layer + m + 1)
                    dve.wait_ge(emb_done, KT * layer + m + 1)
                    dve.tensor_tensor(c32[:, 1, :], emb[:, m, :], s32[:, :], ALU.mult).then_inc(ple_done, 1)
                    dve.wait_ge(ple_done, KT * layer + m + 1)
                    residual_add(m, c32[:, 1, :])
                    if 2 <= m < KT - 1:
                        split_lo(n + LOOK + 1)
                next_input(KT - 1)
            inverse(NORM_FINAL)
            dve.wait_ge(y_copied, KT)
            for t in range(TT // 2):
                dve.tensor_scalar(y_tok[:, t, :], y_tok[:, t, :], icol[:, t:t + 1], None, ALU.mult).then_inc(y_dve, 1)

        @block.tensor
        def _(pe):
            def exact(dst, parts, start=True, stop=True):
                for i, ((w1, w0), (m1, m0), before) in enumerate(parts):
                    before()
                    pe.matmul(dst, w1, m1, start=start and i == 0, stop=False)
                    pe.matmul(dst, w1, m0, start=False, stop=False)
                    last = pe.matmul(dst, w0, m1, start=False, stop=stop and i == len(parts) - 1)
                return last

            def no_wait():
                pass

            def block_of(slot, k):
                return w_hi[slot][:, k * P:(k + 1) * P], w_lo[slot][:, k * P:(k + 1) * P]

            def x_parts(slot, ready=None):
                def wait(k):
                    return (lambda: pe.wait_ge(x_ready, ready + k)) if ready else no_wait
                return [(block_of(slot, k), (x_hi[:, k, :], x_lo[:, k, :]), wait(k)) for k in range(KT)]

            def y_transposes(m):
                pe.wait_ge(gained_done, m + 1)
                if m >= 2:
                    pe.wait_ge(y_copied, m - 1)
                else:
                    pe.wait_ge(emb_done, DEPTH * KT)
                for t in range(TT):
                    last = pe.transpose(bank[5 + m % 2][:, t * P:(t + 1) * P], y_gained[:, m, t * P:(t + 1) * P], ident[:, :])
                last.then_inc(y_T, 1)

            pe.wait_ge(const_done, 3)
            pe.wait_ge(gain0_in, 16)
            pe.transpose(bank[7][:, 0:KT], gain0_rows[:, :], ident[0:KT, 0:KT]).then_inc(gain0_T, 1)
            for t in range(TT):
                pe.wait_ge(x_in[t], 16)
                for kt in range(KT):
                    if t == 0 and kt == KT - 1:
                        pe.wait_ge(gain0_done, 1)
                    last = pe.transpose(bank[kt][:, t * P:(t + 1) * P], x_tok[:, t, kt * P:(kt + 1) * P], ident[:, :])
                    if t == TT - 1:
                        last.then_inc(x_T, 1)

            def project(hd, which, before):
                pe.wait_ge(lo_done, 3 * hd + which + 1)
                before()
                ready = 1 if isinstance(hd, int) and hd == 0 and which == 0 else None
                exact(bank[which % 2][:, :], x_parts(which, ready)).then_inc(unit_done, 1)

            def scores(hd, back):
                pe.wait_ge(qlo_done, 2 * hd + 2)
                pe.wait_ge(klo_done, hd + 1)
                for qt in range(TT):
                    if back >= 1:
                        if qt == 0:
                            pe.wait_ge(wtlo_done, 3 * hd - 1)
                        if qt == 2:
                            pe.wait_ge(wtlo_done, 3 * hd)
                            pe.wait_ge(vlo_done, hd)
                        if qt == 3:
                            pe.wait_ge(osq_done, hd)
                    if back >= 2 and qt == 3:
                        pe.wait_ge(onorm_done, hd - 1)
                    w = (qt + 1) * P
                    keys = slice(qt * P, (qt + 1) * P)
                    for c in range(2):
                        dst = scores_at(qt, c)
                        for i, (q, k) in enumerate(((q_hi, k_hi), (q_hi, k_lo), (q_lo, k_hi))):
                            pe.matmul(dst, q[:, c, keys], k[:, 0:w], start=i == 0, stop=False)
                        last = pe.matmul(dst[:, w - P:w], ident16[:, :], mask16[:, :], start=False, stop=True)
                    if qt:
                        last.then_inc(scores_done, 1)

            def head_transposes(hp):
                pe.wait_ge(vT_done, hp + 1)
                pe.wait_ge(exp_done, 2 * TT * (hp + 1))
                for t in range(TT):
                    last = pe.transpose(bank[5][:, t * P:(t + 1) * P], vT[:, t * P:(t + 1) * P], ident[:, :])
                last.then_inc(v_T, 1)
                pe.wait_ge(w_done, TT * (hp + 1))
                for kt in range(TT):
                    for qt in range(kt, TT):
                        b = min(kt, 2)
                        at = wt_off(kt) + (qt - kt) * P - WT_BANKS[b][0]
                        src = key_off(qt) + kt * P
                        last = pe.transpose(bank[2 + b][:, at:at + P], probs[:, 0, src:src + P], ident[:, :])
                    if kt != 2:
                        last.then_inc(w_T, 1)

            def head_product(hp):
                pe.wait_ge(vlo_done, hp + 1)
                for kt in range(TT):
                    pe.wait_ge(wtlo_done, 3 * hp + min(kt, 2) + 1)
                    at, w = wt_off(kt), (TT - kt) * P
                    last = exact(bank[6][:, kt * P:SEQ],
                                 [((v_hi[:, kt, :], v_lo[:, kt, :]), (wT_hi[:, at:at + w], wT_lo[:, at:at + w]), no_wait)],
                                 start=kt == 0, stop=kt == TT - 1)
                last.then_inc(pv_done, 1)

            def token_sums(dst, squares):
                for t in range(TT):
                    last = pe.matmul(dst[:, t:t + 1], squares[:, t * P:(t + 1) * P], ones[:, 0:1], start=True, stop=True)
                return last

            def spread(dst):
                for t in range(TT):
                    last = pe.matmul(dst[:, t * P:(t + 1) * P], ones[:, :], diag[:, t, :], start=True, stop=True)
                return last

            def output_sums(hp, dst):
                pe.wait_ge(osq_done, hp + 1)
                token_sums(dst, sq[:, 0, :]).then_inc(oss_done, 1)

            def output_spread(hp):
                pe.wait_ge(odiag_done, hp + 1)
                spread(bank[7]).then_inc(ospread_done, 1)

            def start_rest():
                pe.wait_ge(par_in, 16 * (6 * DEPTH + 4))
                pe.wait_ge(h_dve, KT // 2)
                for t in range(4):
                    last = pe.transpose(bank[3][:, t * P:t * P + par_count[t]], par_rows[0:par_count[t], t, :],
                                        ident[0:par_count[t], 0:par_count[t]])
                last.then_inc(par_T, 1)
                pe.wait_ge(p_in, 16)
                pe.wait_ge(h_act, KT // 2)
                for j in range(DEPTH * PLE_KT):
                    i, k = divmod(j, PLE_KT)
                    for t in range(TT):
                        last = pe.transpose(bank[4 + j][:, t * P:(t + 1) * P],
                                            p_tok[:, i * TT + t, k * P:(k + 1) * P], ident[:, :])
                    last.then_inc(p_T, 1)
                pe.wait_ge(lam_prod, 2)
                pe.wait_ge(inv_done, 1)
                pe.matmul(bank[2][:, 0:2], ones[0:HEAD_DIM, :], lam_rows[:, 4:6], start=True, stop=True).then_inc(lam_sum, 1)

            def head(hd, back):
                if back == 0:
                    project(hd, 0, lambda: pe.wait_ge(h_dve, 1))
                    pe.wait_ge(diag_done, 1)
                    pe.wait_ge(h_dve, 3)
                    spread(bank[2]).then_inc(spread_done, 1)
                    project(hd, 1, no_wait)
                    start_rest()
                else:
                    project(hd, 0, lambda: pe.wait_ge(vT_done, hd))
                    project(hd, 1, (lambda: pe.wait_ge(orms_done, hd - 1)) if back >= 2 else no_wait)
                    head_transposes(hd - 1)
                if back >= 2:
                    output_spread(hd - 2)
                project(hd, 2, lambda: pe.wait_ge(qlo_done, 2 * hd + 2))
                if back >= 1:
                    head_product(hd - 1)
                else:
                    pe.wait_ge(mask_done, 2)
                    pe.wait_ge(par_done, 4)
                    pe.wait_ge(pT_done, DEPTH * PLE_KT)
                    pe.wait_ge(lam_exp, 1)
                scores(hd, back)
                if back >= 1:
                    output_sums(hd - 1, bank[1])

            head(0, 0)
            head(1, 1)
            with pe.Fori(2, N_HEADS) as hd:
                head(hd, 2)

            def wo_part(m, heads, start=False, stop=False):
                n = PHASES["wo"][0] + m
                if start:
                    pe.wait_ge(lo_done, n + 1)
                    if m >= SLOTS:
                        pe.wait_ge(evac_done, result_of("wo", m - SLOTS))
                done = exact(bank[m % SLOTS][:, :],
                             [(block_of(slot_of(n), k), (oT_hi[:, k, :], oT_lo[:, k, :]), no_wait) for k in heads],
                             start=start, stop=stop)
                if stop:
                    done.then_inc(unit_done, 1)

            last_head = N_HEADS - 1
            pe.wait_ge(olo_done, last_head - 1)
            pe.wait_ge(vT_done, N_HEADS)
            wo_part(0, range(0, last_head - 1), start=True)
            pe.wait_ge(orms_done, last_head)
            wo_part(1, range(0, last_head - 1), start=True)
            head_transposes(last_head)
            output_spread(last_head - 1)
            head_product(last_head)
            pe.wait_ge(olo_done, last_head)
            for m in range(2):
                wo_part(m, [last_head - 1])
            pe.wait_ge(wtlo_done, 3 * N_HEADS)
            output_sums(last_head, bank[4])
            wo_part(2, range(0, last_head), start=True)
            pe.wait_ge(onorm_done, last_head)
            output_spread(last_head)
            wo_part(3, range(0, last_head), start=True)
            pe.wait_ge(olo_done, N_HEADS)
            for m in range(SLOTS):
                wo_part(m, [last_head], stop=True)
            for m in range(SLOTS, KT):
                wo_part(m, range(N_HEADS), start=True, stop=True)

            def unit(name, u, a, parts, stop=True):
                pe.wait_ge(lo_done, SLOTS * a + PHASES[name][0] + u + 1)
                pe.wait_ge(evac_done, SLOTS * a + result_of(name, u) - SLOTS)
                last = exact(bank[u % SLOTS][:, :], parts, stop=stop)
                if stop:
                    last.then_inc(unit_done, 1)

            def norm_sums(norm):
                pe.wait_ge(acc_done, KT * norm)
                token_sums(bank[7], acc).then_inc(ss_done, 1)

            def norm_spread(norm):
                pe.wait_ge(diag_done, spread_of[norm])
                spread(bank[7]).then_inc(spread_done, 1)

            def embedding(n, layer, half):
                pe.wait_ge(lo_done, n + 1)
                slot = slot_of(n)
                for m in range(half * TT, (half + 1) * TT):
                    done = KT * layer + m
                    bank_of = bank[4 + m % 3]
                    if m >= 3:
                        pe.wait_ge(emb_done, done - 2)
                    parts = []
                    for k in range(PLE_KT):
                        at = k * TT + m % TT
                        j = layer * PLE_KT + k
                        parts.append((block_of(slot, at), (pT_hi[:, j, :], pT_lo[:, j, :]), no_wait))
                    exact(bank_of[:, :], parts).then_inc(unit_done if m % TT == TT - 1 else emb_mm, 1)

            embedding(PHASES["emb0"][0], 0, 0)
            norm_sums(NORM_FFN0)
            embedding(PHASES["emb0"][0] + 1, 0, 1)
            norm_spread(NORM_FFN0)
            for layer in range(DEPTH):
                if layer:
                    embedding(PHASES["emb1a"][0], 1, 0)
                    width = POOL_KT * P

                    def pool_product(half, t):
                        n = PHASES["pool"][0] + half
                        i = half * TT + t
                        if t == 0:
                            pe.wait_ge(lo_done, n + 1)
                        if i < 3:
                            pe.wait_ge(emb_done, KT + TT)
                        else:
                            pe.wait_ge(zlo_done, i - 2)
                        for g in range(2):
                            tiles = [half * TT + g * POOL_KT + k for k in range(POOL_KT)]
                            ws = [slice((g * POOL_KT + k) * width, (g * POOL_KT + k + 1) * width) for k in range(POOL_KT)]
                            tok = slice(t * P, (t + 1) * P)
                            pe.wait_ge(x_ready, KT * NORM_MIX1 + tiles[-1] + 1)
                            mm = exact(bank[4 + i % 3][:, g * width:(g + 1) * width], [
                                ((xp_hi[:, c, tok], xp_lo[:, c, tok]), (w_hi[slot_of(n)][:, w], w_lo[slot_of(n)][:, w]),
                                 no_wait) for c, w in zip(tiles, ws)])
                        mm.then_inc(unit_done if t == TT - 1 else z_mm, 1)

                    def pool_means(m):
                        half, g = m // TT, m // POOL_KT
                        pe.wait_ge(zlo_done, TT * (half + 1))
                        pe.wait_ge(evac_done, result_of("pool", m) - SLOTS)
                        feat = slice(m % TT * P, (m % TT + 1) * P)
                        for t in range(TT):
                            hi, lo = z_hi[half][:, t, feat], z_lo[half][:, t, feat]
                            begin, end = t * P, min(t * P + BAND, SEQ)
                            if t == 0:
                                dst = bank[m % SLOTS][:, 0:EDGE]
                                pe.matmul(dst, hi, edge_hi[:, g, :], start=True, stop=False, skip_group_check=True)
                                pe.matmul(dst, hi, edge_lo[:, g, :], start=False, stop=False, skip_group_check=True)
                                pe.matmul(dst, lo, edge_hi[:, g, :], start=False, stop=False, skip_group_check=True)
                                begin = EDGE
                            dst = bank[m % SLOTS][:, begin:end]
                            mat = band[:, g, begin - t * P:end - t * P]
                            pe.matmul(dst, hi, mat, start=False, stop=False, skip_group_check=True)
                            mm = pe.matmul(dst, lo, mat, start=False, stop=t == TT - 1, skip_group_check=True)
                        mm.then_inc(pool_mm, 1)

                    pe.wait_ge(edge_done, 1)
                    pool_product(0, 0)
                    norm_sums(NORM_MIX1)
                    for t in range(1, TT):
                        pool_product(0, t)
                    pool_product(1, 0)
                    pool_product(1, 1)
                    pool_means(0)
                    pool_product(1, 2)
                    pool_means(1)
                    pool_product(1, 3)
                    for m in range(2, KT):
                        pool_means(m)
                    embedding(PHASES["emb1b"][0], 1, 1)
                norm = NORM_FFN1 if layer else NORM_FFN0
                for part, tiles in enumerate(FFN_PARTS):
                    name = f"up{layer}{part}"

                    def up_body(a, first):
                        for u in range(SLOTS):
                            parts = x_parts(slot_of(PHASES[name][0] + u), KT * norm + 1 if first and u == 0 else None)
                            if first and u == 0 and layer:
                                weights, moving, ready = parts[KT // 2 + 1]

                                def ready_and_sums():
                                    norm_sums(norm)
                                    ready()

                                parts[KT // 2 + 1] = (weights, moving, ready_and_sums)
                            unit(name, u, a, parts)
                            if first and u == 0 and layer:
                                norm_spread(norm)

                    if part == 0:
                        up_body(0, True)
                    with pe.Fori(1 if part == 0 else 0, PHASES[name][1] // SLOTS) as a:
                        up_body(a, False)
                    name = f"down{layer}{part}"
                    pairs = layer * FT + sum(FFN_PARTS[:part])

                    def down_parts(u, ks, wait):
                        return [(block_of(slot_of(PHASES[name][0] + u), k), (g_hi[:, k, :], g_lo[:, k, :]),
                                 (lambda k=k: pe.wait_ge(glo_done, pairs + k + 1)) if wait else no_wait) for k in ks]

                    for u in range(2):
                        unit(name, u, 0, down_parts(u, range(tiles - 1), u == 0), stop=False)
                    for u in range(2):
                        exact(bank[u][:, :], down_parts(u, [tiles - 1], True), start=False).then_inc(unit_done, 1)
                    for m in range(2, KT):
                        unit(name, m % SLOTS, m // SLOTS, down_parts(m % SLOTS, range(tiles), False))
                norm = NORM_PLE1 if layer else NORM_PLE0
                name = f"ple{layer}"
                for m in range(KT):
                    unit(name, m, 0, x_parts(slot_of(PHASES[name][0] + m), KT * norm + 1 if m == 0 else None))
                    if m == 0:
                        norm_sums(norm)
                    if m == 1:
                        norm_spread(norm)
                    if layer == DEPTH - 1 and m >= 2:
                        y_transposes(m - 2)
            y_transposes(KT - 2)
            norm_sums(NORM_FINAL)
            y_transposes(KT - 1)


_INS = ['x', 'p', 'mix_norm_g', 'w_qkv', 'lam_q1', 'lam_k1', 'lam_q2', 'lam_k2', 'attn_sub_g', 'w_attn_out',
        'w_pool', 'b_pool', 'pool_scale', 'ffn_norm_g', 'w_up', 'conv_w', 'conv_b', 'w_down',
        'ple_norm_g', 'w_ple_gate', 'w_ple_proj', 'final_norm_g']


def kernel(**inputs):
    import concourse.bacc as bacc
    from concourse.bass_utils import run_bass_kernel_spmd

    nc = bacc.Bacc("TRN2", target_bir_lowering=False, num_devices=1)
    arrays, args = {}, []
    for name in _INS:
        a = np.ascontiguousarray(inputs[name])
        arrays[f"in_{name}"] = a
        args.append(nc.dram_tensor(f"in_{name}", a.shape, mybir.dt.from_np(a.dtype), kind="ExternalInput").ap())
    result = nc.dram_tensor("out", (1, SEQ, D_MODEL), F32, kind="ExternalOutput").ap()
    hybrid_trunk(nc, *args, result)
    r = run_bass_kernel_spmd(nc, [arrays], core_ids=[0])
    return r.results[0]["out"]
```

```python
import math
from contextlib import ExitStack

import numpy as np

import concourse.bass as bass
from concourse import mybir

F32 = mybir.dt.float32
F32R = mybir.dt.float32r
BF16 = mybir.dt.bfloat16
ALU = mybir.AluOpType
ACT = mybir.ActivationFunctionType
AX_X = mybir.AxisListType.X

P = 128
D_MODEL = 1024
SEQ = 512
DEPTH = 2
N_HEADS = 8
HEAD_DIM = 64
POOL_WINDOWS = (2, 4, 8, 16)
D_FF = 2816
PLE_DIM = 256
EPS = 1e-6
ATTN_SCALE = HEAD_DIM ** -0.5
LAMBDA_INIT = 0.8 - 0.6 * math.exp(-0.3 * 0)
MASKED = -1e30

KT = D_MODEL // P
TT = SEQ // P
FT = D_FF // P
PLE_KT = PLE_DIM // P
POOL_KT = D_MODEL // len(POOL_WINDOWS) // P
FFN_PARTS = (8, 8, 6)
SLOTS = 4
UNIT_BLOCKS = KT
LOOK = 2
PAD = 2
EDGE = max(POOL_WINDOWS)
BAND = P + EDGE


def plan():
    phases, before, n, results = {}, {}, 0, 0

    def add(name, units, blocks, gives):
        nonlocal n, results
        phases[name], before[name] = (n, units, blocks), results
        n, results = n + units, results + gives

    add("qkv", 3 * N_HEADS, KT, 0)
    add("wo", KT, KT, KT)
    add("emb0", 2, KT, 0)
    for layer in range(DEPTH):
        if layer:
            add("emb1a", 1, KT, 0)
            add("pool", 2, KT, KT)
            add("emb1b", 1, KT, 0)
        for part, tiles in enumerate(FFN_PARTS):
            add(f"up{layer}{part}", 2 * tiles, KT, 2 * tiles)
            add(f"down{layer}{part}", KT, tiles, KT)
        add(f"ple{layer}", KT, KT, KT)
    return phases, before, n


PHASES, RESULTS_BEFORE, N_UNITS = plan()
FIRST_RING4 = 3 * N_HEADS


def blocks_of(n):
    return next(b for first, units, b in PHASES.values() if first <= n < first + units)


def slot_of(n):
    return n % 3 if n < FIRST_RING4 else (n + 3) % SLOTS


def uses_before(n):
    if n < FIRST_RING4:
        return n // 3
    return (n - FIRST_RING4) // SLOTS + (N_HEADS if slot_of(n) != 3 else 0)


def landed(n, a=0):
    return 16 * (uses_before(n) + 1) + 16 * a


def result_of(name, u):
    return RESULTS_BEFORE[name] + u + 1


def hybrid_trunk(nc, x, p, mix_norm_g, w_qkv, lam_q1, lam_k1, lam_q2, lam_k2, attn_sub_g, w_attn_out,
                 w_pool, b_pool, pool_scale, ffn_norm_g, w_up, conv_w, conv_b, w_down,
                 ple_norm_g, w_ple_gate, w_ple_proj, final_norm_g, out):
    with ExitStack() as ctx:
        def sem(name):
            return ctx.enter_context(nc.semaphore(name))

        def sb(name, shape, dt, scope=ctx):
            return scope.enter_context(nc.sbuf_tensor(name, shape, dt))

        w_raw = [sb(f"w_raw{s}", [P, UNIT_BLOCKS * P], F32) for s in range(SLOTS)]
        w_hi = [sb(f"w_hi{s}", [P, UNIT_BLOCKS * P], F32R) for s in range(SLOTS)]
        w_lo = [sb(f"w_lo{s}", [P, UNIT_BLOCKS * P], F32R) for s in range(SLOTS)]
        h = sb("h", [P, KT, SEQ], F32)
        x_hi = sb("x_hi", [P, KT, SEQ], F32R)
        x_lo = sb("x_lo", [P, KT, SEQ], F32R)
        pT_hi = sb("pT_hi", [P, DEPTH * PLE_KT, SEQ], F32R)
        pT_lo = sb("pT_lo", [P, DEPTH * PLE_KT, SEQ], F32R)
        inv = sb("inv", [P, SEQ], F32)
        sq = sb("sq", [P, 2, SEQ], F32)
        col_parts = sb("col_parts", [P, 2 * TT], F32R)
        diag = sb("diag", [P, 2, SEQ], F32R)
        acc = sb("acc", [P, SEQ], F32)
        params = sb("params", [P, 4, P], F32)
        ident = sb("ident", [P, P], F32)
        ones = sb("ones", [P, P], F32)
        ones_r = sb("ones_r", [P, P], F32R)
        eps = sb("eps", [P, 1], F32)
        small = sb("small", [P, 64], F32)
        gain0 = sb("gain0", [P, KT], F32)
        bs = sb("bs", [P, KT], F32)
        ident16 = sb("ident16", [P, P], BF16)
        mask16 = sb("mask16", [P, 2, P], BF16)

        start = ExitStack()
        x_tok = sb("x_tok", [P, TT, D_MODEL], F32, start)
        p_tok = sb("p_tok", [P, DEPTH * TT, PLE_DIM], F32, start)
        par_rows = sb("par_rows", [P, 4, P], F32, start)
        lam_rows = sb("lam_rows", [HEAD_DIM, 8], F32, start)
        gain0_rows = sb("gain0_rows", [KT, P], F32, start)
        square_scratch = sb("square_scratch", [P, D_MODEL], F32, start)
        start.close()

        attn = ExitStack()
        oT_hi = sb("oT_hi", [P, N_HEADS, SEQ], F32R, attn)
        oT_lo = sb("oT_lo", [P, N_HEADS, SEQ], F32R, attn)
        k32 = sb("k32", [P, SEQ], F32, attn)
        q_hi = sb("q_hi", [P, 2, SEQ], F32R, attn)
        q_lo = sb("q_lo", [P, 2, SEQ], F32R, attn)
        k_hilo = sb("k_hilo", [P, 2, SEQ], F32R, attn)
        vT = sb("vT", [P, SEQ], F32, attn)
        v_hi = sb("v_hi", [P, TT, P], F32R, attn)
        v_lo = sb("v_lo", [P, TT, P], F32R, attn)
        CAUSAL = P * TT * (TT + 1) // 2
        probs = sb("probs", [P, 2, CAUSAL], F32, attn)
        wT_hi = sb("wT_hi", [P, CAUSAL], F32R, attn)
        wT_lo = sb("wT_lo", [P, CAUSAL], F32R, attn)
        o32 = acc
        attn.close()

        ffn = ExitStack()
        g_hi = sb("g_hi", [P, KT, SEQ], F32R, ffn)
        g_lo = sb("g_lo", [P, KT, SEQ], F32R, ffn)
        emb = sb("emb", [P, KT, SEQ], F32, ffn)
        xp_hi, xp_lo = g_hi, g_lo
        G = len(POOL_WINDOWS)
        band32 = sb("band32", [P, G, BAND], F32, ffn)
        edge32 = sb("edge32", [P, G, EDGE], F32, ffn)
        band = sb("band", [P, G, BAND], F32R, ffn)
        first_band = sb("first_band", [P, G, BAND], F32R, ffn)
        edge_lo = sb("edge_lo", [P, G, EDGE], F32R, ffn)
        mlp = ExitStack()
        u32 = sb("u32", [P, 2, PAD + SEQ], F32, mlp)
        c32 = sb("c32", [P, 2, SEQ], F32, mlp)
        s32 = sb("s32", [P, SEQ], F32, mlp)
        g32 = sb("g32", [P, SEQ], F32, mlp)
        mlp.close()
        z0_hi = sb("z0_hi", [P, TT, SEQ], F32R, ffn)
        z0_lo = sb("z0_lo", [P, TT, SEQ], F32R, ffn)
        z_hi, z_lo = (z0_hi, g_hi), (z0_lo, g_lo)
        ffn.close()

        tail = ExitStack()
        y_tok = sb("y_tok", [P, TT, D_MODEL], F32, tail)
        y_gained = sb("y_gained", [P, KT, SEQ], F32, tail)
        tail.close()

        bank = [ctx.enter_context(nc.psum_tensor(f"bank{b}", [P, SEQ], F32)) for b in range(8)]

        raw_in = [sem(f"raw_in{s}") for s in range(SLOTS)]
        hi_done, lo_done, unit_done, evac_done = sem("hi_done"), sem("lo_done"), sem("unit_done"), sem("evac_done")
        x_in = [sem(f"x_in{t}") for t in range(TT)]
        par_in, p_in, lam_in = sem("par_in"), sem("p_in"), sem("lam_in")
        gain0_in, gain0_T, gain0_done = sem("gain0_in"), sem("gain0_T"), sem("gain0_done")
        ident_zero, const_done, mask_done = sem("ident_zero"), sem("const_done"), sem("mask_done")
        par_T, par_done, x_T, p_T, pT_hi_done, pT_done = (
            sem("par_T"), sem("par_done"), sem("x_T"), sem("p_T"), sem("pT_hi_done"), sem("pT_done"))
        tok_ss, qpad_zero, qscale_done = sem("tok_ss"), sem("qpad_zero"), sem("qscale_done")
        lam_prod, lam_sum, lam_exp, lam_diff, lam_done, subg_done = (
            sem("lam_prod"), sem("lam_sum"), sem("lam_exp"), sem("lam_diff"), sem("lam_done"), sem("subg_done"))
        h_dve, h_act = sem("h_dve"), sem("h_act")
        xhi_done, x_ready, sq_done, acc_done = sem("xhi_done"), sem("x_ready"), sem("sq_done"), sem("acc_done")
        ones_done, parts_done, oparts_done = sem("ones_done"), sem("parts_done"), sem("oparts_done")
        ss_done, rms_done, icol_done, diag_done, spread_done, inv_done = (
            sem("ss_done"), sem("rms_done"), sem("icol_done"), sem("diag_done"), sem("spread_done"), sem("inv_done"))
        qhi_done, qtwin_done, qlo_done, k32_done, khi_done, klo_done = (
            sem("qhi_done"), sem("qtwin_done"), sem("qlo_done"), sem("k32_done"), sem("khi_done"), sem("klo_done"))
        v_T, vhi_done, vlo_done = sem("v_T"), sem("vhi_done"), sem("vlo_done")
        scores_done, max_done, neg_done, exp_done = sem("scores_done"), sem("max_done"), sem("neg_done"), sem("exp_done")
        rsum_done, second_done, w_done = sem("rsum_done"), sem("second_done"), sem("w_done")
        w_T, wthi_done, wtlo_done = sem("w_T"), sem("wthi_done"), sem("wtlo_done")
        pv_done, o32_done, osq_done, oss_done, orms_done, oicol_done, odiag_done, ospread_done = (
            sem("pv_done"), sem("o32_done"), sem("osq_done"), sem("oss_done"), sem("orms_done"), sem("oicol_done"),
            sem("odiag_done"), sem("ospread_done"))
        onorm_done, ohi_done, olo_done = sem("onorm_done"), sem("ohi_done"), sem("olo_done")
        pad_zero, vT_done, tap_done, conv1_done, conv_done, silu_done, gmul_done, ghi_done, glo_done = (
            sem("pad_zero"), sem("vT_done"), sem("tap_done"), sem("conv1_done"), sem("conv_done"), sem("silu_done"),
            sem("gmul_done"), sem("ghi_done"), sem("glo_done"))
        emb_mm, emb_done, arg_done, sig_done, ple_done = (
            sem("emb_mm"), sem("emb_done"), sem("arg_done"), sem("sig_done"), sem("ple_done"))
        bs_done, h_biased = sem("bs_done"), sem("h_biased")
        band_one, band_below, band_set, band_diff, band_done, edge_done = (
            sem("band_one"), sem("band_below"), sem("band_set"), sem("band_diff"), sem("band_done"), sem("edge_done"))
        z_mm, zhi_done, zlo_done, pool_mm = sem("z_mm"), sem("zhi_done"), sem("zlo_done"), sem("pool_mm")
        gained_done, y_T, y_copied, y_dve, y_act, out_done = (
            sem("gained_done"), sem("y_T"), sem("y_copied"), sem("y_dve"), sem("y_act"), sem("out_done"))
        table_loaded = sem("table_loaded")

        CH = 2 * FT

        def tap(layer, w, j):
            return params[:, 2 * layer + w // 2, bass.ds((w % 2) * CH + j, 1)]

        def conv_bias(layer, j):
            return params[:, 2 * layer + 1, bass.ds(CH + j, 1)]

        MIX, FFN, PLE = 0, 1, 2

        def gain(layer, which, kt):
            return params[:, 2 * layer, bass.ds(2 * CH + which * KT + kt, 1)]

        B_POOL = 2 * CH + 3 * KT
        pool_b = params[:, 0, B_POOL:B_POOL + KT]
        pool_s = params[:, 0, B_POOL + KT:B_POOL + 2 * KT]
        sub_g = params[:, 1, 2 * CH:2 * CH + 1]
        final_gain = params[:, 1, 2 * CH + 1:2 * CH + 1 + KT]
        par_count = [2 * CH + 5 * KT, 2 * CH + 1 + KT, 2 * CH + 3 * KT, 2 * CH]

        tok_sum = small[:, 0:TT]
        lam = small[:, 8:9]
        lam_e = small[:, 9:11]
        sub_g_scaled = small[:, 11:12]
        mx = small[:, 16:24]
        negmx = small[:, 24:32]
        sums = small[:, 32:40]
        rsums = small[:, 40:48]
        rms_col = small[:, 48:52]
        icol = small[:, 52:56]
        qscale = small[:, 56:60]
        neg_qscale = small[:, 12:16]
        orms_col = small[:, 4:8]
        oicol = small[:, 60:64]
        table_scratch = small[:, 8:9]

        NORM_MIX0, NORM_FFN0, NORM_PLE0, NORM_MIX1, NORM_FFN1, NORM_PLE1, NORM_FINAL = range(7)
        spread_of = {NORM_MIX0: 1, NORM_FFN0: 2, NORM_PLE0: 3, NORM_FFN1: 4, NORM_PLE1: 5}
        LAST = len(FFN_PARTS) - 1

        def key_off(qt):
            return P * qt * (qt + 1) // 2

        def wt_off(kt):
            return P * (kt * TT - kt * (kt - 1) // 2)

        def scores_at(qt, c):
            w = (qt + 1) * P
            if qt < 2:
                return bank[2 + qt][:, c * w:(c + 1) * w]
            return bank[2 * qt + c][:, 0:w]

        def z_bank(i):
            return bank[4 + (i + 1) % 3]

        WT_BANKS = [(0, 512), (512, 384), (896, 384)]

        own = [slice(0, HEAD_DIM), slice(HEAD_DIM, P)]
        other = own[::-1]

        block = ctx.enter_context(nc.Block())

        @block.sync
        def _(sp):
            x_view = x.rearrange("b (t p) d -> p (b t) d", p=P)

            def load(slot, blocks, src, width=P):
                dst = w_raw[slot][:, 0:blocks * P].rearrange("p (k c) -> p k c", c=width)
                return sp.dma_start(dst, src)

            wq = w_qkv[0].rearrange("(k p) f -> p k f", p=P)

            def load_qkv(hd, which):
                load(which, KT, wq[:, :, bass.ds(hd * P + which * D_MODEL, P)]).then_inc(raw_in[which], 16)

            for t in range(TT):
                if t == TT - 1:
                    load_qkv(0, 0)
                sp.dma_start(x_tok[:, t, :], x_view[:, t, :]).then_inc(x_in[t], 16)
            load_qkv(0, 1)
            load_qkv(0, 2)

            def rows(t, at, src):
                sp.dma_start(par_rows[at:at + src.shape[0], t, :], src).then_inc(par_in, 16)

            for i in range(DEPTH):
                rows(2 * i, 0, conv_w[i, 0:2].rearrange("w (j p) -> (w j) p", p=P))
                rows(2 * i, 2 * CH, mix_norm_g[i].rearrange("(j p) -> j p", p=P))
                rows(2 * i, 2 * CH + KT, ffn_norm_g[i].rearrange("(j p) -> j p", p=P))
                rows(2 * i, 2 * CH + 2 * KT, ple_norm_g[i].rearrange("(j p) -> j p", p=P))
                rows(2 * i + 1, 0, conv_w[i, 2].rearrange("(j p) -> j p", p=P))
                rows(2 * i + 1, CH, conv_b[i].rearrange("(j p) -> j p", p=P))
            rows(0, B_POOL, b_pool[0].rearrange("g (j p) -> (g j) p", p=P))
            rows(0, B_POOL + KT, pool_scale[0].rearrange("(j p) -> j p", p=P))
            rows(1, 2 * CH, attn_sub_g)
            rows(1, 2 * CH + 1, final_norm_g.rearrange("(j p) -> j p", p=P))
            for i, v in enumerate((lam_q1, lam_k1, lam_q2, lam_k2)):
                sp.dma_start(lam_rows[:, i:i + 1], v.rearrange("a d -> d a")).then_inc(lam_in, 16)
            sp.dma_start(p_tok[:, :, :], p.rearrange("i b (t p) d -> p (i b t) d", p=P)).then_inc(p_in, 16)
            with sp.Fori(1, N_HEADS) as hd:
                for which in range(3):
                    sp.wait_ge(lo_done, 3 * hd + which - 2)
                    load_qkv(hd, which)

            def load_unit(n, src, a=0, width=P):
                if n > FIRST_RING4:
                    sp.wait_ge(lo_done, SLOTS * a + n - SLOTS + 1)
                load(slot_of(n), blocks_of(n), src, width).then_inc(raw_in[slot_of(n)], 16)

            def stream(name, src_of):
                first, units, _ = PHASES[name]
                with sp.Fori(0, units // SLOTS) as a:
                    for u in range(SLOTS):
                        load_unit(first + u, src_of(a, u), a)

            def load_emb(n, layer, half):
                proj = w_ple_proj[layer].rearrange("(k p) f -> p k f", p=P)
                load_unit(n, proj[:, :, half * SEQ:(half + 1) * SEQ], width=SEQ)

            wo = w_attn_out[0].rearrange("(k p) f -> p k f", p=P)
            for m in range(KT):
                load_unit(PHASES["wo"][0] + m, wo[:, :, m * P:(m + 1) * P])
            for half in range(2):
                load_emb(PHASES["emb0"][0] + half, 0, half)
            for layer in range(DEPTH):
                if layer:
                    load_emb(PHASES["emb1a"][0], 1, 0)
                    wp = w_pool[0].rearrange("g (k p) e -> p (g k) e", p=P)
                    for half in range(2):
                        load_unit(PHASES["pool"][0] + half, wp[:, half * TT:(half + 1) * TT, :], width=POOL_KT * P)
                    load_emb(PHASES["emb1b"][0], 1, 1)
                up = w_up[layer].rearrange("(k p) f -> p k f", p=P)
                down = w_down[layer].rearrange("(k p) f -> p k f", p=P)
                gate = w_ple_gate[layer].rearrange("(k p) f -> p k f", p=P)
                done = 0
                for part, tiles in enumerate(FFN_PARTS):
                    stream(f"up{layer}{part}",
                           lambda a, u: up[:, :, bass.ds((2 * a + u // 2 + done) * P + (u % 2) * D_FF, P)])
                    stream(f"down{layer}{part}",
                           lambda a, u: down[:, done:done + tiles, bass.ds((SLOTS * a + u) * P, P)])
                    done += tiles
                stream(f"ple{layer}", lambda a, u: gate[:, :, bass.ds((SLOTS * a + u) * P, P)])
            half = TT // 2
            for t in range(half):
                for scaled, tile in ((y_dve, t), (y_act, half + t)):
                    sp.wait_ge(scaled, t + 1)
                    sp.dma_start(out.rearrange("b (t p) d -> p (b t) d", p=P)[:, tile, :], y_tok[:, tile, :]).then_inc(out_done, 16)
            sp.wait_ge(out_done, 16 * TT)

        @block.scalar
        def _(act):
            def split_hi(n, a=0):
                if n >= N_UNITS:
                    return
                s, w = slot_of(n), blocks_of(n) * P
                act.wait_ge(raw_in[s], landed(n, a))
                if n >= FIRST_RING4 + 1:
                    act.wait_ge(unit_done, SLOTS * a + n - SLOTS + 1)
                act.activation(w_hi[s][:, 0:w], w_raw[s][:, 0:w], ACT.Copy).then_inc(hi_done, 1)

            def split_hi_qkv(hd, which):
                act.wait_ge(raw_in[which], 16 * hd + 16)
                if not isinstance(hd, int) or hd > 0:
                    act.wait_ge(unit_done, 3 * hd + which - 2)
                act.activation(w_hi[which][:, 0:KT * P], w_raw[which][:, 0:KT * P], ACT.Copy).then_inc(hi_done, 1)

            def rms_of(norm):
                act.wait_ge(ss_done, norm)
                act.activation(rms_col, bank[7][:, 0:TT], ACT.Sqrt, bias=eps[:, 0:1]).then_inc(rms_done, 1)

            def inverse(norm):
                act.wait_ge(spread_done, spread_of[norm])
                act.activation(inv[:, :], bank[7 if norm else 2][:, :], ACT.Copy, scale=float(D_MODEL)).then_inc(inv_done, 1)

            act.dma_start(gain0_rows[:, :], mix_norm_g[0].rearrange("(j p) -> j p", p=P)).then_inc(gain0_in, 16)

            def token_squares(t):
                act.wait_ge(x_in[t], 16)
                if t:
                    act.wait_ge(tok_ss, t)
                act.activation(square_scratch[:, :], x_tok[:, t, :], ACT.Square,
                               accum_out=tok_sum[:, t:t + 1]).then_inc(tok_ss, 1)

            for t in range(TT - 1):
                token_squares(t)
            split_hi_qkv(0, 0)
            act.wait_ge(gain0_done, 1)
            for kt in range(KT):
                act.wait_ge(x_T, kt + 1)
                act.activation(x_hi[:, kt, :], bank[kt][:, :], ACT.Copy, scale=gain0[:, kt:kt + 1]).then_inc(xhi_done, 1)
                if kt == KT // 2 - 1:
                    token_squares(TT - 1)
            split_hi_qkv(0, 1)
            act.wait_ge(tok_ss, TT)
            act.wait_ge(const_done, 3)
            act.activation(rms_col, tok_sum, ACT.Sqrt, bias=eps[:, 0:1], scale=1.0 / D_MODEL).then_inc(rms_done, 1)
            for kt in range(KT // 2, KT):
                act.wait_ge(x_ready, kt + 1)
                act.activation(h[:, kt, :], bank[kt][:, :], ACT.Copy).then_inc(h_act, 1)

            def start_rest():
                for j in range(DEPTH * PLE_KT):
                    act.wait_ge(p_T, j + 1)
                    act.activation(pT_hi[:, j, :], bank[4 + j][:, :], ACT.Copy).then_inc(pT_hi_done, 1)
                act.wait_ge(lam_sum, 1)
                act.activation(lam_e, bank[2][:, 0:2], ACT.Exp, scale=float(D_MODEL)).then_inc(lam_exp, 1)

            def q_high(hd):
                act.wait_ge(unit_done, 3 * hd + 1)
                for c in range(2):
                    act.activation(q_hi[own[c], c, :], bank[0][own[c], :], ACT.Copy).then_inc(qhi_done, 1)
                for c in range(2):
                    act.wait_ge(qhi_done, 2 * hd + c + 1)
                    act.activation(q_hi[other[c], c, :], q_hi[own[c], c, :].bitcast(F32), ACT.Copy).then_inc(qtwin_done, 1)

            def k_high(hd):
                act.wait_ge(k32_done, hd + 1)
                for c in range(2):
                    act.activation(k_hilo[own[c], c, :], k32[own[c], :], ACT.Copy).then_inc(khi_done, 1)

            def transposed_high(hp):
                act.wait_ge(v_T, hp + 1)
                act.activation(v_hi[:, :, :].rearrange("p t c -> p (t c)"), bank[5][:, :], ACT.Copy).then_inc(vhi_done, 1)
                for b, (at, w) in enumerate(WT_BANKS):
                    act.wait_ge(w_T, 3 * hp + b + 1)
                    act.activation(wT_hi[:, at:at + w], bank[2 + b][:, 0:w], ACT.Copy).then_inc(wthi_done, 1)

            def output_high(hp):
                act.wait_ge(onorm_done, hp + 1)
                act.activation(oT_hi[:, hp, :], o32[:, :], ACT.Copy).then_inc(ohi_done, 1)

            def output_copy(hp, back):
                act.wait_ge(pv_done, hp + 1)
                act.activation(sq[:, 0, :], bank[6][:, :], ACT.Square).then_inc(osq_done, 1)
                if back:
                    act.wait_ge(olo_done, hp)
                act.activation(o32[:, :], bank[6][:, :], ACT.Copy, scale=sub_g_scaled).then_inc(o32_done, 1)

            def output_rms(hp, src):
                act.wait_ge(oss_done, hp + 1)
                act.activation(orms_col, src[:, 0:TT], ACT.Sqrt, bias=eps[:, 0:1],
                               scale=float(D_MODEL // P)).then_inc(orms_done, 1)

            def exps(hd):
                for qt in range(TT):
                    w = (qt + 1) * P
                    act.wait_ge(neg_done, 2 * hd + qt // 2 + 1)
                    for c in range(2):
                        at = key_off(qt)
                        act.activation(probs[:, c, at:at + w], scores_at(qt, c), ACT.Exp, scale=qscale[:, qt:qt + 1],
                                       bias=negmx[:, 2 * qt + c:2 * qt + c + 1],
                                       accum_out=sums[:, 2 * qt + c:2 * qt + c + 1]).then_inc(exp_done, 1)

            def head(hd, back, split_next):
                split_hi_qkv(hd, 2)
                q_high(hd)
                if back == 0:
                    inverse(NORM_MIX0)
                k_high(hd)
                if back == 0:
                    start_rest()
                else:
                    transposed_high(hd - 1)
                split_next(0)
                split_next(1)
                if back >= 2:
                    output_high(hd - 2)
                if back >= 1:
                    output_copy(hd - 1, back >= 2)
                    output_rms(hd - 1, bank[1])
                exps(hd)

            head(0, 0, lambda i: split_hi_qkv(1, i))
            act.wait_ge(subg_done, 1)
            head(1, 1, lambda i: split_hi_qkv(2, i))
            with act.Fori(2, N_HEADS - 1) as hd:
                head(hd, 2, lambda i: split_hi_qkv(hd + 1, i))
            last = N_HEADS - 1
            head(last, 2, lambda i: split_hi(FIRST_RING4 + i))
            transposed_high(last)
            split_hi(FIRST_RING4 + 2)
            act.wait_ge(pv_done, last + 1)
            act.activation(sq[:, 0, :], bank[6][:, :], ACT.Square).then_inc(osq_done, 1)
            output_high(last - 1)
            act.wait_ge(olo_done, last)
            act.activation(o32[:, :], bank[6][:, :], ACT.Copy, scale=sub_g_scaled).then_inc(o32_done, 1)
            split_hi(FIRST_RING4 + 3)
            output_rms(last, bank[4])
            output_high(last)

            def loop(name, body):
                bodies = PHASES[name][1] // SLOTS
                alone = 1 if name == "up10" else 0
                if alone:
                    body(0, split_ahead=True)
                with act.Fori(alone, bodies - 1) as a:
                    body(a)
                body(bodies - 1)

            def look_hi(name, u, a):
                n = PHASES[name][0] + u + LOOK
                if isinstance(a, int):
                    split_hi(n + SLOTS * a)
                else:
                    split_hi(n, a)

            def y_copy(m):
                act.wait_ge(y_T, m + 1)
                act.activation(y_tok[:, :, m * P:(m + 1) * P],
                               bank[5 + m % 2][:, :].rearrange("p (t c) -> p t c", c=P), ACT.Copy).then_inc(y_copied, 1)

            def residual_tile(name, m, norm, g, dst=x_hi):
                n_sq = KT * (norm - 1) + m
                act.wait_ge(evac_done, result_of(name, m))
                if g is not None:
                    act.activation(dst[:, m, :], h[:, m, :], ACT.Copy, scale=g).then_inc(xhi_done, 1)
                if n_sq >= 2:
                    act.wait_ge(acc_done, n_sq - 1)
                act.activation(sq[:, n_sq % 2, :], h[:, m, :], ACT.Square).then_inc(sq_done, 1)

            def residual_phase(name, norm, layer, which, look=LOOK, before_last=None):
                for m in range(KT):
                    if m + look < KT + LOOK:
                        split_hi(PHASES[name][0] + m + look)
                    if before_last and m == KT - 1:
                        before_last()
                    if norm is not None:
                        residual_tile(name, m, norm, gain(layer, which, m))

            def add_pool_bias(m):
                act.wait_ge(x_ready, KT * NORM_MIX1 + m + 1)
                act.activation(h[:, m, :], h[:, m, :], ACT.Identity, bias=bs[:, m:m + 1]).then_inc(h_biased, 1)

            def wait_tile(n, t, tile_sem, before):
                if t == TT - 1:
                    act.wait_ge(unit_done, n + 1)
                else:
                    act.wait_ge(tile_sem, before + t + 1)

            def emb_copy(layer, half, n, tiles=range(TT)):
                for m in (half * TT + t for t in tiles):
                    wait_tile(n, m % TT, emb_mm, (2 * layer + half) * (TT - 1))
                    act.activation(emb[:, m, :], bank[4 + m % 3][:, :], ACT.Copy).then_inc(emb_done, 1)

            residual_phase("wo", NORM_FFN0, 0, FFN, look=SLOTS,
                           before_last=lambda: emb_copy(0, 0, PHASES["emb0"][0], range(0, 2)))
            split_hi(PHASES["emb0"][0] + LOOK)
            emb_copy(0, 0, PHASES["emb0"][0], range(2, 4))
            rms_of(NORM_FFN0)
            split_hi(PHASES["emb0"][0] + 1 + LOOK)
            emb_copy(0, 1, PHASES["emb0"][0] + 1)
            inverse(NORM_FFN0)
            for layer in range(DEPTH):
                if layer:
                    split_hi(PHASES["emb1a"][0] + LOOK)
                    rms_of(NORM_MIX1)
                    act.wait_ge(icol_done, NORM_MIX1 + 1)

                    def z_high(half, t):
                        wait_tile(PHASES["pool"][0] + half, t, z_mm, half * (TT - 1))
                        act.activation(z_hi[half][:, t, :], z_bank(half * TT + t)[:, :], ACT.Copy,
                                       scale=icol[:, t:t + 1]).then_inc(zhi_done, 1)

                    def pooled_tile(m):
                        residual_tile("pool", m, NORM_FFN1, gain(1, FFN, m))

                    for t in range(TT):
                        z_high(0, t)
                        if t == 0:
                            emb_copy(1, 0, PHASES["emb1a"][0], [TT - 1])
                        if t % 2:
                            split_hi(PHASES["pool"][0] + t // 2 + LOOK)
                    z_high(1, 0)
                    z_high(1, 1)
                    for m in range(KT):
                        pooled_tile(m)
                        if m < 2:
                            z_high(1, m + 2)
                        if m == 1:
                            split_hi(PHASES["emb1b"][0] + LOOK)
                        if 3 <= m < KT - 1:
                            emb_copy(1, 1, PHASES["emb1b"][0], [m - 3])
                    rms_of(NORM_FFN1)
                    split_hi(PHASES["emb1b"][0] + 1 + LOOK)
                    inverse(NORM_FFN1)
                done = 0
                for part, tiles in enumerate(FFN_PARTS):
                    name = f"up{layer}{part}"
                    pairs = layer * FT + done

                    def up_body(a, split_ahead=False):
                        for v in range(2):
                            j = 2 * a + v + done
                            pair = 2 * a + v + pairs
                            for c in range(2):
                                if v + c > 0 or not split_ahead:
                                    look_hi(name, 2 * v + c, a)
                                act.wait_ge(evac_done, SLOTS * a + result_of(name, 2 * v + c))
                                act.activation(c32[:, c, :], u32[:, c, PAD:PAD + SEQ], ACT.Identity,
                                               scale=tap(layer, 2, j + c * FT),
                                               bias=conv_bias(layer, j + c * FT)).then_inc(tap_done, 1)
                                if c == 0:
                                    act.wait_ge(conv_done, 2 * pair + 1)
                                    act.activation(s32[:, :], c32[:, 0, :], ACT.Silu).then_inc(silu_done, 1)
                            act.wait_ge(gmul_done, pair + 1)
                            act.activation(g_hi[:, 2 * a + v, :], g32[:, :], ACT.Copy).then_inc(ghi_done, 1)

                    loop(name, up_body)
                    norm = (NORM_PLE1 if layer else NORM_PLE0) if part == LAST else None
                    residual_phase(f"down{layer}{part}", norm, layer, PLE)
                    done += tiles
                name = f"ple{layer}"
                norm = NORM_PLE1 if layer else NORM_PLE0
                split_hi(PHASES[name][0] + LOOK)
                rms_of(norm)
                split_hi(PHASES[name][0] + LOOK + 1)
                split_hi(PHASES[name][0] + LOOK + 2)
                inverse(norm)
                for m in range(KT):
                    act.wait_ge(arg_done, KT * layer + m + 1)
                    act.activation(s32[:, :], c32[:, 0, :], ACT.Sigmoid).then_inc(sig_done, 1)
                    if 2 <= m < KT - 1:
                        split_hi(PHASES[name][0] + m + LOOK + 1)
                    if layer == 0:
                        if m == 1:
                            act.wait_ge(band_diff, 2)
                            act.activation(band[:, :, :], band32[:, :, :], ACT.Copy).then_inc(band_done, 1)
                            act.activation(first_band[:, :, 0:EDGE], edge32[:, :, :], ACT.Copy).then_inc(band_done, 1)
                            act.activation(first_band[:, :, EDGE:], band32[:, :, EDGE:], ACT.Copy).then_inc(band_done, 1)
                        if m == KT - 1:
                            emb_copy(1, 0, PHASES["emb1a"][0], range(0, 2))
                        residual_tile(name, m, NORM_MIX1, gain(1, MIX, m), xp_hi)
                        if m > 0:
                            add_pool_bias(m - 1)
                    else:
                        if m >= 2:
                            y_copy(m - 2)
                        if m == KT - 1:
                            act.activation(table_scratch, eps[:, 0:1], ACT.Sqrt).then_inc(table_loaded, 1)
                        residual_tile(name, m, NORM_FINAL, None)
                        act.activation(y_gained[:, m, :], h[:, m, :], ACT.Copy, scale=final_gain[:, m:m + 1]).then_inc(gained_done, 1)
                if layer == 0:
                    emb_copy(1, 0, PHASES["emb1a"][0], [2])
                    add_pool_bias(KT - 1)
            y_copy(KT - 2)
            rms_of(NORM_FINAL)
            y_copy(KT - 1)
            act.wait_ge(icol_done, NORM_FINAL + 1)
            act.wait_ge(y_copied, KT)
            for t in range(TT // 2, TT):
                act.activation(y_tok[:, t, :], y_tok[:, t, :], ACT.Copy, scale=icol[:, t:t + 1]).then_inc(y_act, 1)

        @block.gpsimd
        def _(pool):
            pool.memset(ident[:, :], 0.0).then_inc(ident_zero, 1)
            pool.memset(ones[:, :], 1.0 / D_MODEL).then_inc(const_done, 1)
            pool.memset(eps[:, :], EPS).then_inc(const_done, 1)
            pool.wait_ge(ident_zero, 1)
            pool.affine_select(out=ident[:, :], in_=ident[:, :], compare_op=ALU.not_equal, fill=1.0, base=0,
                               pattern=[[-1, P]], channel_multiplier=1).then_inc(const_done, 1)
            pool.memset(mask16[:, :, :], 0.0).then_inc(ident_zero, 1)
            pool.memset(ident16[:, :], 0.0).then_inc(ident_zero, 1)
            pool.wait_ge(ident_zero, 3)
            pool.affine_select(out=mask16[:, :, :], in_=mask16[:, :, :], compare_op=ALU.is_ge, fill=MASKED, base=0,
                               pattern=[[0, 2], [-1, P]], channel_multiplier=1).then_inc(mask_done, 1)
            pool.affine_select(out=ident16[:, :], in_=ident16[:, :], compare_op=ALU.not_equal, fill=1.0, base=0,
                               pattern=[[-1, P]], channel_multiplier=1).then_inc(mask_done, 1)
            pool.memset(q_lo[:, :, :].bitcast(F32), 0.0).then_inc(qpad_zero, 1)
            pool.wait_ge(evac_done, result_of("wo", KT - 1))
            for g, win in enumerate(POOL_WINDOWS):
                pool.memset(band32[:, g, :], 1.0 / win).then_inc(band_one, 1)
                pool.memset(edge32[:, g, win - 1:], 1.0 / win).then_inc(band_one, 1)
                for t in range(win - 1):
                    pool.memset(edge32[:, g, t:t + 1], 1.0 / (t + 1)).then_inc(band_one, 1)
            pool.wait_ge(band_one, len(POOL_WINDOWS) + sum(POOL_WINDOWS))
            for mat, width in ((band32, BAND), (edge32, EDGE)):
                pool.affine_select(out=mat[:, :, :], in_=mat[:, :, :], compare_op=ALU.is_ge, fill=0.0, base=0,
                                   pattern=[[0, G], [1, width]], channel_multiplier=-1).then_inc(band_below, 1)
            pool.wait_ge(band_below, 2)
            for mat, width in ((band32, BAND), (edge32, EDGE)):
                for g, win in enumerate(POOL_WINDOWS):
                    pool.affine_select(out=mat[:, g, :], in_=mat[:, g, :], compare_op=ALU.is_ge, fill=0.0, base=win - 1,
                                       pattern=[[-1, width]], channel_multiplier=1).then_inc(band_set, 1)

        @block.vector
        def _(dve):
            def split_lo(n, a=0):
                if n >= N_UNITS:
                    return
                s, w = slot_of(n), blocks_of(n) * P
                dve.wait_ge(hi_done, SLOTS * a + n + 1)
                dve.tensor_tensor(w_lo[s][:, 0:w], w_raw[s][:, 0:w], w_hi[s][:, 0:w].bitcast(F32),
                                  ALU.subtract).then_inc(lo_done, 1)

            def split_lo_qkv(hd, which):
                w = KT * P
                dve.wait_ge(hi_done, 3 * hd + which + 1)
                dve.tensor_tensor(w_lo[which][:, 0:w], w_raw[which][:, 0:w], w_hi[which][:, 0:w].bitcast(F32),
                                  ALU.subtract).then_inc(lo_done, 1)

            dve.wait_ge(const_done, 3)
            dve.tensor_copy(ones_r[:, :], ones[:, :]).then_inc(ones_done, 1)
            dve.wait_ge(gain0_T, 1)
            dve.tensor_copy(gain0[:, :], bank[7][:, 0:KT]).then_inc(gain0_done, 1)

            def h_copy(kt):
                dve.wait_ge(xhi_done, kt + 1)
                dve.tensor_copy(h[:, kt, :], bank[kt][:, :]).then_inc(h_dve, 1)

            def x0_low(kt):
                dve.wait_ge(xhi_done, kt + 1)
                dve.scalar_tensor_tensor(out=x_lo[:, kt, :], in0=bank[kt][:, :], scalar=gain0[:, kt:kt + 1],
                                         in1=x_hi[:, kt, :].bitcast(F32), op0=ALU.mult, op1=ALU.subtract).then_inc(x_ready, 1)

            def x_low(norm, m, g, hi=x_hi, lo=x_lo):
                dve.wait_ge(xhi_done, KT * norm + m + 1)
                dve.scalar_tensor_tensor(out=lo[:, m, :], in0=h[:, m, :], scalar=g, in1=hi[:, m, :].bitcast(F32),
                                         op0=ALU.mult, op1=ALU.subtract).then_inc(x_ready, 1)

            def spread(column, parts_sem, before):
                hi, lo = col_parts[:, 0:TT], col_parts[:, TT:2 * TT]
                dve.tensor_copy(hi, column).then_inc(parts_sem, 1)
                dve.wait_ge(parts_sem, before + 1)
                dve.tensor_tensor(lo, column, hi.bitcast(F32), ALU.subtract).then_inc(parts_sem, 1)
                dve.wait_ge(parts_sem, before + 2)
                return dve.tensor_tensor(
                    diag[:, :, :].rearrange("p x (t c) -> p (x t) c", c=P),
                    ident[:, :].rearrange("p (o c) -> p o c", o=1).broadcast_to((P, 2 * TT, P)),
                    col_parts[:, :].bitcast(F32).rearrange("p (t o) -> p t o", o=1).broadcast_to((P, 2 * TT, P)), ALU.mult)

            def inverse(norm):
                dve.wait_ge(rms_done, norm + 1)
                dve.reciprocal(icol, rms_col).then_inc(icol_done, 1)
                dve.wait_ge(icol_done, norm + 1)
                if norm in spread_of:
                    spread(icol, parts_done, 2 * spread_of[norm] - 2).then_inc(diag_done, 1)

            split_lo_qkv(0, 0)
            x0_low(0)
            h_copy(0)
            for kt in range(1, KT):
                x0_low(kt)
            h_copy(1)
            split_lo_qkv(0, 1)
            h_copy(2)
            inverse(NORM_MIX0)
            for scaled, s in ((qscale, ATTN_SCALE), (neg_qscale, -ATTN_SCALE)):
                dve.tensor_scalar(scaled, icol, s, None, ALU.mult).then_inc(qscale_done, 1)
            h_copy(3)

            def lambda_products():
                dve.wait_ge(lam_in, 64)
                for i in range(2):
                    dve.tensor_tensor(lam_rows[:, 4 + i:5 + i], lam_rows[:, 2 * i:2 * i + 1],
                                      lam_rows[:, 2 * i + 1:2 * i + 2], ALU.mult).then_inc(lam_prod, 1)

            def start_rest():
                dve.wait_ge(par_T, 1)
                for t in range(4):
                    dve.tensor_copy(params[:, t, 0:par_count[t]], bank[3][:, t * P:t * P + par_count[t]]).then_inc(par_done, 1)
                dve.wait_ge(par_done, 4)
                dve.tensor_tensor(bs[:, :], pool_b, pool_s, ALU.mult).then_inc(bs_done, 1)
                dve.tensor_scalar(sub_g_scaled, sub_g, 1.0 - LAMBDA_INIT, None, ALU.mult).then_inc(subg_done, 1)
                for j in range(DEPTH * PLE_KT):
                    dve.wait_ge(pT_hi_done, j + 1)
                    dve.tensor_tensor(pT_lo[:, j, :], bank[4 + j][:, :], pT_hi[:, j, :].bitcast(F32),
                                      ALU.subtract).then_inc(pT_done, 1)
                dve.wait_ge(lam_exp, 1)
                dve.tensor_tensor(lam, lam_e[:, 0:1], lam_e[:, 1:2], ALU.subtract).then_inc(lam_diff, 1)
                dve.wait_ge(lam_diff, 1)
                dve.tensor_scalar(lam, lam, LAMBDA_INIT, None, ALU.add).then_inc(lam_done, 1)

            def q_low(hd):
                for c in range(2):
                    dve.wait_ge(qhi_done, 2 * hd + c + 1)
                    dve.tensor_tensor(q_lo[own[c], c, :], bank[0][own[c], :], q_hi[own[c], c, :].bitcast(F32),
                                      ALU.subtract).then_inc(qlo_done, 1)

            def k_rows(hd):
                dve.wait_ge(unit_done, 3 * hd + 2)
                dve.tensor_tensor(k32[:, :], bank[1][:, :], inv[:, :], ALU.mult).then_inc(k32_done, 1)

            def k_low(hd):
                for c in range(2):
                    dve.wait_ge(khi_done, 2 * hd + c + 1)
                    dve.tensor_tensor(k_hilo[other[c], c, :], k32[own[c], :], k_hilo[own[c], c, :].bitcast(F32),
                                      ALU.subtract).then_inc(klo_done, 1)

            def softmax_first(hd):
                for qt in range(TT):
                    dve.wait_ge(scores_done, 3 * hd + max(qt, 1))
                    if qt < 2:
                        both = bank[2 + qt][:, 0:2 * (qt + 1) * P].rearrange("p (c w) -> p c w", c=2)
                        dve.tensor_reduce(mx[:, 2 * qt:2 * qt + 2], both, AX_X, ALU.max).then_inc(max_done, 2)
                    else:
                        for c in range(2):
                            i = 2 * qt + c
                            dve.tensor_reduce(mx[:, i:i + 1], scores_at(qt, c), AX_X, ALU.max).then_inc(max_done, 1)
                    if qt % 2:
                        neg(hd, qt // 2)

            def neg(hd, half):
                dve.wait_ge(max_done, 2 * TT * hd + 4 * half + 4)
                both = neg_qscale[:, 2 * half:2 * half + 2].rearrange("p (t o) -> p t o", o=1).broadcast_to((P, 2, 2))
                dve.tensor_tensor(negmx[:, 4 * half:4 * half + 4].rearrange("p (t c) -> p t c", c=2),
                                  mx[:, 4 * half:4 * half + 4].rearrange("p (t c) -> p t c", c=2), both,
                                  ALU.mult).then_inc(neg_done, 1)

            def v_rows(hd):
                dve.wait_ge(unit_done, 3 * hd + 3)
                dve.tensor_tensor(vT[:, :], bank[0][:, :], inv[:, :], ALU.mult).then_inc(vT_done, 1)

            def softmax_second(hd):
                def second(qt):
                    at, w = key_off(qt), (qt + 1) * P
                    dve.tensor_scalar(probs[:, 1, at:at + w], probs[:, 1, at:at + w], rsums[:, 2 * qt + 1:2 * qt + 2], lam,
                                      ALU.mult, ALU.mult).then_inc(second_done, 1)

                def difference(qt):
                    at, w = key_off(qt), (qt + 1) * P
                    dve.wait_ge(second_done, TT * hd + qt + 1)
                    dve.scalar_tensor_tensor(out=probs[:, 0, at:at + w], in0=probs[:, 0, at:at + w],
                                             scalar=rsums[:, 2 * qt:2 * qt + 1], in1=probs[:, 1, at:at + w],
                                             op0=ALU.mult, op1=ALU.subtract).then_inc(w_done, 1)

                for half in range(2):
                    first, cols = TT // 2 * half, slice(TT * half, TT * (half + 1))
                    dve.wait_ge(exp_done, 2 * TT * hd + TT * (half + 1))
                    dve.reciprocal(rsums[:, cols], sums[:, cols]).then_inc(rsum_done, 1)
                    dve.wait_ge(rsum_done, 2 * hd + half + 1)
                    second(first)
                    second(first + 1)
                    difference(first)
                    difference(first + 1)

            def transposed_low(hp):
                dve.wait_ge(vhi_done, hp + 1)
                dve.tensor_tensor(v_lo[:, :, :].rearrange("p t c -> p (t c)"), bank[5][:, :],
                                  v_hi[:, :, :].rearrange("p t c -> p (t c)").bitcast(F32), ALU.subtract).then_inc(vlo_done, 1)
                for b, (at, w) in enumerate(WT_BANKS):
                    dve.wait_ge(wthi_done, 3 * hp + b + 1)
                    dve.tensor_tensor(wT_lo[:, at:at + w], bank[2 + b][:, 0:w], wT_hi[:, at:at + w].bitcast(F32),
                                      ALU.subtract).then_inc(wtlo_done, 1)

            def output_inverse(hp):
                dve.wait_ge(orms_done, hp + 1)
                dve.reciprocal(oicol, orms_col).then_inc(oicol_done, 1)
                dve.wait_ge(oicol_done, hp + 1)
                spread(oicol, oparts_done, 2 * hp).then_inc(odiag_done, 1)

            def output_norm(hp):
                dve.wait_ge(ospread_done, hp + 1)
                dve.scalar_tensor_tensor(out=o32[:, :], in0=bank[7][:, :], scalar=float(D_MODEL), in1=o32[:, :],
                                         op0=ALU.mult, op1=ALU.mult).then_inc(onorm_done, 1)

            def output_low(hp):
                dve.wait_ge(ohi_done, hp + 1)
                dve.tensor_tensor(oT_lo[:, hp, :], o32[:, :], oT_hi[:, hp, :].bitcast(F32), ALU.subtract).then_inc(olo_done, 1)

            def head(hd, back, split_next):
                q_low(hd)
                split_lo_qkv(hd, 2)
                if back >= 2:
                    output_inverse(hd - 2)
                if back == 0:
                    dve.wait_ge(inv_done, 1)
                k_rows(hd)
                k_low(hd)
                if back == 0:
                    start_rest()
                else:
                    transposed_low(hd - 1)
                split_next(0)
                if back >= 2:
                    output_norm(hd - 2)
                split_next(1)
                if back >= 2:
                    output_low(hd - 2)
                v_rows(hd)
                softmax_first(hd)
                softmax_second(hd)

            lambda_products()
            dve.wait_ge(qpad_zero, 1)
            dve.wait_ge(qscale_done, 2)
            head(0, 0, lambda i: split_lo_qkv(1, i))
            head(1, 1, lambda i: split_lo_qkv(2, i))
            with dve.Fori(2, N_HEADS - 1) as hd:
                head(hd, 2, lambda i: split_lo_qkv(hd + 1, i))
            last = N_HEADS - 1
            head(last, 2, lambda i: split_lo(FIRST_RING4 + i))
            output_inverse(last - 1)
            transposed_low(last)
            split_lo(FIRST_RING4 + 2)
            output_norm(last - 1)
            output_low(last - 1)
            split_lo(FIRST_RING4 + 3)
            output_inverse(last)
            output_norm(last)
            output_low(last)

            def residual_add(m, src):
                dve.tensor_tensor(h[:, m, :], src, h[:, m, :], ALU.add).then_inc(evac_done, 1)

            def sum_squares(norm, m):
                n_sq = KT * (norm - 1) + m
                dve.wait_ge(sq_done, n_sq + 1)
                if m:
                    dve.wait_ge(acc_done, n_sq)
                    dve.tensor_tensor(acc[:, :], acc[:, :], sq[:, n_sq % 2, :], ALU.add).then_inc(acc_done, 1)
                else:
                    dve.tensor_copy(acc[:, :], sq[:, n_sq % 2, :]).then_inc(acc_done, 1)

            def residual_phase(name, norm, layer, which, look=LOOK):
                for m in range(KT):
                    n = PHASES[name][0] + m
                    if m + look < KT + LOOK:
                        split_lo(n + look)
                    dve.wait_ge(unit_done, n + 1)
                    residual_add(m, bank[m % SLOTS][:, :])
                    if norm is not None and m > 0:
                        x_low(norm, m - 1, gain(layer, which, m - 1))
                        sum_squares(norm, m - 1)
                if norm is not None:
                    x_low(norm, KT - 1, gain(layer, which, KT - 1))
                    sum_squares(norm, KT - 1)

            def loop(name, body):
                bodies = PHASES[name][1] // SLOTS
                alone = 1 if name == "up10" else 0
                if alone:
                    body(0, split_ahead=True)
                with dve.Fori(alone, bodies - 1) as a:
                    body(a)
                body(bodies - 1)

            def look_lo(name, u, a):
                n = PHASES[name][0] + u + LOOK
                if isinstance(a, int):
                    split_lo(n + SLOTS * a)
                else:
                    split_lo(n, a)

            residual_phase("wo", NORM_FFN0, 0, FFN, look=SLOTS)
            split_lo(PHASES["emb0"][0] + LOOK)
            inverse(NORM_FFN0)
            split_lo(PHASES["emb0"][0] + 1 + LOOK)
            dve.wait_ge(inv_done, spread_of[NORM_FFN0])
            for layer in range(DEPTH):
                if layer:
                    split_lo(PHASES["emb1a"][0] + LOOK)
                    inverse(NORM_MIX1)

                    def z_low(half, t):
                        i = half * TT + t
                        dve.wait_ge(zhi_done, i + 1)
                        dve.scalar_tensor_tensor(out=z_lo[half][:, t, :], in0=z_bank(i)[:, :],
                                                 scalar=icol[:, t:t + 1], in1=z_hi[half][:, t, :].bitcast(F32),
                                                 op0=ALU.mult, op1=ALU.subtract).then_inc(zlo_done, 1)

                    def add_pooled(m):
                        dve.wait_ge(pool_mm, m + 1)
                        dve.wait_ge(h_biased, m + 1)
                        dve.scalar_tensor_tensor(out=h[:, m, :], in0=bank[m % SLOTS][:, :], scalar=pool_s[:, m:m + 1],
                                                 in1=h[:, m, :], op0=ALU.mult, op1=ALU.add).then_inc(evac_done, 1)

                    def next_input(m):
                        x_low(NORM_FFN1, m, gain(1, FFN, m))
                        sum_squares(NORM_FFN1, m)

                    for t in range(TT):
                        z_low(0, t)
                        if t % 2:
                            split_lo(PHASES["pool"][0] + t // 2 + LOOK)
                    z_low(1, 0)
                    for m in range(KT):
                        add_pooled(m)
                        if m < 3:
                            z_low(1, m + 1)
                        if m == 2:
                            split_lo(PHASES["emb1b"][0] + LOOK)
                        if m > 0:
                            next_input(m - 1)
                    next_input(KT - 1)
                    inverse(NORM_FFN1)
                    split_lo(PHASES["emb1b"][0] + 1 + LOOK)
                    dve.wait_ge(inv_done, spread_of[NORM_FFN1])
                dve.memset(u32[:, :, 0:PAD], 0.0).then_inc(pad_zero, 1)
                dve.wait_ge(pad_zero, layer + 1)
                done = 0
                for part, tiles in enumerate(FFN_PARTS):
                    name = f"up{layer}{part}"
                    pairs = layer * FT + done

                    def up_body(a, split_ahead=False):
                        for v in range(2):
                            j = 2 * a + v + done
                            pair = 2 * a + v + pairs
                            for c in range(2):
                                n = PHASES[name][0] + 2 * v + c
                                dve.wait_ge(unit_done, SLOTS * a + n + 1)
                                dve.tensor_tensor(u32[:, c, PAD:], bank[2 * v + c][:, :], inv[:, :],
                                                  ALU.mult).then_inc(evac_done, 1)
                                if v + c > 0 or not split_ahead:
                                    look_lo(name, 2 * v + c, a)
                                dve.wait_ge(tap_done, 2 * pair + c + 1)
                                dve.scalar_tensor_tensor(
                                    out=c32[:, c, :], in0=u32[:, c, PAD - 1:PAD - 1 + SEQ],
                                    scalar=tap(layer, 1, j + c * FT), in1=c32[:, c, :],
                                    op0=ALU.mult, op1=ALU.add).then_inc(conv1_done, 1)
                                dve.wait_ge(conv1_done, 2 * pair + c + 1)
                                dve.scalar_tensor_tensor(
                                    out=c32[:, c, :], in0=u32[:, c, PAD - 2:PAD - 2 + SEQ],
                                    scalar=tap(layer, 0, j + c * FT), in1=c32[:, c, :],
                                    op0=ALU.mult, op1=ALU.add).then_inc(conv_done, 1)
                            dve.wait_ge(silu_done, pair + 1)
                            dve.wait_ge(conv_done, 2 * pair + 2)
                            dve.tensor_tensor(g32[:, :], s32[:, :], c32[:, 1, :], ALU.mult).then_inc(gmul_done, 1)
                            dve.wait_ge(ghi_done, pair + 1)
                            dve.tensor_tensor(g_lo[:, 2 * a + v, :], g32[:, :], g_hi[:, 2 * a + v, :].bitcast(F32),
                                              ALU.subtract).then_inc(glo_done, 1)

                    loop(name, up_body)
                    norm = (NORM_PLE1 if layer else NORM_PLE0) if part == LAST else None
                    residual_phase(f"down{layer}{part}", norm, layer, PLE)
                    done += tiles
                name = f"ple{layer}"
                norm = NORM_PLE1 if layer else NORM_PLE0
                split_lo(PHASES[name][0] + LOOK)
                inverse(norm)
                if layer == 0:
                    dve.wait_ge(band_set, 2 * G)
                    for mat, width in ((band32, P), (edge32, EDGE)):
                        dve.tensor_tensor(mat[:, :, 0:width], mat[:, :, 0:width],
                                          ident[:, 0:width].rearrange("p (o c) -> p o c", o=1).broadcast_to((P, G, width)),
                                          ALU.subtract).then_inc(band_diff, 1)
                split_lo(PHASES[name][0] + LOOK + 1)
                split_lo(PHASES[name][0] + LOOK + 2)
                dve.wait_ge(inv_done, spread_of[norm])
                squared = NORM_FINAL if layer else NORM_MIX1

                def next_input(m):
                    if layer == 0:
                        x_low(NORM_MIX1, m, gain(1, MIX, m), xp_hi, xp_lo)
                    sum_squares(squared, m)

                for m in range(KT):
                    n = PHASES[name][0] + m
                    dve.wait_ge(unit_done, n + 1)
                    dve.tensor_tensor(c32[:, 0, :], bank[m % SLOTS][:, :], inv[:, :], ALU.mult).then_inc(arg_done, 1)
                    if m > 0:
                        next_input(m - 1)
                    if layer == 0 and m == 2:
                        dve.wait_ge(band_done, 3)
                        dve.tensor_tensor(edge_lo[:, :, :], edge32[:, :, :], first_band[:, :, 0:EDGE].bitcast(F32),
                                          ALU.subtract).then_inc(edge_done, 1)
                    dve.wait_ge(sig_done, KT * layer + m + 1)
                    dve.wait_ge(emb_done, KT * layer + m + 1)
                    dve.tensor_tensor(c32[:, 1, :], emb[:, m, :], s32[:, :], ALU.mult).then_inc(ple_done, 1)
                    dve.wait_ge(ple_done, KT * layer + m + 1)
                    residual_add(m, c32[:, 1, :])
                    if 2 <= m < KT - 1:
                        split_lo(n + LOOK + 1)
                if layer == 0:
                    next_input(KT - 1)
            inverse(NORM_FINAL)
            dve.wait_ge(y_copied, KT)
            for t in range(TT // 2):
                dve.tensor_scalar(y_tok[:, t, :], y_tok[:, t, :], icol[:, t:t + 1], None, ALU.mult).then_inc(y_dve, 1)

        @block.tensor
        def _(pe):
            def exact(dst, parts, start=True, stop=True):
                for i, ((w1, w0), (m1, m0), before) in enumerate(parts):
                    before()
                    pe.matmul(dst, w1, m1, start=start and i == 0, stop=False)
                    pe.matmul(dst, w1, m0, start=False, stop=False)
                    last = pe.matmul(dst, w0, m1, start=False, stop=stop and i == len(parts) - 1)
                return last

            def no_wait():
                pass

            def block_of(slot, k):
                return w_hi[slot][:, k * P:(k + 1) * P], w_lo[slot][:, k * P:(k + 1) * P]

            def x_parts(slot, ready=None):
                def wait(k):
                    return (lambda: pe.wait_ge(x_ready, ready + k)) if ready else no_wait
                return [(block_of(slot, k), (x_hi[:, k, :], x_lo[:, k, :]), wait(k)) for k in range(KT)]

            def y_transposes(m):
                pe.wait_ge(gained_done, m + 1)
                if m >= 2:
                    pe.wait_ge(y_copied, m - 1)
                else:
                    pe.wait_ge(emb_done, DEPTH * KT)
                for t in range(TT):
                    last = pe.transpose(bank[5 + m % 2][:, t * P:(t + 1) * P], y_gained[:, m, t * P:(t + 1) * P], ident[:, :])
                last.then_inc(y_T, 1)

            pe.wait_ge(const_done, 3)
            pe.wait_ge(gain0_in, 16)
            pe.transpose(bank[7][:, 0:KT], gain0_rows[:, :], ident[0:KT, 0:KT]).then_inc(gain0_T, 1)
            for t in range(TT):
                pe.wait_ge(x_in[t], 16)
                for kt in range(KT):
                    if t == 0 and kt == KT - 1:
                        pe.wait_ge(gain0_done, 1)
                    last = pe.transpose(bank[kt][:, t * P:(t + 1) * P], x_tok[:, t, kt * P:(kt + 1) * P], ident[:, :])
                    if t == TT - 1:
                        last.then_inc(x_T, 1)

            def project(hd, which, before):
                pe.wait_ge(lo_done, 3 * hd + which + 1)
                before()
                ready = 1 if isinstance(hd, int) and hd == 0 and which == 0 else None
                exact(bank[which % 2][:, :], x_parts(which, ready)).then_inc(unit_done, 1)

            def scores(hd, back):
                pe.wait_ge(qlo_done, 2 * hd + 2)
                pe.wait_ge(qtwin_done, 2 * hd + 2)
                pe.wait_ge(klo_done, 2 * hd + 2)
                for qt in range(TT):
                    if back >= 1:
                        if qt == 0:
                            pe.wait_ge(wtlo_done, 3 * hd - 1)
                        if qt == 2:
                            pe.wait_ge(wtlo_done, 3 * hd)
                            pe.wait_ge(vlo_done, hd)
                        if qt == 3:
                            pe.wait_ge(o32_done, hd)
                    if back >= 2 and qt == 3:
                        pe.wait_ge(onorm_done, hd - 1)
                    w = (qt + 1) * P
                    keys = slice(qt * P, (qt + 1) * P)
                    shared = qt < 2
                    for c in range(2):
                        dst = scores_at(qt, c)
                        pe.matmul(dst, q_hi[:, c, keys], k_hilo[:, c, 0:w], start=not (shared and c), stop=False,
                                  skip_group_check=shared)
                        pe.matmul(dst, q_lo[:, c, keys], k_hilo[:, c, 0:w], start=False, stop=False, skip_group_check=shared)
                        if not shared:
                            last = pe.matmul(dst[:, w - P:w], ident16[:, :], mask16[:, 0, :], start=False, stop=True)
                    if shared:
                        diagonals = bank[2 + qt][:, 0:2 * w].rearrange("p (c w) -> p c w", c=2)[:, :, w - P:w]
                        last = pe.matmul(diagonals, ident16[:, :], mask16[:, :, :], start=False, stop=True, skip_group_check=True)
                    if qt:
                        last.then_inc(scores_done, 1)
                    if qt == 1 and back >= 1:
                        output_sums(hd - 1, bank[1])

            def head_transposes(hp):
                pe.wait_ge(vT_done, hp + 1)
                pe.wait_ge(exp_done, 2 * TT * (hp + 1))
                for t in range(TT):
                    last = pe.transpose(bank[5][:, t * P:(t + 1) * P], vT[:, t * P:(t + 1) * P], ident[:, :])
                last.then_inc(v_T, 1)
                pe.wait_ge(w_done, TT * (hp + 1))
                for kt in range(TT):
                    for qt in range(kt, TT):
                        b = min(kt, 2)
                        at = wt_off(kt) + (qt - kt) * P - WT_BANKS[b][0]
                        src = key_off(qt) + kt * P
                        last = pe.transpose(bank[2 + b][:, at:at + P], probs[:, 0, src:src + P], ident[:, :])
                    if kt != 2:
                        last.then_inc(w_T, 1)

            def head_product(hp):
                pe.wait_ge(vlo_done, hp + 1)
                for kt in range(TT):
                    pe.wait_ge(wtlo_done, 3 * hp + min(kt, 2) + 1)
                    at, w = wt_off(kt), (TT - kt) * P
                    last = exact(bank[6][:, kt * P:SEQ],
                                 [((v_hi[:, kt, :], v_lo[:, kt, :]), (wT_hi[:, at:at + w], wT_lo[:, at:at + w]), no_wait)],
                                 start=kt == 0, stop=kt == TT - 1)
                last.then_inc(pv_done, 1)

            def token_sums(dst, squares):
                for t in range(TT):
                    last = pe.matmul(dst[:, t:t + 1], squares[:, t * P:(t + 1) * P], ones[:, 0:1], start=True, stop=True)
                return last

            def spread(dst):
                pe.matmul(dst[:, :], ones_r[:, :], diag[:, 0, :], start=True, stop=False)
                return pe.matmul(dst[:, :], ones_r[:, :], diag[:, 1, :], start=False, stop=True)

            def output_sums(hp, dst):
                pe.wait_ge(osq_done, hp + 1)
                token_sums(dst, sq[:, 0, :]).then_inc(oss_done, 1)

            def output_spread(hp):
                pe.wait_ge(odiag_done, hp + 1)
                spread(bank[7]).then_inc(ospread_done, 1)

            def start_rest():
                pe.wait_ge(diag_done, 1)
                pe.wait_ge(h_dve, 3)
                spread(bank[2]).then_inc(spread_done, 1)
                pe.wait_ge(par_in, 16 * (6 * DEPTH + 4))
                pe.wait_ge(h_dve, KT // 2)
                for t in range(4):
                    last = pe.transpose(bank[3][:, t * P:t * P + par_count[t]], par_rows[0:par_count[t], t, :],
                                        ident[0:par_count[t], 0:par_count[t]])
                last.then_inc(par_T, 1)
                pe.wait_ge(p_in, 16)
                pe.wait_ge(h_act, KT // 2)
                for j in range(DEPTH * PLE_KT):
                    i, k = divmod(j, PLE_KT)
                    for t in range(TT):
                        last = pe.transpose(bank[4 + j][:, t * P:(t + 1) * P],
                                            p_tok[:, i * TT + t, k * P:(k + 1) * P], ident[:, :])
                    last.then_inc(p_T, 1)
                pe.wait_ge(lam_prod, 2)
                pe.wait_ge(inv_done, 1)
                pe.matmul(bank[2][:, 0:2], ones[0:HEAD_DIM, :], lam_rows[:, 4:6], start=True, stop=True).then_inc(lam_sum, 1)

            def head(hd, back):
                if back == 0:
                    project(hd, 0, lambda: pe.wait_ge(h_dve, 1))
                    project(hd, 1, lambda: pe.wait_ge(h_dve, 2))
                    start_rest()
                else:
                    project(hd, 0, lambda: pe.wait_ge(vT_done, hd))
                    project(hd, 1, (lambda: pe.wait_ge(orms_done, hd - 1)) if back >= 2 else no_wait)
                    head_transposes(hd - 1)
                if back >= 2:
                    output_spread(hd - 2)
                project(hd, 2, lambda: pe.wait_ge(qlo_done, 2 * hd + 2))
                if back >= 1:
                    head_product(hd - 1)
                else:
                    pe.wait_ge(mask_done, 2)
                    pe.wait_ge(par_done, 4)
                    pe.wait_ge(pT_done, DEPTH * PLE_KT)
                    pe.wait_ge(lam_exp, 1)
                scores(hd, back)

            head(0, 0)
            head(1, 1)
            with pe.Fori(2, N_HEADS) as hd:
                head(hd, 2)

            def wo_part(m, heads, start=False, stop=False):
                n = PHASES["wo"][0] + m
                if start:
                    pe.wait_ge(lo_done, n + 1)
                    if m >= SLOTS:
                        pe.wait_ge(evac_done, result_of("wo", m - SLOTS))
                done = exact(bank[m % SLOTS][:, :],
                             [(block_of(slot_of(n), k), (oT_hi[:, k, :], oT_lo[:, k, :]), no_wait) for k in heads],
                             start=start, stop=stop)
                if stop:
                    done.then_inc(unit_done, 1)

            last_head = N_HEADS - 1
            pe.wait_ge(olo_done, last_head - 1)
            pe.wait_ge(vT_done, N_HEADS)
            wo_part(0, range(0, last_head - 1), start=True)
            pe.wait_ge(orms_done, last_head)
            wo_part(1, range(0, last_head - 1), start=True)
            head_transposes(last_head)
            output_spread(last_head - 1)
            head_product(last_head)
            pe.wait_ge(wtlo_done, 3 * N_HEADS)
            wo_part(2, range(0, 3), start=True)
            output_sums(last_head, bank[4])
            wo_part(2, range(3, last_head - 1))
            pe.wait_ge(olo_done, last_head)
            for m in range(3):
                wo_part(m, [last_head - 1])
            pe.wait_ge(onorm_done, last_head)
            output_spread(last_head)
            wo_part(3, range(0, 4), start=True)
            pe.wait_ge(olo_done, N_HEADS)
            for m in range(3):
                wo_part(m, [last_head], stop=True)
            wo_part(3, range(4, N_HEADS), stop=True)
            for m in range(SLOTS, KT):
                wo_part(m, range(N_HEADS), start=True, stop=True)

            def unit(name, u, a, parts, stop=True):
                pe.wait_ge(lo_done, SLOTS * a + PHASES[name][0] + u + 1)
                pe.wait_ge(evac_done, SLOTS * a + result_of(name, u) - SLOTS)
                last = exact(bank[u % SLOTS][:, :], parts, stop=stop)
                if stop:
                    last.then_inc(unit_done, 1)

            def norm_sums(norm):
                pe.wait_ge(acc_done, KT * norm)
                token_sums(bank[7], acc).then_inc(ss_done, 1)

            def norm_spread(norm):
                pe.wait_ge(diag_done, spread_of[norm])
                spread(bank[7]).then_inc(spread_done, 1)

            def embedding(n, layer, m):
                if m % TT == 0:
                    pe.wait_ge(lo_done, n + 1)
                if m >= 3:
                    pe.wait_ge(emb_done, KT * layer + m - 2)
                parts = []
                for k in range(PLE_KT):
                    j = layer * PLE_KT + k
                    parts.append((block_of(slot_of(n), k * TT + m % TT), (pT_hi[:, j, :], pT_lo[:, j, :]), no_wait))
                exact(bank[4 + m % 3][:, :], parts).then_inc(unit_done if m % TT == TT - 1 else emb_mm, 1)

            for m in range(TT):
                embedding(PHASES["emb0"][0], 0, m)
            norm_sums(NORM_FFN0)
            for m in range(TT, KT):
                embedding(PHASES["emb0"][0] + 1, 0, m)
            norm_spread(NORM_FFN0)
            for layer in range(DEPTH):
                if layer:
                    for m in range(TT - 1):
                        embedding(PHASES["emb1a"][0], 1, m)
                    width = POOL_KT * P

                    def pool_product(half, t):
                        n = PHASES["pool"][0] + half
                        i = half * TT + t
                        if t == 0:
                            pe.wait_ge(lo_done, n + 1)
                        if i < 3:
                            pe.wait_ge(emb_done, KT + i + 2)
                        else:
                            pe.wait_ge(zlo_done, i - 2)
                        for g in range(2):
                            tiles = [half * TT + g * POOL_KT + k for k in range(POOL_KT)]
                            ws = [slice((g * POOL_KT + k) * width, (g * POOL_KT + k + 1) * width) for k in range(POOL_KT)]
                            tok = slice(t * P, (t + 1) * P)
                            pe.wait_ge(x_ready, KT * NORM_MIX1 + tiles[-1] + 1)
                            mm = exact(z_bank(i)[:, g * width:(g + 1) * width], [
                                ((xp_hi[:, c, tok], xp_lo[:, c, tok]), (w_hi[slot_of(n)][:, w], w_lo[slot_of(n)][:, w]),
                                 no_wait) for c, w in zip(tiles, ws)])
                        mm.then_inc(unit_done if t == TT - 1 else z_mm, 1)

                    def pool_means(m):
                        half, g = m // TT, m // POOL_KT
                        pe.wait_ge(zlo_done, TT * (half + 1))
                        pe.wait_ge(evac_done, result_of("pool", m) - SLOTS)
                        feat = slice(m % TT * P, (m % TT + 1) * P)
                        for t in range(TT):
                            hi, lo = z_hi[half][:, t, feat], z_lo[half][:, t, feat]
                            w = min(BAND, SEQ - t * P)
                            dst = bank[m % SLOTS][:, t * P:t * P + w]
                            mat = band if t else first_band
                            pe.matmul(dst, hi, mat[:, g, 0:w], start=t == 0, stop=False, skip_group_check=True)
                            if t == 0:
                                pe.matmul(dst[:, 0:EDGE], hi, edge_lo[:, g, :], start=False, stop=False, skip_group_check=True)
                            mm = pe.matmul(dst, lo, mat[:, g, 0:w], start=False, stop=t == TT - 1, skip_group_check=True)
                        mm.then_inc(pool_mm, 1)

                    pe.wait_ge(edge_done, 1)
                    pool_product(0, 0)
                    norm_sums(NORM_MIX1)
                    embedding(PHASES["emb1a"][0], 1, TT - 1)
                    for t in range(1, TT):
                        pool_product(0, t)
                    for t in range(TT):
                        pool_product(1, t)
                        if t < TT - 1:
                            pool_means(t)
                    for m in range(TT, KT):
                        if m < TT + 2:
                            pe.wait_ge(zlo_done, 2 * TT - 1 + m - TT)
                        embedding(PHASES["emb1b"][0], 1, m)
                        pool_means(m - 1 if m == TT else m)
                        if m == TT:
                            pool_means(m)
                norm = NORM_FFN1 if layer else NORM_FFN0
                for part, tiles in enumerate(FFN_PARTS):
                    name = f"up{layer}{part}"

                    def up_body(a, first):
                        for u in range(SLOTS):
                            parts = x_parts(slot_of(PHASES[name][0] + u), KT * norm + 1 if first and u == 0 else None)
                            if first and u == 1 and layer:
                                weights, moving, ready = parts[KT // 2]

                                def ready_and_spread():
                                    norm_spread(norm)
                                    ready()

                                parts[KT // 2] = (weights, moving, ready_and_spread)
                            unit(name, u, a, parts)
                            if first and u == 0 and layer:
                                norm_sums(norm)

                    if part == 0:
                        up_body(0, True)
                    with pe.Fori(1 if part == 0 else 0, PHASES[name][1] // SLOTS) as a:
                        up_body(a, False)
                    name = f"down{layer}{part}"
                    pairs = layer * FT + sum(FFN_PARTS[:part])

                    def down_parts(u, ks, wait):
                        return [(block_of(slot_of(PHASES[name][0] + u), k), (g_hi[:, k, :], g_lo[:, k, :]),
                                 (lambda k=k: pe.wait_ge(glo_done, pairs + k + 1)) if wait else no_wait) for k in ks]

                    for u in range(2):
                        unit(name, u, 0, down_parts(u, range(tiles - 1), u == 0), stop=False)
                    for u in range(2):
                        exact(bank[u][:, :], down_parts(u, [tiles - 1], True), start=False).then_inc(unit_done, 1)
                    for m in range(2, KT):
                        unit(name, m % SLOTS, m // SLOTS, down_parts(m % SLOTS, range(tiles), False))
                norm = NORM_PLE1 if layer else NORM_PLE0
                name = f"ple{layer}"
                for m in range(KT):
                    unit(name, m, 0, x_parts(slot_of(PHASES[name][0] + m), KT * norm + 1 if m == 0 else None))
                    if m == 0:
                        norm_sums(norm)
                    if m == 1:
                        norm_spread(norm)
                    if layer == DEPTH - 1 and m >= 2:
                        y_transposes(m - 2)
            y_transposes(KT - 2)
            pe.wait_ge(acc_done, KT * NORM_FINAL - 1)
            for t in range(TT):
                pe.matmul(bank[7][:, t:t + 1], acc[:, t * P:(t + 1) * P], ones[:, 0:1], start=t == 0, stop=False,
                          skip_group_check=True)
            pe.wait_ge(sq_done, KT * NORM_FINAL)
            for t in range(TT):
                last = pe.matmul(bank[7][:, t:t + 1], sq[:, (KT - 1) % 2, t * P:(t + 1) * P], ones[:, 0:1], start=False,
                                 stop=t == TT - 1, skip_group_check=True)
            last.then_inc(ss_done, 1)
            y_transposes(KT - 1)


_INS = ['x', 'p', 'mix_norm_g', 'w_qkv', 'lam_q1', 'lam_k1', 'lam_q2', 'lam_k2', 'attn_sub_g', 'w_attn_out',
        'w_pool', 'b_pool', 'pool_scale', 'ffn_norm_g', 'w_up', 'conv_w', 'conv_b', 'w_down',
        'ple_norm_g', 'w_ple_gate', 'w_ple_proj', 'final_norm_g']


def kernel(**inputs):
    import concourse.bacc as bacc
    from concourse.bass_utils import run_bass_kernel_spmd

    nc = bacc.Bacc("TRN2", target_bir_lowering=False, num_devices=1)
    arrays, args = {}, []
    for name in _INS:
        a = np.ascontiguousarray(inputs[name])
        arrays[f"in_{name}"] = a
        args.append(nc.dram_tensor(f"in_{name}", a.shape, mybir.dt.from_np(a.dtype), kind="ExternalInput").ap())
    result = nc.dram_tensor("out", (1, SEQ, D_MODEL), F32, kind="ExternalOutput").ap()
    hybrid_trunk(nc, *args, result)
    r = run_bass_kernel_spmd(nc, [arrays], core_ids=[0])
    return r.results[0]["out"]
```
